# Optimizing a Trainium2 kernel written in Bass

```python
import math
import jax, jax.numpy as jnp
from jax import lax
import numpy as np

D_MODEL = 1024
BATCH = 1
SEQ = 256
DEPTH = 2

N_MIXERS = 4
ALPHA = (2 * DEPTH) ** 0.25
BETA = (8 * DEPTH) ** -0.25
LN_EPS = 1e-5

ML_HEADS = 4
ML_DV = D_MODEL // ML_HEADS
ML_DK = ML_DV // 2
ML_CHUNK = 64
ML_IN = 2 * ML_HEADS * ML_DK + 2 * D_MODEL + 4 * ML_HEADS

GLA_HEADS = 4
GLA_DK = D_MODEL // 2 // GLA_HEADS
GLA_DV = D_MODEL // GLA_HEADS
GLA_RANK = 16
GLA_TAU = 16.0
GLA_CHUNK = 32
GLA_IN = 2 * GLA_HEADS * GLA_DK + 2 * D_MODEL + 2 * GLA_RANK

LRU_WIDTH = D_MODEL
LRU_BLOCKS = 4
LRU_BW = LRU_WIDTH // LRU_BLOCKS
CONV_WIDTH = 4
LRU_C = 8.0
LRU_IN = 2 * LRU_WIDTH

MLA_HEADS = 8
MLA_NOPE = 128
MLA_ROPE = 64
MLA_DV = 128
MLA_Q_RANK = 384
MLA_KV_RANK = 256
MLA_IN = MLA_Q_RANK + MLA_KV_RANK + MLA_ROPE
ROPE_THETA = 10000.0
Q_BLOCK = 128

N_EXPERTS = 16
EXPERT_FF = 1024
CAPACITY_FACTOR = 2

N_MLSTM = (DEPTH - 0 + N_MIXERS - 1) // N_MIXERS
N_GLA = (DEPTH - 1 + N_MIXERS - 1) // N_MIXERS
N_LRU = (DEPTH - 2 + N_MIXERS - 1) // N_MIXERS
N_MLA = (DEPTH - 3 + N_MIXERS - 1) // N_MIXERS


def layer_norm(x, g, b):
    xf = x.astype(jnp.float32)
    mu = jnp.mean(xf, axis=-1, keepdims=True)
    var = jnp.mean(jnp.square(xf - mu), axis=-1, keepdims=True)
    return ((xf - mu) * lax.rsqrt(var + LN_EPS) * g + b).astype(x.dtype)

def rms_norm(x, g):
    xf = x.astype(jnp.float32)
    return (xf * lax.rsqrt(jnp.mean(jnp.square(xf), axis=-1, keepdims=True) + LN_EPS) * g).astype(x.dtype)

def head_norm(h, g):
    hf = h.astype(jnp.float32)
    mu = jnp.mean(hf, axis=-1, keepdims=True)
    var = jnp.mean(jnp.square(hf - mu), axis=-1, keepdims=True)
    hn = (hf - mu) * lax.rsqrt(var + LN_EPS)
    return hn.reshape(h.shape[0], h.shape[1], -1) * g.astype(jnp.float32)

def to_chunks(t, L):
    B, S = t.shape[0], t.shape[1]
    t = t.reshape((B, S // L, L) + t.shape[2:])
    return jnp.moveaxis(t, (1, 2), (0, 3))

def from_chunks(t):
    t = jnp.moveaxis(t, (0, 3), (1, 2))
    return t.reshape((t.shape[0], t.shape[1] * t.shape[2]) + t.shape[3:])

def flip_seq(t):
    return jnp.flip(t, axis=1)

def mlstm_chunked(q, k, v, ig, fg):
    B, S, H, DK = q.shape
    DV = v.shape[-1]
    L = ML_CHUNK
    mask = jnp.tril(jnp.ones((L, L), dtype=bool))

    def step(carry, inp):
        C, n, m = carry
        qb, kb, vb, ib, fb = inp
        b = jnp.cumsum(jax.nn.log_sigmoid(fb), axis=-1)
        g = b[..., -1]
        logD = jnp.where(mask, b[..., :, None] - b[..., None, :] + ib[..., None, :], -jnp.inf)
        inter = b + m[..., None]
        m_t = jnp.maximum(inter, jnp.max(logD, axis=-1))
        s = jnp.einsum('bhtd,bhsd->bhts', qb, kb) * jnp.exp(logD - m_t[..., None])
        w_inter = jnp.exp(inter - m_t)
        num = jnp.einsum('bhts,bhsv->bhtv', s, vb) + w_inter[..., None] * jnp.einsum('bhtd,bhdv->bhtv', qb, C)
        den = jnp.sum(s, axis=-1) + w_inter * jnp.einsum('bhtd,bhd->bht', qb, n)
        h = num / jnp.maximum(jnp.abs(den), jnp.exp(-m_t))[..., None]
        lw = g[..., None] - b + ib
        m_new = jnp.maximum(g + m, jnp.max(lw, axis=-1))
        ws = jnp.exp(lw - m_new[..., None])
        wc = jnp.exp(g + m - m_new)
        kw = kb * ws[..., None]
        C = wc[..., None, None] * C + jnp.einsum('bhsd,bhsv->bhdv', kw, vb)
        n = wc[..., None] * n + jnp.sum(kw, axis=-2)
        return (C, n, m_new), h

    init = (jnp.zeros((B, H, DK, DV), jnp.float32), jnp.zeros((B, H, DK), jnp.float32),
            jnp.zeros((B, H), jnp.float32))
    xs = (to_chunks(q, L), to_chunks(k, L), to_chunks(v, L), to_chunks(ig, L), to_chunks(fg, L))
    _, h = lax.scan(step, init, xs)
    return from_chunks(h)

def mlstm_mixer(x, w_in, gate_b, norm_g, w_out):
    B, S, _ = x.shape
    f32 = jnp.float32
    qk = ML_HEADS * ML_DK
    z = x @ w_in
    q, k, v, o, gates = jnp.split(z, [qk, 2 * qk, 2 * qk + D_MODEL, 2 * qk + 2 * D_MODEL], axis=-1)
    q = q.reshape(B, S, ML_HEADS, ML_DK).astype(f32) * (ML_DK ** -0.5)
    k = k.reshape(B, S, ML_HEADS, ML_DK).astype(f32)
    v = v.reshape(B, S, ML_HEADS, ML_DV).astype(f32)
    gates = gates.reshape(B, S, 2, 2, ML_HEADS).astype(f32) + gate_b.astype(f32)
    h_fwd = mlstm_chunked(q, k, v, gates[:, :, 0, 0], gates[:, :, 0, 1])
    h_bwd = flip_seq(mlstm_chunked(flip_seq(q), flip_seq(k), flip_seq(v),
                                   flip_seq(gates[:, :, 1, 0]), flip_seq(gates[:, :, 1, 1])))
    h = head_norm(h_fwd + h_bwd, norm_g).astype(x.dtype)
    return (jax.nn.sigmoid(o) * h) @ w_out

def gla_chunked(q, k, v, loga):
    B, S, H, DK = q.shape
    DV = v.shape[-1]
    L = GLA_CHUNK
    mask = jnp.tril(jnp.ones((L, L), dtype=bool))[:, :, None]

    def step(state, inp):
        qb, kb, vb, ab = inp
        b = jnp.cumsum(ab, axis=-2)
        dec = jnp.exp(jnp.where(mask, b[:, :, :, None, :] - b[:, :, None, :, :], -jnp.inf))
        A = jnp.einsum('bhtd,bhtsd,bhsd->bhts', qb, dec, kb)
        o = jnp.einsum('bhts,bhsv->bhtv', A, vb) + jnp.einsum('bhtd,bhdv->bhtv', qb * jnp.exp(b), state)
        g = b[:, :, -1, :]
        state = jnp.exp(g)[..., None] * state + jnp.einsum('bhsd,bhsv->bhdv', kb * jnp.exp(g[:, :, None, :] - b), vb)
        return state, o

    init = jnp.zeros((B, H, DK, DV), jnp.float32)
    xs = (to_chunks(q, L), to_chunks(k, L), to_chunks(v, L), to_chunks(loga, L))
    _, o = lax.scan(step, init, xs)
    return from_chunks(o)

def gla_mixer(x, w_in, gate_w, gate_b, norm_g, w_out):
    B, S, _ = x.shape
    f32 = jnp.float32
    qk = GLA_HEADS * GLA_DK
    z = x @ w_in
    q, k, v, r, glr = jnp.split(z, [qk, 2 * qk, 2 * qk + D_MODEL, 2 * qk + 2 * D_MODEL], axis=-1)
    q = q.reshape(B, S, GLA_HEADS, GLA_DK).astype(f32) * (GLA_DK ** -0.5)
    k = k.reshape(B, S, GLA_HEADS, GLA_DK).astype(f32)
    v = v.reshape(B, S, GLA_HEADS, GLA_DV).astype(f32)
    glr = glr.reshape(B, S, 2, GLA_RANK).astype(f32)
    loga = jax.nn.log_sigmoid(jnp.einsum('bsgr,grk->bsgk', glr, gate_w.astype(f32)) + gate_b.astype(f32)) / GLA_TAU
    loga = loga.reshape(B, S, 2, GLA_HEADS, GLA_DK)
    o_fwd = gla_chunked(q, k, v, loga[:, :, 0])
    o_bwd = flip_seq(gla_chunked(flip_seq(q), flip_seq(k), flip_seq(v), flip_seq(loga[:, :, 1])))
    o = head_norm(o_fwd + o_bwd, norm_g).astype(x.dtype)
    return (jax.nn.silu(r) * o) @ w_out

def rglru_direction(u, wa, ba, wx, bx, lam):
    B, S, W = u.shape
    ub = u.reshape(B, S, LRU_BLOCKS, LRU_BW)
    r = jax.nn.sigmoid(jnp.einsum('bsni,nij->bsnj', ub, wa).reshape(B, S, W) + ba)
    i = jax.nn.sigmoid(jnp.einsum('bsni,nij->bsnj', ub, wx).reshape(B, S, W) + bx)
    log_a = LRU_C * r * jax.nn.log_sigmoid(lam)
    a = jnp.exp(log_a)
    gated = jnp.sqrt(-jnp.expm1(2.0 * log_a)) * (i * u)

    def step(h, inp):
        a_t, g_t = inp
        h = a_t * h + g_t
        return h, h

    _, hs = lax.scan(step, jnp.zeros((B, W), jnp.float32), (jnp.swapaxes(a, 0, 1), jnp.swapaxes(gated, 0, 1)))
    return jnp.swapaxes(hs, 0, 1)

def rglru_mixer(x, w_in, conv_w, conv_b, gate_a_w, gate_a_b, gate_x_w, gate_x_b, lam, w_out):
    f32 = jnp.float32
    z = x @ w_in
    gate_branch, u = jnp.split(z, [LRU_WIDTH], axis=-1)
    u = lax.conv_general_dilated(u, conv_w[:, None, :].astype(u.dtype), window_strides=(1,),
                                 padding=[(CONV_WIDTH // 2, CONV_WIDTH - 1 - CONV_WIDTH // 2)],
                                 dimension_numbers=('NWC', 'WIO', 'NWC'),
                                 feature_group_count=LRU_WIDTH) + conv_b
    u = u.astype(f32)
    h_fwd = rglru_direction(u, gate_a_w[0].astype(f32), gate_a_b[0].astype(f32), gate_x_w[0].astype(f32),
                            gate_x_b[0].astype(f32), lam[0].astype(f32))
    h_bwd = flip_seq(rglru_direction(flip_seq(u), gate_a_w[1].astype(f32), gate_a_b[1].astype(f32),
                                     gate_x_w[1].astype(f32), gate_x_b[1].astype(f32), lam[1].astype(f32)))
    h = (h_fwd + h_bwd).astype(x.dtype)
    return (jax.nn.gelu(gate_branch) * h) @ w_out

def apply_rope(t, cos, sin):
    half = t.shape[-1] // 2
    t1, t2 = t[..., :half], t[..., half:]
    return jnp.concatenate([t1 * cos - t2 * sin, t2 * cos + t1 * sin], axis=-1)

def mla_mixer(x, positions, w_in, q_norm_g, kv_norm_g, w_uq, w_ukv, w_out):
    B, S, _ = x.shape
    f32 = jnp.float32
    z = x @ w_in
    cq, ckv, k_rope = jnp.split(z, [MLA_Q_RANK, MLA_Q_RANK + MLA_KV_RANK], axis=-1)
    q = (rms_norm(cq, q_norm_g) @ w_uq).reshape(B, S, MLA_HEADS, MLA_NOPE + MLA_ROPE)
    kv = (rms_norm(ckv, kv_norm_g) @ w_ukv).reshape(B, S, MLA_HEADS, MLA_NOPE + MLA_DV)
    q_nope, q_rope = jnp.split(q, [MLA_NOPE], axis=-1)
    k_nope, v = jnp.split(kv, [MLA_NOPE], axis=-1)
    half = MLA_ROPE // 2
    freq = ROPE_THETA ** (-jnp.arange(half, dtype=f32) / half)
    ang = positions.astype(f32)[..., None] * freq
    cos = jnp.cos(ang).astype(x.dtype)
    sin = jnp.sin(ang).astype(x.dtype)
    q_rope = apply_rope(q_rope, cos[:, :, None, :], sin[:, :, None, :])
    k_rope = apply_rope(k_rope, cos, sin)
    scale = (MLA_NOPE + MLA_ROPE) ** -0.5
    nq = S // Q_BLOCK
    qn_blocks = jnp.moveaxis(q_nope.reshape(B, nq, Q_BLOCK, MLA_HEADS, MLA_NOPE), 1, 0)
    qr_blocks = jnp.moveaxis(q_rope.reshape(B, nq, Q_BLOCK, MLA_HEADS, MLA_ROPE), 1, 0)

    def attend(blk):
        qn, qr = blk
        s = (jnp.einsum('bqhd,bkhd->bhqk', qn, k_nope) + jnp.einsum('bqhd,bkd->bhqk', qr, k_rope)).astype(f32) * scale
        p = jax.nn.softmax(s, axis=-1).astype(v.dtype)
        return jnp.einsum('bhqk,bkhv->bqhv', p, v)

    out = lax.map(attend, (qn_blocks, qr_blocks))
    out = jnp.moveaxis(out, 0, 1).reshape(B, S, MLA_HEADS * MLA_DV)
    return out @ w_out

def ec_moe(x, w_router, w_gate, w_up, w_down):
    B, N, _ = x.shape
    cap = CAPACITY_FACTOR * N // N_EXPERTS
    aff = jax.nn.softmax(jnp.einsum('bnd,de->bne', x, w_router).astype(jnp.float32), axis=-1)
    gates, idx = lax.top_k(jnp.swapaxes(aff, 1, 2), cap)
    bidx = jnp.arange(B)[:, None, None]
    xin = x[bidx, idx]
    h = jax.nn.silu(jnp.einsum('becd,edf->becf', xin, w_gate)) * jnp.einsum('becd,edf->becf', xin, w_up)
    out = jnp.einsum('becf,efd->becd', h, w_down) * gates[..., None].astype(x.dtype)
    return jnp.zeros_like(x).at[bidx, idx].add(out.astype(x.dtype))

def first_inputs(seed: int = 0) -> dict:
    key = jax.random.key(seed)
    keys = iter(jax.random.split(key, 64))
    f32 = jnp.float32

    def nrm(shape, scale):
        return jax.random.normal(next(keys), shape, f32) * scale

    def gain(shape):
        return 1.0 + nrm(shape, 0.02)

    D = D_MODEL
    x = jax.random.normal(next(keys), (BATCH, SEQ, D), f32)
    positions = (jnp.arange(SEQ, dtype=jnp.int32)[None, :]
                 + jax.random.randint(next(keys), (BATCH, 1), 0, SEQ, dtype=jnp.int32))
    mlstm_w_in = nrm((N_MLSTM, D, ML_IN), D ** -0.5)
    ig_b = nrm((N_MLSTM, 2, 1, ML_HEADS), 0.1)
    fg_b = 3.0 + 3.0 * jax.random.uniform(next(keys), (N_MLSTM, 2, 1, ML_HEADS), f32)
    mlstm_gate_b = jnp.concatenate([ig_b, fg_b], axis=2)
    mlstm_norm_g = gain((N_MLSTM, D))
    mlstm_w_out = nrm((N_MLSTM, D, D), BETA * D ** -0.5)
    gla_w_in = nrm((N_GLA, D, GLA_IN), D ** -0.5)
    gla_gate_w = nrm((N_GLA, 2, GLA_RANK, GLA_HEADS * GLA_DK), GLA_RANK ** -0.5)
    gla_gate_b = nrm((N_GLA, 2, GLA_HEADS * GLA_DK), 0.1)
    gla_norm_g = gain((N_GLA, D))
    gla_w_out = nrm((N_GLA, D, D), BETA * D ** -0.5)
    lru_w_in = nrm((N_LRU, D, LRU_IN), D ** -0.5)
    lru_conv_w = nrm((N_LRU, CONV_WIDTH, LRU_WIDTH), CONV_WIDTH ** -0.5)
    lru_conv_b = nrm((N_LRU, LRU_WIDTH), 0.02)
    lru_gate_a_w = nrm((N_LRU, 2, LRU_BLOCKS, LRU_BW, LRU_BW), LRU_BW ** -0.5)
    lru_gate_a_b = nrm((N_LRU, 2, LRU_WIDTH), 0.1)
    lru_gate_x_w = nrm((N_LRU, 2, LRU_BLOCKS, LRU_BW, LRU_BW), LRU_BW ** -0.5)
    lru_gate_x_b = nrm((N_LRU, 2, LRU_WIDTH), 0.1)
    a0 = jax.random.uniform(next(keys), (N_LRU, 2, LRU_WIDTH), f32, minval=0.9, maxval=0.999)
    s0 = a0 ** (1.0 / LRU_C)
    lru_lambda = jnp.log(s0) - jnp.log1p(-s0)
    lru_w_out = nrm((N_LRU, LRU_WIDTH, D), BETA * LRU_WIDTH ** -0.5)
    mla_w_in = nrm((N_MLA, D, MLA_IN), D ** -0.5)
    mla_q_norm_g = gain((N_MLA, MLA_Q_RANK))
    mla_kv_norm_g = gain((N_MLA, MLA_KV_RANK))
    mla_w_uq = nrm((N_MLA, MLA_Q_RANK, MLA_HEADS * (MLA_NOPE + MLA_ROPE)), MLA_Q_RANK ** -0.5)
    mla_w_ukv = nrm((N_MLA, MLA_KV_RANK, MLA_HEADS * (MLA_NOPE + MLA_DV)), MLA_KV_RANK ** -0.5)
    mla_w_out = nrm((N_MLA, MLA_HEADS * MLA_DV, D), BETA * (MLA_HEADS * MLA_DV) ** -0.5)
    moe_router = nrm((DEPTH, D, N_EXPERTS), D ** -0.5)
    moe_w_gate = nrm((DEPTH, N_EXPERTS, D, EXPERT_FF), D ** -0.5)
    moe_w_up = nrm((DEPTH, N_EXPERTS, D, EXPERT_FF), D ** -0.5)
    moe_w_down = nrm((DEPTH, N_EXPERTS, EXPERT_FF, D), BETA * EXPERT_FF ** -0.5)
    ln_g = gain((DEPTH, 2, D))
    ln_b = nrm((DEPTH, 2, D), 0.02)
    return {
        'x': x, 'positions': positions,
        'mlstm_w_in': mlstm_w_in, 'mlstm_gate_b': mlstm_gate_b, 'mlstm_norm_g': mlstm_norm_g, 'mlstm_w_out': mlstm_w_out,
        'gla_w_in': gla_w_in, 'gla_gate_w': gla_gate_w, 'gla_gate_b': gla_gate_b, 'gla_norm_g': gla_norm_g, 'gla_w_out': gla_w_out,
        'lru_w_in': lru_w_in, 'lru_conv_w': lru_conv_w, 'lru_conv_b': lru_conv_b,
        'lru_gate_a_w': lru_gate_a_w, 'lru_gate_a_b': lru_gate_a_b, 'lru_gate_x_w': lru_gate_x_w, 'lru_gate_x_b': lru_gate_x_b,
        'lru_lambda': lru_lambda, 'lru_w_out': lru_w_out,
        'mla_w_in': mla_w_in, 'mla_q_norm_g': mla_q_norm_g, 'mla_kv_norm_g': mla_kv_norm_g,
        'mla_w_uq': mla_w_uq, 'mla_w_ukv': mla_w_ukv, 'mla_w_out': mla_w_out,
        'moe_router': moe_router, 'moe_w_gate': moe_w_gate, 'moe_w_up': moe_w_up, 'moe_w_down': moe_w_down,
        'ln_g': ln_g, 'ln_b': ln_b,
    }

def first_block(x, positions,
              mlstm_w_in, mlstm_gate_b, mlstm_norm_g, mlstm_w_out,
              gla_w_in, gla_gate_w, gla_gate_b, gla_norm_g, gla_w_out,
              lru_w_in, lru_conv_w, lru_conv_b, lru_gate_a_w, lru_gate_a_b, lru_gate_x_w, lru_gate_x_b,
              lru_lambda, lru_w_out,
              mla_w_in, mla_q_norm_g, mla_kv_norm_g, mla_w_uq, mla_w_ukv, mla_w_out,
              moe_router, moe_w_gate, moe_w_up, moe_w_down,
              ln_g, ln_b):
    for i in range(DEPTH):
        m = i % N_MIXERS
        j = i // N_MIXERS
        if m == 0:
            h = mlstm_mixer(x, mlstm_w_in[j], mlstm_gate_b[j], mlstm_norm_g[j], mlstm_w_out[j])
        elif m == 1:
            h = gla_mixer(x, gla_w_in[j], gla_gate_w[j], gla_gate_b[j], gla_norm_g[j], gla_w_out[j])
        elif m == 2:
            h = rglru_mixer(x, lru_w_in[j], lru_conv_w[j], lru_conv_b[j], lru_gate_a_w[j], lru_gate_a_b[j],
                            lru_gate_x_w[j], lru_gate_x_b[j], lru_lambda[j], lru_w_out[j])
        else:
            h = mla_mixer(x, positions, mla_w_in[j], mla_q_norm_g[j], mla_kv_norm_g[j],
                          mla_w_uq[j], mla_w_ukv[j], mla_w_out[j])
        x = layer_norm(ALPHA * x + h, ln_g[i, 0], ln_b[i, 0])
        y = ec_moe(x, moe_router[i], moe_w_gate[i], moe_w_up[i], moe_w_down[i])
        x = layer_norm(ALPHA * x + y, ln_g[i, 1], ln_b[i, 1])
    return x


N_MIXERS_2 = 2
N_POOL_LAYERS = (DEPTH + 1) // 2
N_ATTN_LAYERS = DEPTH // 2
ALPHA_2 = (2.0 * DEPTH) ** 0.25
BETA_2 = (8.0 * DEPTH) ** -0.25
POOL_WINDOWS = (2, 4, 8, 16)
N_GROUPS = len(POOL_WINDOWS)
GROUP_W = D_MODEL // N_GROUPS
HEAD_DIM = 64
N_HEADS = D_MODEL // (2 * HEAD_DIM)
V_DIM = 2 * HEAD_DIM
D_ATTN = N_HEADS * V_DIM
NUM_BUCKETS = 32
MAX_EXACT = NUM_BUCKETS // 2
MAX_DISTANCE = 128
D_FF = ((int(math.ceil(8 * D_MODEL / 3)) + 255) // 256) * 256


def _layernorm(x, g, b):
    xf = x.astype(jnp.float32)
    mu = jnp.mean(xf, axis=-1, keepdims=True)
    var = jnp.mean(jnp.square(xf - mu), axis=-1, keepdims=True)
    y = (xf - mu) * lax.rsqrt(var + LN_EPS)
    return (y * g.astype(jnp.float32) + b.astype(jnp.float32)).astype(x.dtype)

def _multiscale_pool(x, w, scale):
    B, S, D = x.shape
    xg = x.astype(jnp.float32).reshape(B, S, N_GROUPS, GROUP_W)
    cs = jnp.pad(jnp.cumsum(xg, axis=1), ((0, 0), (1, 0), (0, 0), (0, 0)))
    t = jnp.arange(S)
    pooled = []
    for g, win in enumerate(POOL_WINDOWS):
        hi = cs[:, 1:, g]
        lo = jnp.pad(cs[:, :S + 1 - win, g], ((0, 0), (win - 1, 0), (0, 0)))
        cnt = jnp.minimum(t + 1, win).astype(jnp.float32)[None, :, None]
        pooled.append((hi - lo) / cnt)
    pooled = jnp.stack(pooled, axis=2)
    mixed = jnp.einsum('bsgc,gcd->bsgd', pooled - xg, w.astype(jnp.float32))
    return (mixed.reshape(B, S, D) * scale.astype(jnp.float32)).astype(x.dtype)

def _rel_bucket(rel):
    n = jnp.maximum(rel, 0)
    is_small = n < MAX_EXACT
    nf = jnp.maximum(n, 1).astype(jnp.float32)
    large = MAX_EXACT + (jnp.log(nf / MAX_EXACT) / math.log(MAX_DISTANCE / MAX_EXACT)
                         * (NUM_BUCKETS - MAX_EXACT)).astype(jnp.int32)
    large = jnp.minimum(large, NUM_BUCKETS - 1)
    return jnp.where(is_small, n, large)

def _diff_attention(x, w_qkv, w_o, lam_p, subln_g, rel_table, lambda_init):
    B, S, D = x.shape
    qkv = x @ w_qkv
    q, k, v = jnp.split(qkv, 3, axis=-1)
    q = q.reshape(B, S, N_HEADS, 2, HEAD_DIM).transpose(0, 2, 3, 1, 4)
    k = k.reshape(B, S, N_HEADS, 2, HEAD_DIM).transpose(0, 2, 3, 1, 4)
    v = v.reshape(B, S, N_HEADS, V_DIM).transpose(0, 2, 1, 3)
    lp = lam_p.astype(jnp.float32)
    lam = (jnp.exp(jnp.sum(lp[0] * lp[1])) - jnp.exp(jnp.sum(lp[2] * lp[3])) + lambda_init)
    sm_scale = HEAD_DIM ** -0.5
    outs = []
    for qb in range(S // Q_BLOCK):
        q0 = qb * Q_BLOCK
        kend = q0 + Q_BLOCK
        s = jnp.einsum('bhcqd,bhckd->bhcqk', q[:, :, :, q0:kend], k[:, :, :, :kend]).astype(jnp.float32) * sm_scale
        rel = (q0 + jnp.arange(Q_BLOCK))[:, None] - jnp.arange(kend)[None, :]
        bias = rel_table[_rel_bucket(rel)].astype(jnp.float32).transpose(2, 0, 1)
        s = jnp.where(rel >= 0, s + bias[None, :, None], -jnp.inf)
        p = jax.nn.softmax(s, axis=-1)
        a = p[:, :, 0] - lam * p[:, :, 1]
        outs.append(jnp.einsum('bhqk,bhkv->bhqv', a.astype(v.dtype), v[:, :, :kend]))
    o = jnp.concatenate(outs, axis=2).astype(jnp.float32)
    o = o * lax.rsqrt(jnp.mean(jnp.square(o), axis=-1, keepdims=True) + LN_EPS)
    o = o * subln_g.astype(jnp.float32) * (1.0 - lambda_init)
    o = o.transpose(0, 2, 1, 3).reshape(B, S, D_ATTN).astype(x.dtype)
    return o @ w_o

def _swiglu(x, w_gate, w_up, w_down):
    return (jax.nn.silu(x @ w_gate) * (x @ w_up)) @ w_down

def second_inputs(seed: int = 0) -> dict:
    key = jax.random.key(seed)
    ks = jax.random.split(key, 20)
    f32 = jnp.float32
    nrm = lambda k, s: jax.random.normal(k, s, f32)
    x = nrm(ks[0], (BATCH, SEQ, D_MODEL))
    pool_w = nrm(ks[1], (N_POOL_LAYERS, N_GROUPS, GROUP_W, GROUP_W)) * (GROUP_W ** -0.5) * BETA_2
    pool_scale = 1.0 + 0.02 * nrm(ks[2], (N_POOL_LAYERS, D_MODEL))
    w_qk = nrm(ks[3], (N_ATTN_LAYERS, D_MODEL, 2 * D_ATTN)) * (D_MODEL ** -0.5)
    w_v = nrm(ks[4], (N_ATTN_LAYERS, D_MODEL, D_ATTN)) * (D_MODEL ** -0.5) * BETA_2
    w_qkv = jnp.concatenate([w_qk, w_v], axis=-1)
    w_o = nrm(ks[5], (N_ATTN_LAYERS, D_ATTN, D_MODEL)) * (D_ATTN ** -0.5) * BETA_2
    lam_p = 0.1 * nrm(ks[6], (N_ATTN_LAYERS, 4, HEAD_DIM))
    subln_g = 1.0 + 0.02 * nrm(ks[7], (N_ATTN_LAYERS, V_DIM))
    rel_table = 0.5 * nrm(ks[8], (NUM_BUCKETS, N_HEADS))
    w_gate = nrm(ks[9], (DEPTH, D_MODEL, D_FF)) * (D_MODEL ** -0.5) * BETA_2
    w_up = nrm(ks[10], (DEPTH, D_MODEL, D_FF)) * (D_MODEL ** -0.5) * BETA_2
    w_down = nrm(ks[11], (DEPTH, D_FF, D_MODEL)) * (D_FF ** -0.5) * BETA_2
    ln_mix_g = 1.0 + 0.02 * nrm(ks[12], (DEPTH, D_MODEL))
    ln_mix_b = 0.02 * nrm(ks[13], (DEPTH, D_MODEL))
    ln_ffn_g = 1.0 + 0.02 * nrm(ks[14], (DEPTH, D_MODEL))
    ln_ffn_b = 0.02 * nrm(ks[15], (DEPTH, D_MODEL))
    return {"x": x, "pool_w": pool_w, "pool_scale": pool_scale, "w_qkv": w_qkv, "w_o": w_o,
            "lam_p": lam_p, "subln_g": subln_g, "rel_table": rel_table, "w_gate": w_gate,
            "w_up": w_up, "w_down": w_down, "ln_mix_g": ln_mix_g, "ln_mix_b": ln_mix_b,
            "ln_ffn_g": ln_ffn_g, "ln_ffn_b": ln_ffn_b}

def second_block(x, pool_w, pool_scale, w_qkv, w_o, lam_p, subln_g, rel_table, w_gate,
              w_up, w_down, ln_mix_g, ln_mix_b, ln_ffn_g, ln_ffn_b):
    for i in range(DEPTH):
        j = i // N_MIXERS_2
        if i % N_MIXERS_2 == 0:
            h = _multiscale_pool(x, pool_w[j], pool_scale[j])
        else:
            lambda_init = 0.8 - 0.6 * math.exp(-0.3 * i)
            h = _diff_attention(x, w_qkv[j], w_o[j], lam_p[j], subln_g[j], rel_table, lambda_init)
        x = _layernorm(ALPHA_2 * x + h, ln_mix_g[i], ln_mix_b[i])
        x = _layernorm(ALPHA_2 * x + _swiglu(x, w_gate[i], w_up[i], w_down[i]), ln_ffn_g[i], ln_ffn_b[i])
    return x


def setup_inputs(seed=0):
    out = dict(first_inputs(seed))
    for name, value in second_inputs(seed + 1).items():
        if name != "x":
            out[name + "_2"] = value
    return out


def reference(
    x, positions, mlstm_w_in, mlstm_gate_b, mlstm_norm_g, mlstm_w_out, gla_w_in, gla_gate_w,
    gla_gate_b, gla_norm_g, gla_w_out, lru_w_in, lru_conv_w, lru_conv_b, lru_gate_a_w,
    lru_gate_a_b, lru_gate_x_w, lru_gate_x_b, lru_lambda, lru_w_out, mla_w_in, mla_q_norm_g,
    mla_kv_norm_g, mla_w_uq, mla_w_ukv, mla_w_out, moe_router, moe_w_gate, moe_w_up, moe_w_down,
    ln_g, ln_b, pool_w_2, pool_scale_2, w_qkv_2, w_o_2, lam_p_2, subln_g_2, rel_table_2,
    w_gate_2, w_up_2, w_down_2, ln_mix_g_2, ln_mix_b_2, ln_ffn_g_2, ln_ffn_b_2,
):
    x = first_block(
        x, positions, mlstm_w_in, mlstm_gate_b, mlstm_norm_g, mlstm_w_out, gla_w_in, gla_gate_w,
        gla_gate_b, gla_norm_g, gla_w_out, lru_w_in, lru_conv_w, lru_conv_b, lru_gate_a_w,
        lru_gate_a_b, lru_gate_x_w, lru_gate_x_b, lru_lambda, lru_w_out, mla_w_in, mla_q_norm_g,
        mla_kv_norm_g, mla_w_uq, mla_w_ukv, mla_w_out, moe_router, moe_w_gate, moe_w_up,
        moe_w_down, ln_g, ln_b,
    )
    return second_block(
        x, pool_w_2, pool_scale_2, w_qkv_2, w_o_2, lam_p_2, subln_g_2, rel_table_2, w_gate_2,
        w_up_2, w_down_2, ln_mix_g_2, ln_mix_b_2, ln_ffn_g_2, ln_ffn_b_2,
    )


_drawn_inputs = setup_inputs


def setup_inputs(seed=0):
    import zlib

    import numpy as np

    out = dict(_drawn_inputs(seed))
    spreads = {}
    factors = {'mlstm_norm_g': 8.0,
     'gla_gate_b': 5.971,
     'gla_norm_g': 8.0,
     'pool_scale_2': 8.0,
     'subln_g_2': 8.0}
    for name, (base, spread) in spreads.items():
        noise = np.random.default_rng([zlib.crc32(name.encode()), seed]).standard_normal(out[name].shape)
        drawn = base * np.exp(spread * noise) if base else spread * noise
        out[name] = __import__('jax').numpy.asarray(drawn.astype(out[name].dtype))
    for name, factor in factors.items():
        out[name] = (out[name] * factor).astype(out[name].dtype)
    return out
```

```python
import math
from contextlib import ExitStack

import numpy as np

import concourse.bass as bass
import concourse.mybir as mybir
from concourse.alu_op_type import AluOpType as ALU

ACT = mybir.ActivationFunctionType
AX = mybir.AxisListType
F32 = mybir.dt.float32
F32R = mybir.dt.float32r
U32 = mybir.dt.uint32
U8 = mybir.dt.uint8

P = 128
SEQ, D = 256, 1024
NT = SEQ // P
KD = D // P
DEPTH = 2
ALPHA = (2 * DEPTH) ** 0.25
EPS = 1e-5
HALF = 512

HEADS = 4
DK, DV = 128, 256
QK = HEADS * DK
RANK, TAU = 16, 16.0

NE, FF, CAP = 16, 1024, 32
GROUP = 4
NGROUP = NE // GROUP
SLOTS_E = GROUP * CAP

WINDOWS = (2, 4, 8, 16)
A_HEADS, HD = 8, 64
V_DIM = 2 * HD
BUCKETS, MAX_EXACT, MAX_DIST = 32, 16, 128
D_FF = 2816
NF = D_FF // P
LAMBDA_INIT = 0.8 - 0.6 * math.exp(-0.3)
MASKED = -1e30

RING = 8
SLOT = 2048
CHUNK = 1024
LEVELS = (1, 2, 4, 8, 16, 32, 64, 128)

C_ID, C_EYE, C_SEL, C_XOR, C_REL, C_TOK, C_EPS = 0, 128, 640, 1152, 1280, 1664, 1666
C_W = 1668


def shape_constants():
    c = np.zeros((P, C_W), np.float32)
    c[:, C_ID:C_ID + P] = np.eye(P)
    for e in range(NE):
        c[e, C_EYE + e * CAP:C_EYE + (e + 1) * CAP] = 1.0
    for h in range(HEADS):
        c[h, C_SEL + h * P:C_SEL + (h + 1) * P] = 1.0
    s = np.arange(P)
    c[:, C_XOR:C_XOR + P] = s[:, None] ^ s[None, :]
    for m in range(3 * P):
        rel = 255 - m
        if rel < 0:
            b = BUCKETS
        elif rel < MAX_EXACT:
            b = rel
        else:
            b = MAX_EXACT + int(math.log(rel / MAX_EXACT) / math.log(MAX_DIST / MAX_EXACT) * (BUCKETS - MAX_EXACT))
            b = min(b, BUCKETS - 1)
        c[b, C_REL + m] = 1.0
    for i in range(NT):
        c[:, C_TOK + i] = s + i * P
    c[:, C_EPS] = EPS
    band = np.zeros((SEQ, len(WINDOWS), SEQ), np.float32)
    for g, win in enumerate(WINDOWS):
        for t in range(SEQ):
            n = min(t + 1, win)
            band[t - n + 1:t + 1, g, t] = np.float32(1.0) / np.float32(n)
            band[t, g, t] -= 1.0
    band = band.reshape(NT, P, len(WINDOWS), SEQ).transpose(1, 0, 2, 3).reshape(P, -1)
    return c, np.ascontiguousarray(band)


class Unit:

    def __init__(self, n, slot, landed, n_step=0, landed_step=0):
        self.n, self.slot, self.landed = n, slot, landed
        self.n_step, self.landed_step = n_step, landed_step

    def landed_at(self, i=0):
        return self.landed + i * self.landed_step if self.landed_step else self.landed

    def done_at(self, i=0):
        return i * self.n_step + self.n + 1 if self.n_step else self.n + 1

    def free_at(self, i=0):
        return i * self.n_step + self.n + 1 - RING if self.n_step else self.n + 1 - RING


class Stream:
    def __init__(self):
        self.n, self.landed = 0, [0] * RING

    def unit(self, dmas=1):
        s = self.n % RING
        self.landed[s] += 16 * dmas
        self.n += 1
        return Unit(self.n - 1, s, self.landed[s])

    def skip(self):
        self.n += 1

    def units(self, count):
        return [self.unit() for _ in range(count)]

    def loop(self, count, dmas):
        assert len(dmas) % RING == 0
        body, per, start = [], [0] * RING, list(self.landed)
        for b, d in enumerate(dmas):
            s = (self.n + b) % RING
            per[s] += 16 * d
            if d:
                body.append((self.n + b, s, start[s] + per[s]))
        self.n += count * len(dmas)
        self.landed = [a + count * p for a, p in zip(start, per)]
        return [Unit(n, s, at, len(dmas), per[s]) for n, s, at in body]


def program(nc, a, out, upto=8):
    ctx = ExitStack()
    with ctx:
        def sb(name, cols, dt=F32):
            return ctx.enter_context(nc.sbuf_tensor(name, [P, cols], dt))

        def sem(name):
            return ctx.enter_context(nc.semaphore(name))

        ring = sb("ring", RING * SLOT)
        cst = sb("cst", C_W)
        lvl_mask = sb("lvl_mask", 7 * P, U8)
        ln_rows, ln_cols = sb("ln_rows", P), sb("ln_cols", P)
        mix_rows, mix_cols = sb("mix_rows", P), sb("mix_cols", 33)
        x_tok, xT, y, gb = sb("x_tok", NT * D), sb("xT", KD * SEQ), sb("y", NT * D), sb("gb", 2 * D)
        gate_w = sb("gate_w", KD * 16)
        glr_w = sb("glr_w", KD * 32)
        rout_w = sb("rout_w", 2 * KD * NE)
        gk_w = sb("gk_w", 2 * QK)
        gate_b = sb("gate_b", 4)
        lam_p = sb("lam_p", 4 * HD)
        rel_t = sb("rel_t", A_HEADS)
        ones = sb("ones", SEQ)
        xT_hi, xT_lo = sb("xT_hi", KD * SEQ, F32R), sb("xT_lo", KD * SEQ, F32R)
        w_hi, w_lo = sb("w_hi", 2 * CHUNK, F32R), sb("w_lo", 2 * CHUNK, F32R)
        h_hi, h_lo = sb("h_hi", 4 * SEQ, F32R), sb("h_lo", 4 * SEQ, F32R)
        stats = sb("stats", 64)
        mv = sb("mv", 16)
        std, rstd, nmr = sb("std", 8), sb("rstd", 8), sb("nmr", 8)
        small = sb("small", 128)
        arena_w = 13312
        arena = sb("arena", arena_w)

        class Arena:
            def __init__(self):
                self.at = 0

            def __call__(self, cols):
                self.at += cols
                assert self.at <= arena_w, self.at
                return arena[:, self.at - cols:self.at]

        ident = cst[:, C_ID:C_ID + P]
        eye16 = cst[0:NE, C_EYE:C_EYE + NE * CAP]
        eps = cst[:, C_EPS:C_EPS + 1]
        x3, y3 = (t[:, :].rearrange("p (i d) -> p i d", i=NT) for t in (x_tok, y))
        xT3, xT_hi3, xT_lo3 = (t[:, :].rearrange("p (k t) -> p k t", k=KD) for t in (xT, xT_hi, xT_lo))
        w_parts = [t[:, :].rearrange("p (b n) -> p b n", b=2) for t in (w_hi, w_lo)]
        h_parts = [t[:, :].rearrange("p (b t) -> p b t", b=4) for t in (h_hi, h_lo)]
        PARTS = ((0, 0), (0, 1), (1, 0))
        ps = [ctx.enter_context(nc.psum_tensor(f"bank{b}", [P, HALF], F32)) for b in range(8)]
        rel_dram = nc.dram_tensor("rel_scratch", (A_HEADS, P * 3 * P), F32, kind="Internal").ap()

        def slot(u, k):
            return ring[:, u.slot * SLOT:(u.slot + 1) * SLOT].rearrange("p (k n) -> p k n", k=k)

        st = Stream()
        MOE_UNITS = 48
        ml_u = st.units(16)
        moe_u = [None, None]
        moe_u[0] = st.loop(NGROUP, [1] * MOE_UNITS)
        gla_u = st.units(16)
        moe_u[1] = st.loop(NGROUP, [1] * MOE_UNITS)
        pool_u = st.unit()

        def ffn_units():
            return st.units(2), st.loop(5, [1, 1, 1, 0] * 2), st.unit()

        ffn_u = [ffn_units(), None]
        att_u = st.units(16)
        ffn_u[1] = ffn_units()

        slot_landed = [sem(f"slot{s}_landed") for s in range(RING)]
        unit_done = sem("unit_done")
        hi_ready, split_ready, chunk_done = sem("hi_ready"), sem("split_ready"), sem("chunk_done")
        xhi_vec, xlo_ready = sem("xhi_vec"), sem("xlo_ready")
        x_in, ident_in, const_in = sem("x_in"), sem("ident_in"), sem("const_in")
        gate_in, par_in, misc_in = sem("gate_in"), sem("par_in"), sem("misc_in")
        act_chain, vec_chain, pool_chain = sem("act_chain"), sem("vec_chain"), sem("pool_chain")
        const_ready = sem("const_ready")
        rel_out, rel_in = sem("rel_out"), sem("rel_in")
        var_ready, std_ready, rstd_ready = sem("var_ready"), sem("std_ready"), sem("rstd_ready")
        xhat_act, xhat_vec = sem("xhat_act"), sem("xhat_vec")
        xT_psum, xT_act, xT_vec = sem("xT_psum"), sem("xT_act"), sem("xT_vec")
        rows_in, x_ready = sem("rows_in"), sem("x_ready")
        y_free = sem("y_free")
        x_out = sem("x_out")

        def chain(eng, s):
            count = [0]

            def link(ins):
                count[0] += 1
                ins.then_inc(s, 1)
                eng.wait_ge(s, count[0])
            return link

        def ln_vector(dve, link, n, stats_done=()):
            for i in range(NT):
                for c in range(2):
                    if (i, c) not in stats_done:
                        ins = nc.vector.bn_stats(stats[:, i * 12 + c * 6:i * 12 + c * 6 + 6],
                                                 y3[:, i, c * HALF:(c + 1) * HALF])
                link(ins)
                nc.vector.bn_aggr(mv[:, 2 * i:2 * i + 2], stats[:, i * 12:i * 12 + 12]).then_inc(var_ready, 1)
            for i in range(NT):
                dve.wait_ge(std_ready, NT * n + i + 1)
                link(nc.vector.reciprocal(rstd[:, i:i + 1], std[:, i:i + 1]))
                nc.vector.scalar_tensor_tensor(nmr[:, i:i + 1], mv[:, 2 * i:2 * i + 1], -1.0, rstd[:, i:i + 1],
                                               ALU.mult, ALU.mult).then_inc(rstd_ready, 1)
            dve.wait_ge(rstd_ready, NT * n + NT)
            nc.vector.tensor_scalar(y3[:, 1, :], y3[:, 1, :], rstd[:, 1:2], nmr[:, 1:2],
                                    ALU.mult, ALU.add).then_inc(xhat_vec, 1)

        def ln_scalar(act, n):
            for i in range(NT):
                act.wait_ge(var_ready, NT * n + i + 1)
                nc.scalar.activation(std[:, i:i + 1], mv[:, 2 * i + 1:2 * i + 2], ACT.Sqrt,
                                     bias=eps).then_inc(std_ready, 1)
            act.wait_ge(rstd_ready, NT * n + 1)
            nc.scalar.activation(y3[:, 0, :], y3[:, 0, :], ACT.Identity, bias=nmr[:, 0:1],
                                 scale=rstd[:, 0:1]).then_inc(xhat_act, 1)

        def ln_gpsimd(pool, link, n, g_row, b_row):
            if n:
                pool.wait_ge(x_ready, NT * n)
            pool.dma_start(gb[0:1, 0:D], g_row).then_inc(rows_in, 16)
            pool.dma_start(gb[0:1, D:2 * D], b_row).then_inc(rows_in, 16)
            pool.wait_ge(rows_in, 32 * (n + 1))
            link(nc.gpsimd.partition_broadcast(gb[:, :], gb[0:1, :], channels=P))
            for i in range(NT):
                pool.wait_ge((xhat_act, xhat_vec)[i], n + 1)
                nc.gpsimd.tensor_tensor(x3[:, i, :], y3[:, i, :], gb[:, 0:D], ALU.mult).then_inc(y_free, 1)
                pool.wait_ge(y_free, NT * n + i + 1)
                nc.gpsimd.tensor_tensor(x3[:, i, :], x3[:, i, :], gb[:, D:2 * D], ALU.add).then_inc(x_ready, 1)

        T_INDEX = (0, 1, 2, 3, None, 4, 5, 6)
        SPLIT = (0, 2, 5, 6, 7)

        def transpose_x(pe, gen):
            src = y3 if gen else x3
            if not gen:
                pe.wait_ge(ident_in, 16)
                pe.wait_ge(x_in, 16 * NT)
            for i in range(NT):
                if gen:
                    pe.wait_ge((xhat_act, xhat_vec)[i], gen)
            for k in range(KD):
                for i in range(NT):
                    last = nc.tensor.transpose(ps[k // 2][:, (k % 2) * SEQ + i * P:(k % 2) * SEQ + (i + 1) * P],
                                               src[:, i, k * P:(k + 1) * P], ident)
                if k % 2:
                    last.then_inc(xT_psum, 1)

        def xT_scalar(act, gen):
            for k in range(KD) if gen in SPLIT else (0, 1, 4, 5):
                act.wait_ge(xT_psum, KD // 2 * T_INDEX[gen] + k // 2 + 1)
                src = ps[k // 2][:, k % 2 * SEQ:(k % 2 + 1) * SEQ]
                if gen:
                    g, b = ln_col(gen - 1)
                    nc.scalar.activation(xT3[:, k, :], src, ACT.Identity, bias=ln_cols[:, b + k:b + k + 1],
                                         scale=ln_cols[:, g + k:g + k + 1]).then_inc(xT_act, 1)
                else:
                    nc.scalar.activation(xT3[:, k, :], src, ACT.Copy).then_inc(xT_act, 1)

        def xT_vector(dve, gen):
            if gen in SPLIT:
                split_T(dve, "x", gen, xT3, xT_act, xT_acts(gen) - KD)
                return
            for k in (2, 3, 6, 7):
                dve.wait_ge(xT_psum, KD // 2 * T_INDEX[gen] + k // 2 + 1)
                src = ps[k // 2][:, k % 2 * SEQ:(k % 2 + 1) * SEQ]
                if gen:
                    g, b = ln_col(gen - 1)
                    nc.vector.tensor_scalar(xT3[:, k, :], src, ln_cols[:, g + k:g + k + 1],
                                            ln_cols[:, b + k:b + k + 1], ALU.mult, ALU.add).then_inc(xT_vec, 1)
                else:
                    nc.vector.tensor_copy(xT3[:, k, :], src).then_inc(xT_vec, 1)

        SPLIT_ORDER = [("x", 0), ("z", 0), ("x", 2), ("z", 1), ("x", 5), ("x", 6), ("z", 2), ("x", 7)]

        def split_before(kind, n):
            return 4 * SPLIT_ORDER.index((kind, n))

        def split_T(dve, kind, m, src, ready, before):
            n = split_before(kind, m)
            for b in range(4):
                c = slice(2 * b, 2 * b + 2)
                dve.wait_ge(ready, before + 2 * b + 2)
                nc.vector.tensor_copy(xT_hi3[:, c, :], src[:, c, :]).then_inc(xhi_vec, 1)
                dve.wait_ge(xhi_vec, n + b + 1)
                nc.vector.tensor_tensor(xT_lo3[:, c, :], src[:, c, :], xT_hi3[:, c, :].bitcast(F32),
                                        ALU.subtract).then_inc(xlo_ready, 1)

        def xT_acts(gen):
            return sum((KD if g in SPLIT else KD // 2) for g in range(gen + 1) if T_INDEX[g] is not None)

        def xT_vecs(gen):
            return sum(0 if g in SPLIT else KD // 2 for g in range(gen + 1) if T_INDEX[g] is not None)

        def wait_xT(eng, gen):
            eng.wait_ge(xT_act, xT_acts(gen))
            eng.wait_ge(xT_vec, xT_vecs(gen))

        def ln_col(n):
            if n < 4:
                return 8 * n, 32 + 8 * n
            layer, ffn = (n - 4) // 2, (n - 4) % 2
            return (96 if ffn else 64) + 8 * layer, (112 if ffn else 80) + 8 * layer

        def ln_dram_rows(n):
            if n < 4:
                g, b = a["ln_g"][n // 2, n % 2], a["ln_b"][n // 2, n % 2]
            else:
                kind = "ffn" if n % 2 else "mix"
                g, b = a[f"ln_{kind}_g_2"][(n - 4) // 2], a[f"ln_{kind}_b_2"][(n - 4) // 2]
            return g.rearrange("(o d) -> o d", o=1), b.rearrange("(o d) -> o d", o=1)

        def token_major(pe, us, i, bank):
            for n, u in enumerate(us):
                pe.wait_ge(slot_landed[u.slot], u.landed)
                w = slot(u, KD // 2)
                for k in range(KD // 2):
                    kk = n * KD // 2 + k
                    last = nc.tensor.matmul(ps[bank][:, :], xT3[:, kk, i * P:(i + 1) * P], w[:, k, :],
                                            start=(kk == 0), stop=(kk == KD - 1))
            if i == NT - 1:
                last.then_inc(unit_done, 2)

        def residual(dve, sem_at, link, gen):
            if gen:
                dve.wait_ge(x_ready, NT * gen)
            for u in range(2):
                dve.wait_ge(*sem_at[u])
                for i in range(NT):
                    c = slice(u * HALF, (u + 1) * HALF)
                    ins = nc.vector.scalar_tensor_tensor(y3[:, i, c], x3[:, i, c], ALPHA, ps[4 + 2 * u + i][:, :],
                                                         ALU.mult, ALU.add)
                    link(ins) if i else ins
                if u == 0 and sem_at[0] != sem_at[1]:
                    for i in range(NT):
                        ins = nc.vector.bn_stats(stats[:, i * 12:i * 12 + 6], y3[:, i, 0:HALF])
                    link(ins)

        def mixer_sync(sp, us, w_in, w_out, n_feature):
            n = 0
            for src, blocks in ((w_in, 6), (w_out, 2)):
                src = src.rearrange("(k p) n -> p k n", p=P)
                for b in range(blocks):
                    for half in range(2):
                        u = us[n]
                        wait_free(sp, u)
                        if n < 2 * n_feature:
                            part = src[:, :, b * HALF + half * 256:b * HALF + (half + 1) * 256]
                        else:
                            part = src[:, half * KD // 2:(half + 1) * KD // 2, b * HALF:(b + 1) * HALF]
                        sp.dma_start(slot(u, part.shape[1]), part).then_inc(slot_landed[u.slot], 16)
                        n += 1

        def wait_free(sp, u):
            if u.n >= RING:
                sp.wait_ge(unit_done, u.free_at())

        z_ready = sem("z_ready")
        zT_psum, zT_act = sem("zT_psum"), sem("zT_act")

        def transpose_z(pe, m):
            pe.wait_ge(z_ready, NT * (m + 1))
            for k in range(KD):
                for i in range(NT):
                    last = nc.tensor.transpose(ps[k // 2][:, (k % 2) * SEQ + i * P:(k % 2) * SEQ + (i + 1) * P],
                                               y3[:, i, k * P:(k + 1) * P], ident)
                if k % 2:
                    last.then_inc(zT_psum, 1)

        def zT_scalar(act, m, zT, col):
            for k in range(KD):
                act.wait_ge(zT_psum, KD // 2 * m + k // 2 + 1)
                nc.scalar.activation(zT[:, k, :], ps[k // 2][:, k % 2 * SEQ:(k % 2 + 1) * SEQ], ACT.Copy,
                                     scale=col(k)).then_inc(zT_act, 1)

        def zT_vector(dve, m, zT):
            split_T(dve, "z", m, zT, zT_act, KD * m)

        MIX_CHUNKS, FFN_CHUNKS = 32, 3 * NF
        chunk0, chunks = {}, 0
        for name, count in (("ml", MIX_CHUNKS), ("gla", 16), ("ffn0", FFN_CHUNKS), ("att", MIX_CHUNKS),
                            ("ffn1", FFN_CHUNKS)):
            chunk0[name], chunks = chunks, chunks + count

        def split_hi(act, u, g, raw, buf, at, first=False):
            act.wait_ge(slot_landed[u.slot], u.landed_at(g))
            if not first:
                act.wait_ge(chunk_done, at - 1)
            dst = w_parts[0][:, buf, :].rearrange("p (k n) -> p k n", k=raw.shape[1])
            nc.scalar.activation(dst, raw, ACT.Copy).then_inc(hi_ready, 1)

        def split_lo(dve, raw, buf, at):
            dve.wait_ge(hi_ready, at + 1)
            hi, lo = (w[:, buf, :].rearrange("p (k n) -> p k n", k=raw.shape[1]) for w in w_parts)
            nc.vector.tensor_tensor(lo, raw, hi.bitcast(F32), ALU.subtract).then_inc(split_ready, 1)

        class Mixer:

            def __init__(self, units, n_feature, at):
                self.units, self.n_feature, self.at = units, n_feature, at

            def raw(self, c):
                u = self.units[c // 2]
                if c // 4 < self.n_feature:
                    return slot(u, KD)[:, :, c % 2 * P:(c % 2 + 1) * P]
                return slot(u, KD // 2)[:, c % 2 * 2:c % 2 * 2 + 2, :]

            def done(self, c):
                return self.at + c + 1

            def hi(self, act, *chunks):
                for c in chunks:
                    split_hi(act, self.units[c // 2], 0, self.raw(c), c % 2, self.at + c, first=self.at + c < 2)

            def lo(self, dve, *chunks):
                for c in chunks:
                    split_lo(dve, self.raw(c), c % 2, self.at + c)

            def products(self, pe, c, todo, operand):
                pe.wait_ge(split_ready, self.at + c + 1)
                for n, (dst, cols, act_at, start, stop, weights_first) in enumerate(todo):
                    if operand and (start or act_at[1] % 2 == 0):
                        pe.wait_ge(xlo_ready, split_before(*operand) + act_at[1] // 2 + 1)
                    for p, (wp, xp) in enumerate(PARTS):
                        ops = [w_parts[wp][:, c % 2, cols], (xT_hi3, xT_lo3)[xp][act_at]]
                        last = nc.tensor.matmul(dst, *(ops if weights_first else ops[::-1]),
                                                start=(start and p == 0), stop=(stop and p == 2))
                        if c % 2 and n == 0 and p == 0:
                            last.then_inc(unit_done, 1)
                last.then_inc(chunk_done, 1)

            def feature_chunk(self, pe, c, bank, operand=None):
                self.products(pe, c, [(ps[bank][:, c % 2 * SEQ:(c % 2 + 1) * SEQ], slice(k * P, (k + 1) * P),
                                       (slice(None), k), k == 0, k == KD - 1, True) for k in range(KD)], operand)

            def token_chunk(self, pe, c, banks, operand=None):
                self.products(pe, c, [(ps[banks[i]][:, :], slice(k2 * HALF, (k2 + 1) * HALF),
                                       (slice(None), c % 4 * 2 + k2, slice(i * P, (i + 1) * P)),
                                       c % 4 * 2 + k2 == 0, c % 4 * 2 + k2 == KD - 1, False)
                                      for i in range(NT) for k2 in range(2)], operand)

            def token_block(self, pe, b, banks, operand=None):
                for c in range(4 * b, 4 * b + 4):
                    self.token_chunk(pe, c, banks, operand)

        hstat_ready, hstd_ready, hrstd_ready = (sem(s) for s in ("hstat_ready", "hstd_ready", "hrstd_ready"))

        ar = Arena()
        ml_qkT = ar(2 * 4 * SEQ)
        ml_q = ml_qkT[:, 0:1024].rearrange("p (h t) -> p h t", h=4)
        ml_k = ml_qkT[:, 1024:2048].rearrange("p (h t) -> p h t", h=4)
        ml_zT = ml_qkT.rearrange("p (k t) -> p k t", k=KD)
        ml_v = ar(NT * D).rearrange("p (i d) -> p i d", i=NT)
        ml_o = ar(NT * D).rearrange("p (i d) -> p i d", i=NT)
        ml_A = ar(4 * 2 * 384).rearrange("p (h d c) -> p h d c", h=4, d=2)
        row = lambda: ar(2 * SEQ)[0:HEADS, :].rearrange("p (d t) -> p d t", d=2)
        r_i, r_f, r_e, r_l, r_B = (row() for _ in range(5))
        r_a, r_M, r_nm = r_e, r_f, r_l
        ml_t = ar(4 * DV).rearrange("p (h c) -> p h c", h=4)
        a_col = small[:, 0:16].rearrange("p (i d h) -> p i d h", i=2, d=2)
        em_col = small[:, 16:32].rearrange("p (i d h) -> p i d h", i=2, d=2)
        den_c = small[:, 32:48].rearrange("p (i h d) -> p i h d", i=2, d=2)
        gates_psum, gates_in, gate_rows, cols_psum = sem("gates_psum"), sem("gates_in"), sem("gate_rows"), sem("cols_psum")
        cols_ready, em_ready = sem("cols_ready"), sem("em_ready")
        q_ready, k_ready, sc_psum, bc_psum = sem("q_ready"), sem("k_ready"), sem("sc_psum"), sem("bc_psum")
        arg_ready, w_exp, w_masked, w_ready = sem("arg_ready"), sem("w_exp"), sem("w_masked"), sem("w_ready")
        v_ready, o_ready = sem("v_ready"), sem("o_ready")
        den_psum, num_psum, den_ready, bpart_ready, h_done = (sem(s) for s in ("den_psum", "num_psum", "den_ready",
                                                                               "bpart_ready", "h_done"))
        gate_act = sem("gate_act")
        rel_row = y[0:A_HEADS, 0:3 * P]
        neglam, lam_e, sub_g = small[:, 54:55], small[:, 56:58], small[:, 58:59]
        lam_ready, lam_exp = sem("lam_ready"), sem("lam_exp")
        AV_BANK = {(i, h): (h if i == 0 else (5, 6, 7, 0)[h]) for i in range(NT) for h in range(4)}

        ml_mix = Mixer(ml_u, 2, chunk0["ml"])

        def ml_tensor(pe):
            wait_xT(pe, 0)
            pe.wait_ge(gate_in, 32)
            for kk in range(KD):
                for t in range(2):
                    for d in range(2):
                        g = 2 * t + d
                        last = nc.tensor.matmul(ps[4][32 * g:32 * g + 4, 0:SEQ],
                                                gate_w[:, kk * 16 + d * 8 + t * 4:kk * 16 + d * 8 + t * 4 + 4],
                                                xT3[:, kk, :], start=(kk == 0), stop=(kk == KD - 1),
                                                tile_position=(0, 32 * g))
            last.then_inc(gates_psum, 1)
            for c in range(8):
                ml_mix.feature_chunk(pe, c, c // 2, None if c else ("x", 0))
            pe.wait_ge(gate_rows, 2)
            pe.wait_ge(q_ready, 2)
            for i in range(NT):
                for d in range(2):
                    for n, r in enumerate((r_a, r_nm)):
                        c = n * 16 + i * 8 + d * 4
                        nc.tensor.transpose(ps[1][:, c:c + 4], r[:, d, i * P:(i + 1) * P], ident[0:4, 0:4])
            pe.wait_ge(par_in, PAR)
            nc.tensor.transpose(ps[1][:, P:2 * P], ln_rows[:, :], ident)
            nc.tensor.transpose(ps[1][:, 2 * P:2 * P + 33], mix_rows[0:33, :], ident[0:33, 0:33])
            pe.wait_ge(misc_in, MISC)
            pe.wait_ge(const_ready, 2)
            nc.tensor.matmul(ps[0][0:A_HEADS, 0:3 * P], rel_t[0:BUCKETS + 1, :], cst[0:BUCKETS + 1, C_REL:C_REL + 3 * P],
                             start=True, stop=True).then_inc(cols_psum, 1)
            pe.wait_ge(k_ready, 2)
            pe.wait_ge(gates_in, 4)
            for h in range(4):
                for s in range(NT):
                    last = nc.tensor.matmul(ps[4 + h][:, s * SEQ:(s + 1) * SEQ], ml_k[:, h, s * P:(s + 1) * P],
                                            ml_q[:, h, :], start=True, stop=True)
                last.then_inc(sc_psum, 1)

            def broadcast(h):
                if h >= 2:
                    pe.wait_ge(arg_ready, h - 1)
                for d in range(2):
                    last = nc.tensor.matmul(ps[2 + h % 2][:, d * SEQ:(d + 1) * SEQ],
                                            cst[0:4, C_SEL + h * P:C_SEL + (h + 1) * P], r_M[:, d, :],
                                            start=True, stop=True)
                last.then_inc(bc_psum, 1)

            broadcast(0)
            broadcast(1)
            pe.wait_ge(cols_ready, 1)
            ml_mix.token_block(pe, 2, (0, 1))
            broadcast(2)
            broadcast(3)
            pe.wait_ge(v_ready, 2)
            ml_mix.token_block(pe, 3, (0, 1))
            pe.wait_ge(arg_ready, 4)
            ml_mix.token_block(pe, 4, (2, 3))
            pe.wait_ge(v_ready, 4)
            ml_mix.token_block(pe, 5, (0, 1))
            pe.wait_ge(w_ready, 4)
            blocks = {(0, 0): [(0, 0)], (0, 1): [(0, 128), (1, 256)], (1, 0): [(0, 0), (1, 128)], (1, 1): [(1, 256)]}
            for i in range(NT):
                for h in range(4):
                    for d in range(2):
                        todo = blocks[d, i]
                        for n, (s, c) in enumerate(todo):
                            last = nc.tensor.matmul(ps[4][:, i * 8 + h * 2 + d:i * 8 + h * 2 + d + 1],
                                                    ml_A[:, h, d, c:c + P], ones[:, 0:1],
                                                    start=(n == 0), stop=(n == len(todo) - 1))
            last.then_inc(den_psum, 1)
            pe.wait_ge(o_ready, 4)
            for i in range(NT):
                for h in range(4):
                    if i == 1 and h == 3:
                        pe.wait_ge(h_done, 1)
                    for d in range(2):
                        todo = blocks[d, i]
                        for n, (s, c) in enumerate(todo):
                            last = nc.tensor.matmul(ps[AV_BANK[i, h]][:, d * DV:(d + 1) * DV],
                                                    ml_A[:, h, d, c:c + P], ml_v[:, s, h * DV:(h + 1) * DV],
                                                    start=(n == 0), stop=(n == len(todo) - 1))
                    last.then_inc(num_psum, 1)
            transpose_z(pe, 0)
            for u in range(2):
                ml_mix.token_block(pe, 6 + u, (4 + 2 * u, 5 + 2 * u), None if u else ("z", 0))

        def ml_scalar(act):
            hi = ml_mix.hi
            hi(act, *range(4))
            act.wait_ge(gate_rows, 1)
            nc.scalar.activation(r_e, r_e, ACT.Exp).then_inc(gate_act, 1)
            act.wait_ge(gate_act, 1)
            nc.scalar.activation(r_l, r_e, ACT.Ln, bias=ones[0:4, 0:1]).then_inc(gate_act, 1)
            for b in range(2):
                hi(act, 2 * b + 4)
                act.wait_ge(chunk_done, ml_mix.done(2 * b + 1))
                nc.scalar.activation(ml_qkT[:, b * HALF:(b + 1) * HALF], ps[b][:, :], ACT.Copy,
                                     scale=DK ** -0.5).then_inc(q_ready, 1)
                hi(act, 2 * b + 5)
            for b in range(2):
                act.wait_ge(chunk_done, ml_mix.done(2 * b + 5))
                nc.scalar.activation(ml_qkT[:, 1024 + b * HALF:1024 + (b + 1) * HALF], ps[2 + b][:, :],
                                     ACT.Copy).then_inc(k_ready, 1)
            hi(act, 8, 9)
            act.wait_ge(cols_ready, 1)
            nc.scalar.activation(em_col, em_col, ACT.Exp).then_inc(em_ready, 1)
            act.dma_start(rel_dram.rearrange("h (p c) -> h p c", p=P),
                          rel_row[:, None, :].broadcast_to([A_HEADS, P, 3 * P])).then_inc(rel_out, 16)

            def weights(h):
                act.wait_ge(arg_ready, h + 1)
                nc.scalar.activation(ml_A[:, h], ml_A[:, h], ACT.Exp).then_inc(w_exp, 1)

            def values(u):
                act.wait_ge(chunk_done, ml_mix.done(11 + 4 * u))
                for i in range(NT):
                    nc.scalar.activation(ml_v[:, i, u * HALF:(u + 1) * HALF], ps[i][:, :],
                                         ACT.Copy).then_inc(v_ready, 1)

            weights(0)
            hi(act, 10)
            weights(1)
            hi(act, 11, 12, 13)
            values(0)
            weights(2)
            hi(act, 14, 15)
            weights(3)
            hi(act, 16, 17)
            values(1)
            hi(act, 18, 19)
            act.wait_ge(lam_ready, 1)
            nc.scalar.activation(lam_e, lam_e, ACT.Exp).then_inc(lam_exp, 1)
            for u in range(2):
                hi(act, *range(20 + 4 * u, 22 + 4 * u), *((22, 23) if u == 0 else ()))
                act.wait_ge(chunk_done, ml_mix.done(19 + 4 * u))
                for i in range(NT):
                    nc.scalar.activation(ml_o[:, i, u * HALF:(u + 1) * HALF], ps[(2 if u == 0 else 0) + i][:, :],
                                         ACT.Sigmoid).then_inc(o_ready, 1)
            act.wait_ge(den_ready, 1)

            def backward_part(i, h):
                act.wait_ge(num_psum, 4 * i + h + 1)
                if i == 1:
                    act.wait_ge(h_done, h + 1)
                nc.scalar.activation(ml_t[:, h, :], ps[AV_BANK[i, h]][:, DV:2 * DV], ACT.Copy,
                                     scale=den_c[:, i, h, 1:2]).then_inc(bpart_ready, 1)

            for h in range(HEADS):
                backward_part(0, h)
            head_std(act, 0, 0)
            for h in range(HEADS):
                backward_part(1, h)
                if h >= 2:
                    for hh in range(2):
                        head_scale(act, 0, 2 * h - 4 + hh)
            head_std(act, 0, 1)
            zT_scalar(act, 0, ml_zT, lambda k: mix_cols[:, k:k + 1])
            hi(act, *range(26, 32))

        def head_std(act, m, i):
            act.wait_ge(hstat_ready, NT * m + i + 1)
            nc.scalar.activation(std[:, 4 * i:4 * i + 4], mv[:, 8 * i:8 * i + 8].rearrange("p (h s) -> p h s", s=2)[:, :, 1],
                                 ACT.Sqrt, bias=eps).then_inc(hstd_ready, 1)

        def head_scale(act, m, h):
            act.wait_ge(hrstd_ready, NT * m + 1)
            ins = nc.scalar.activation(y3[:, 0, h * DV:(h + 1) * DV], y3[:, 0, h * DV:(h + 1) * DV], ACT.Copy,
                                       scale=rstd[:, h:h + 1])
            if h == HEADS - 1:
                ins.then_inc(z_ready, 1)

        def head_stats(i):
            for h in range(HEADS):
                ins = nc.vector.bn_aggr(mv[:, 8 * i + 2 * h:8 * i + 2 * h + 2], stats[:, i * 24 + h * 6:i * 24 + h * 6 + 6])
            ins.then_inc(hstat_ready, 1)

        def head_center(i, h, src, gate):
            return nc.vector.scalar_tensor_tensor(y3[:, i, h * DV:(h + 1) * DV], src, mv[:, 8 * i + 2 * h:8 * i + 2 * h + 1],
                                                  gate[:, i, h * DV:(h + 1) * DV], ALU.subtract, ALU.mult)

        def head_rstd(dve, m, i):
            dve.wait_ge(hstd_ready, NT * m + i + 1)
            nc.vector.reciprocal(rstd[:, 4 * i:4 * i + 4], std[:, 4 * i:4 * i + 4]).then_inc(hrstd_ready, 1)

        def head_scale_vector(dve, m):
            dve.wait_ge(hrstd_ready, NT * m + 2)
            for h in range(HEADS):
                ins = nc.vector.tensor_scalar(y3[:, 1, h * DV:(h + 1) * DV], y3[:, 1, h * DV:(h + 1) * DV],
                                              rstd[:, 4 + h:5 + h], None, ALU.mult)
            ins.then_inc(z_ready, 1)

        def ml_vector(dve, link):
            lo = ml_mix.lo
            lo(dve, 0, 1)
            dve.wait_ge(gates_psum, 1)
            dve.wait_ge(gate_in, 32)
            for t, r in enumerate((r_i, r_f)):
                for d in range(2):
                    g = 2 * t + d
                    ins = nc.vector.tensor_scalar(r[:, d, :], ps[4][32 * g:32 * g + 4, 0:SEQ],
                                                  gate_b[0:4, 2 * d + t:2 * d + t + 1], None, ALU.add)
                    ins.then_inc(gates_in, 1)
            dve.wait_ge(gates_in, 4)
            nc.vector.scalar_tensor_tensor(r_e, r_f, -1.0, r_f, ALU.mult, ALU.min).then_inc(gate_rows, 1)
            lo(dve, 2, 3)
            dve.wait_ge(gate_act, 2)
            link(nc.vector.scalar_tensor_tensor(r_l, r_f, 0.0, r_l, ALU.min, ALU.subtract))
            order = (slice(None), slice(None, None, -1))
            for d in range(2):
                ins = nc.vector.tensor_tensor_scan(r_B[:, d, order[d]], ones[0:4, :], r_l[:, d, order[d]], 0.0,
                                                   ALU.mult, ALU.add)
            link(ins)
            link(nc.vector.tensor_tensor(r_a, r_i, r_B, ALU.subtract))
            lo(dve, 4)
            for d in range(2):
                ins = nc.vector.tensor_tensor_scan(r_M[:, d, order[d]], ones[0:4, :], r_a[:, d, order[d]], 0.0,
                                                   ALU.mult, ALU.max)
            link(ins)
            link(nc.vector.scalar_tensor_tensor(r_nm, r_B, -1.0, r_M, ALU.mult, ALU.subtract))
            nc.vector.tensor_scalar(r_M, r_M, -1.0, None, ALU.mult).then_inc(gate_rows, 1)
            lo(dve, *range(5, 10))
            dve.wait_ge(cols_psum, 1)
            nc.vector.tensor_copy(small[:, 0:32], ps[1][:, 0:32])
            nc.vector.tensor_copy(ln_cols[:, :], ps[1][:, P:2 * P])
            nc.vector.tensor_copy(mix_cols[:, :], ps[1][:, 2 * P:2 * P + 33])
            nc.vector.tensor_copy(rel_row, ps[0][0:A_HEADS, 0:3 * P]).then_inc(cols_ready, 1)
            dve.wait_ge(cols_ready, 1)

            def args(h):
                dve.wait_ge(bc_psum, h + 1)
                for d, s, t0, n, c in ((0, 0, 0, 256, 0), (0, 1, 128, 128, 256), (1, 0, 0, 128, 0), (1, 1, 0, 256, 128)):
                    ins = nc.vector.tensor_scalar(ml_A[:, h, d, c:c + n], ps[2 + h % 2][:, d * SEQ + t0:d * SEQ + t0 + n],
                                                  a_col[:, s, d, h:h + 1], 0.0, ALU.add, ALU.min)
                ins.then_inc(arg_ready, 1)

            def apply(h):
                dve.wait_ge(w_masked, 2 * h + 2)
                dve.wait_ge(sc_psum, h + 1)
                for d, s, t0, n, c in ((0, 0, 0, 256, 0), (0, 1, 128, 128, 256), (1, 0, 0, 128, 0), (1, 1, 0, 256, 128)):
                    ins = nc.vector.tensor_tensor(ml_A[:, h, d, c:c + n], ml_A[:, h, d, c:c + n],
                                                  ps[4 + h][:, s * SEQ + t0:s * SEQ + t0 + n], ALU.mult)
                ins.then_inc(w_ready, 1)

            args(0)
            args(1)
            lo(dve, *range(10, 14))
            args(2)
            apply(0)
            args(3)
            lo(dve, 14, 15)
            apply(1)
            lo(dve, 16, 17)
            apply(2)
            apply(3)
            nc.vector.tensor_scalar(sub_g, mix_cols[:, 24:25], 1.0 - LAMBDA_INIT, None, ALU.mult)
            dve.wait_ge(misc_in, MISC)
            lp = lam_p[:, :].rearrange("p (n a c) -> p n a c", n=2, a=2)
            link(nc.vector.tensor_tensor(lp[:, :, 0, :], lp[:, :, 0, :], lp[:, :, 1, :], ALU.mult))
            nc.vector.tensor_reduce(lam_e, lp[:, :, 0, :], AX.X, ALU.add).then_inc(lam_ready, 1)
            lo(dve, 18, 19)
            dve.wait_ge(lam_exp, 1)
            link(nc.vector.tensor_tensor(neglam, lam_e[:, 1:2], lam_e[:, 0:1], ALU.subtract))
            link(nc.vector.tensor_scalar(neglam, neglam, -LAMBDA_INIT, None, ALU.add))
            lo(dve, *range(20, 26))
            dve.wait_ge(den_psum, 1)
            dve.wait_ge(em_ready, 1)
            den_v = small[:, 32:48]
            link(nc.vector.tensor_copy(den_v, ps[4][:, 0:16]))
            link(nc.vector.scalar_tensor_tensor(den_v, den_v, -1.0, den_v, ALU.mult, ALU.max))
            for i in range(NT):
                ins = nc.vector.tensor_tensor(den_c[:, i], den_c[:, i], em_col[:, i].rearrange("p d h -> p h d"), ALU.max)
            link(ins)
            nc.vector.reciprocal(den_v, den_v).then_inc(den_ready, 1)
            dve.wait_ge(den_ready, 1)
            dve.wait_ge(rel_out, 16)
            dve.wait_ge(o_ready, 4)

            def head(i, h):
                dve.wait_ge(bpart_ready, 4 * i + h + 1)
                nc.vector.scalar_tensor_tensor(y3[:, i, h * DV:(h + 1) * DV], ps[AV_BANK[i, h]][:, 0:DV],
                                               den_c[:, i, h, 0:1], ml_t[:, h, :], ALU.mult, ALU.add).then_inc(h_done, 1)
                dve.wait_ge(h_done, 4 * i + h + 1)
                return nc.vector.bn_stats(stats[:, i * 24 + h * 6:i * 24 + h * 6 + 6], y3[:, i, h * DV:(h + 1) * DV])

            center = lambda i, h: head_center(i, h, y3[:, i, h * DV:(h + 1) * DV], ml_o)
            for h in range(HEADS):
                ins = head(0, h)
            link(ins)
            head_stats(0)
            dve.wait_ge(hstat_ready, 1)
            for h in range(HEADS):
                ins = head(1, h)
                if h < 2:
                    center(0, 2 * h)
                    ins = center(0, 2 * h + 1)
                if h == 1:
                    head_rstd(dve, 0, 0)
            link(ins)
            head_stats(1)
            dve.wait_ge(hstat_ready, 2)
            for h in range(HEADS):
                center(1, h)
            head_rstd(dve, 0, 1)
            head_scale_vector(dve, 0)
            zT_vector(dve, 0, ml_zT)
            lo(dve, *range(26, 32))
            residual(dve, [(chunk_done, ml_mix.done(c)) for c in (27, 31)], link, 0)

        def ml_gpsimd(pool):
            for h in range(4):
                pool.wait_ge(w_exp, h + 1)
                for d in range(2):
                    v = ml_A[:, h, d].rearrange("p (b t) -> p b t", t=P)[:, 0:3:2, :]
                    sign = 1 if d == 0 else -1
                    nc.gpsimd.affine_select(out=v, in_=v, compare_op=ALU.is_ge, fill=0.0, base=0,
                                            pattern=[[0, 2], [sign, P]], channel_multiplier=-sign).then_inc(w_masked, 1)

        def ml_sync(sp):
            mixer_sync(sp, ml_u, a["mlstm_w_in"][0], a["mlstm_w_out"][0], 2)

        ar = Arena()
        xin = ar(KD * SLOTS_E).rearrange("p (k c) -> p k c", k=KD)
        silu = ar(2 * HALF).rearrange("p (b n) -> p b n", b=2)
        hmid = ar(2 * HALF).rearrange("p (b n) -> p b n", b=2)
        hT = ar(2 * HALF).rearrange("p (b c) -> p b c", b=2)
        e_out = ar(D)
        idx_bc, gate_bc = ar(NE * CAP), ar(NE * CAP)
        pick = ar(NT * SLOTS_E).rearrange("p (i c) -> p i c", i=NT)
        pick_g = ar(NT * SLOTS_E).rearrange("p (i c) -> p i c", i=NT)
        pick_gT = ar(NT * P)
        aff = ar(NT * NE).rearrange("p (i e) -> p i e", i=NT)
        affT = [ar(SEQ)[0:NE, :] for _ in range(2)]
        top_v, top_f = ar(CAP)[0:NE, :], ar(CAP)[0:NE, :]
        top_i = ar(CAP).bitcast(U32)[0:NE, :]
        bd_i, bd_g = ar(NE * CAP)[0:NE, :], ar(NE * CAP)[0:NE, :]
        nmax, esum, ersum = small[:, 48:50], small[:, 50:52], small[:, 52:54]
        lg_psum, lmax_ready, lexp_ready, aff_ready, affT_psum = (sem(s) for s in ("lg_psum", "lmax_ready", "lexp_ready",
                                                                                  "aff_ready", "affT_psum"))
        bd_ready, bdc_psum, idxbc_ready, gatebc_ready = (sem(s) for s in ("bd_ready", "bdc_psum", "idxbc_ready",
                                                                         "gatebc_ready"))
        y_init, pick_ready, pickg_ready, gathered = (sem(s) for s in ("y_init", "pick_ready", "pickg_ready", "gathered"))
        xin_act, xin_vec, pickT_psum, pickT_ready = (sem(s) for s in ("xin_act", "xin_vec", "pickT_psum", "pickT_ready"))
        silu_ready, h_ready, hT_psum, hT_ready = (sem(s) for s in ("silu_ready", "h_ready", "hT_psum", "hT_ready"))
        eout_act, eout_vec, scattered, y_added = (sem(s) for s in ("eout_act", "eout_vec", "scattered", "y_added"))
        B_GU, B_HT, B_DN, B_GA, B_PT = (0, 1), 2, (3, 4), (5, 6), 7
        SC_BANK = ((5, 6), (3, 4))

        def moe_tensor(pe, m, gen):
            us = moe_u[m]
            wait_xT(pe, gen)
            pe.wait_ge(misc_in, MISC)
            for i in range(NT):
                for k in range(KD):
                    last = nc.tensor.matmul(ps[B_PT][:, i * NE:(i + 1) * NE], xT3[:, k, i * P:(i + 1) * P],
                                            rout_w[:, (m * KD + k) * NE:(m * KD + k + 1) * NE],
                                            start=(k == 0), stop=(k == KD - 1))
            last.then_inc(lg_psum, 1)
            pe.wait_ge(aff_ready, m + 1)
            for i in range(NT):
                last = nc.tensor.transpose(ps[B_GU[0]][0:NE, i * P:(i + 1) * P], aff[:, i, :], ident)
            last.then_inc(affT_psum, 1)
            pe.wait_ge(bd_ready, m + 1)
            nc.tensor.matmul(ps[B_GA[0]][:, :], ones[0:NE, 0:P], bd_i, start=True, stop=True)
            nc.tensor.matmul(ps[B_GA[1]][:, :], ones[0:NE, 0:P], bd_g, start=True, stop=True).then_inc(bdc_psum, 1)
            pe.wait_ge(x_ready, NT * gen)
            pe.wait_ge(idxbc_ready, m + 1)
            pe.wait_ge(gatebc_ready, m + 1)
            with pe.Fori(0, NGROUP) as g:
                pe.wait_ge(pick_ready, g + (m * NGROUP + 1))
                for k in range(KD):
                    for i in range(NT):
                        last = nc.tensor.matmul(ps[B_GA[k // 4]][:, (k % 4) * P:(k % 4 + 1) * P],
                                                x3[:, i, k * P:(k + 1) * P], pick[:, i, :],
                                                start=(i == 0), stop=(i == NT - 1))
                    if k % 4 == 3:
                        last.then_inc(gathered, 1)
                pe.wait_ge(pickg_ready, g + (m * NGROUP + 1))
                for i in range(NT):
                    last = nc.tensor.transpose(ps[B_PT][:, i * P:(i + 1) * P], pick_g[:, i, :], ident)
                last.then_inc(pickT_psum, 1)
                pe.wait_ge(xin_act, g + (m * NGROUP + 1))
                pe.wait_ge(xin_vec, g + (m * NGROUP + 1))

                def gate_up(j):
                    for part in range(4):
                        ug, uu = us[8 * j + 2 * part], us[8 * j + 2 * part + 1]
                        pe.wait_ge(slot_landed[ug.slot], ug.landed_at(g))
                        pe.wait_ge(slot_landed[uu.slot], uu.landed_at(g))
                        for k2 in range(2):
                            k = 2 * part + k2
                            for c in range(4):
                                w = slot((ug, uu)[c // 2], 2)[:, k2, (c % 2) * HALF:(c % 2 + 1) * HALF]
                                last = nc.tensor.matmul(ps[B_GU[j % 2]][32 * c:32 * c + 32, :],
                                                        xin[:, k, j * CAP:(j + 1) * CAP], w, start=(k == 0),
                                                        stop=(k == KD - 1), tile_position=(0, 32 * c))
                        last.then_inc(unit_done, 2)

                def transpose_h(pair):
                    if pair:
                        pe.wait_ge(hT_ready, g * 2 + (m * 8 + pair))
                    pe.wait_ge(h_ready, g * 4 + (m * 16 + 2 * pair + 2))
                    for c in range(4):
                        last = nc.tensor.transpose(ps[B_HT][:, c * P:(c + 1) * P], hmid[:, pair, c * P:(c + 1) * P], ident)
                    last.then_inc(hT_psum, 1)

                gate_up(0)
                gate_up(1)
                pe.wait_ge(h_ready, g * 4 + (m * 16 + 1))
                gate_up(2)
                transpose_h(0)
                gate_up(3)
                transpose_h(1)
                pe.wait_ge(hT_ready, g * 2 + (m * 8 + 2))
                for part in range(4):
                    ud = us[32 + 4 * part:36 + 4 * part]
                    for u in ud:
                        pe.wait_ge(slot_landed[u.slot], u.landed_at(g))
                    for f2 in range(2):
                        half, f = part // 2, 2 * (part % 2) + f2
                        for c in range(2):
                            for j in range(GROUP):
                                last = nc.tensor.matmul(ps[B_DN[c]][32 * j:32 * j + 32, :],
                                                        hT[:, j // 2, f * P + (j % 2) * 64 + half * 32:f * P + (j % 2) * 64 + half * 32 + 32],
                                                        slot(ud[j], 2)[:, f2, c * HALF:(c + 1) * HALF],
                                                        start=(half == 0 and f == 0), stop=(half == 1 and f == 3),
                                                        tile_position=(0, 32 * j))
                    last.then_inc(unit_done, 4)
                pe.wait_ge(pickT_ready, g + (m * NGROUP + 1))
                pe.wait_ge(eout_act, g + (m * NGROUP + 1))
                pe.wait_ge(eout_vec, g + (m * NGROUP + 1))
                for i in range(NT):
                    for c in range(2):
                        nc.tensor.matmul(ps[SC_BANK[i][c]][:, :], pick_gT[:, i * P:(i + 1) * P],
                                         e_out[:, c * HALF:(c + 1) * HALF], start=True, stop=True).then_inc(scattered, 1)
                pe.wait_ge(y_added, g * 4 + (m * 16 + 4))

        def moe_scalar(act, m):
            act.wait_ge(lmax_ready, m + 1)
            for i in range(NT):
                ins = nc.scalar.activation(aff[:, i, :], ps[B_PT][:, i * NE:(i + 1) * NE], ACT.Exp, bias=nmax[:, i:i + 1],
                                           accum_out=esum[:, i:i + 1])
            ins.then_inc(lexp_ready, 1)
            act.wait_ge(bdc_psum, m + 1)
            nc.scalar.activation(idx_bc, ps[B_GA[0]][:, :], ACT.Copy).then_inc(idxbc_ready, 1)
            us = moe_u[m]
            with act.Fori(0, NGROUP) as g:
                act.wait_ge(gathered, g * 2 + (m * NGROUP * 2 + 1))
                nc.scalar.activation(xin[:, 0:4, :], ps[B_GA[0]][:, :].rearrange("p (k c) -> p k c", k=4),
                                     ACT.Copy).then_inc(xin_act, 1)
                act.wait_ge(pickT_psum, g + (m * NGROUP + 1))
                nc.scalar.activation(pick_gT, ps[B_PT][:, 0:SEQ], ACT.Copy).then_inc(pickT_ready, 1)
                for j in range(GROUP):
                    act.wait_ge(unit_done, us[8 * j + 7].done_at(g))
                    nc.scalar.activation(silu[64:128, j % 2, :], ps[B_GU[j % 2]][0:64, :], ACT.Silu).then_inc(silu_ready, 1)
                act.wait_ge(unit_done, us[MOE_UNITS - 1].done_at(g))
                nc.scalar.activation(e_out[:, 0:HALF], ps[B_DN[0]][:, :], ACT.Copy).then_inc(eout_act, 1)

        def moe_vector(dve, link, m):
            dve.wait_ge(lg_psum, m + 1)
            nc.vector.tensor_reduce(nmax, ps[B_PT][:, 0:NT * NE].rearrange("p (i e) -> p i e", i=NT), AX.X, ALU.max,
                                    negate=True).then_inc(lmax_ready, 1)
            dve.wait_ge(lexp_ready, m + 1)
            link(nc.vector.reciprocal(ersum, esum))
            for i in range(NT):
                ins = nc.vector.tensor_scalar(aff[:, i, :], aff[:, i, :], ersum[:, i:i + 1], None, ALU.mult)
            ins.then_inc(aff_ready, 1)
            dve.wait_ge(affT_psum, m + 1)
            link(nc.vector.tensor_copy(affT[0], ps[B_GU[0]][0:NE, 0:SEQ]))
            for r in range(CAP // 8):
                c, src, dst = slice(8 * r, 8 * r + 8), affT[r % 2], affT[1 - r % 2]
                link(nc.vector.max(top_v[:, c], src))
                ins = nc.vector.max_index(top_i[:, c], top_v[:, c], src)
                if r < CAP // 8 - 1:
                    ins = nc.vector.match_replace(dst, top_v[:, c], src, -1.0)
                link(ins)
            link(nc.vector.tensor_copy(top_f, top_i))
            eye3 = eye16.rearrange("p (e c) -> p e c", e=NE)
            for src, dst in ((top_f, bd_i), (top_v, bd_g)):
                ins = nc.vector.tensor_tensor(dst.rearrange("p (e c) -> p e c", e=NE), eye3,
                                              src[:, None, :].broadcast_to([NE, NE, CAP]), ALU.mult)
            ins.then_inc(bd_ready, 1)
            dve.wait_ge(bdc_psum, m + 1)
            nc.vector.tensor_copy(gate_bc, ps[B_GA[1]][:, :]).then_inc(gatebc_ready, 1)
            dve.wait_ge(gatebc_ready, m + 1)
            dve.wait_ge(idxbc_ready, m + 1)
            dve.wait_ge(y_init, NT * (m + 1))
            us = moe_u[m]

            def hT_copy(g, j):
                if j % 2 == 0:
                    dve.wait_ge(hT_psum, g * 2 + (m * 8 + j // 2 + 1))
                    nc.vector.tensor_copy(hT[:, j // 2, :], ps[B_HT][:, :]).then_inc(hT_ready, 1)

            with dve.Fori(0, NGROUP) as g:
                cols = bass.ts(g, SLOTS_E)
                for i in range(NT):
                    ins = nc.vector.tensor_scalar(pick[:, i, :], idx_bc[:, cols], cst[:, C_TOK + i:C_TOK + i + 1], None,
                                                  ALU.is_equal)
                ins.then_inc(pick_ready, 1)
                dve.wait_ge(pick_ready, g + (m * NGROUP + 1))
                for i in range(NT):
                    ins = nc.vector.tensor_tensor(pick_g[:, i, :], pick[:, i, :], gate_bc[:, cols], ALU.mult)
                ins.then_inc(pickg_ready, 1)
                dve.wait_ge(gathered, g * 2 + (m * NGROUP * 2 + 2))
                nc.vector.tensor_copy(xin[:, 4:8, :], ps[B_GA[1]][:, :].rearrange("p (k c) -> p k c", k=4)).then_inc(xin_vec, 1)
                for j in range(GROUP):
                    dve.wait_ge(silu_ready, g * 4 + (m * 16 + j + 1))
                    nc.vector.tensor_tensor(hmid[64 * (j % 2):64 * (j % 2) + 64, j // 2, :], silu[64:128, j % 2, :],
                                            ps[B_GU[j % 2]][64:128, :], ALU.mult).then_inc(h_ready, 1)
                    if j >= 2:
                        hT_copy(g, j - 2)
                hT_copy(g, 2)
                dve.wait_ge(unit_done, us[MOE_UNITS - 1].done_at(g))
                nc.vector.tensor_copy(e_out[:, HALF:D], ps[B_DN[1]][:, :]).then_inc(eout_vec, 1)
                for i in range(NT):
                    for c in range(2):
                        dve.wait_ge(scattered, g * 4 + (m * 16 + 2 * i + c + 1))
                        cc = slice(c * HALF, (c + 1) * HALF)
                        nc.vector.tensor_tensor(y3[:, i, cc], y3[:, i, cc], ps[SC_BANK[i][c]][:, :],
                                                ALU.add).then_inc(y_added, 1)
            dve.wait_ge(y_added, 16 * (m + 1))

        def moe_gpsimd(pool, m, gen):
            pool.wait_ge(x_ready, NT * gen)
            pool.wait_ge(xT_psum, KD // 2 * (T_INDEX[gen] + 1))
            for i in range(NT):
                nc.gpsimd.tensor_scalar(y3[:, i, :], x3[:, i, :], ALPHA, None, ALU.mult).then_inc(y_init, 1)

        def moe_sync(sp, m):
            us = moe_u[m]
            with sp.Fori(0, NGROUP) as g:
                for j in range(GROUP):
                    for part in range(4):
                        for n, name in enumerate(("moe_w_gate", "moe_w_up")):
                            u = us[8 * j + 2 * part + n]
                            sp.wait_ge(unit_done, u.free_at(g))
                            src = a[name][m, g * GROUP + j].rearrange("(k p) f -> p k f", p=P)
                            sp.dma_start(slot(u, 2), src[:, 2 * part:2 * part + 2, :]).then_inc(slot_landed[u.slot], 16)
                for part in range(4):
                    for j in range(GROUP):
                        u = us[32 + 4 * part + j]
                        sp.wait_ge(unit_done, u.free_at(g))
                        src = a["moe_w_down"][m, g * GROUP + j].rearrange("(f p) d -> p f d", p=P)
                        sp.dma_start(slot(u, 2), src[:, 2 * part:2 * part + 2, :]).then_inc(slot_landed[u.slot], 16)

        ar = Arena()
        gl_qkT = ar(2 * 4 * SEQ)
        gl_q, gl_k = gl_qkT[:, 0:1024], gl_qkT[:, 1024:2048]
        gl_zT = gl_qkT.rearrange("p (k t) -> p k t", k=KD)
        gl_v = ar(NT * D).rearrange("p (i d) -> p i d", i=NT)
        gl_r = ar(NT * D).rearrange("p (i d) -> p i d", i=NT)
        gl_z = ar(2 * 1024)
        gl_A = gl_z.rearrange("p (s h t) -> p s h t", s=NT, h=4)
        gl_B = y[:, :].rearrange("p (d c) -> p d c", d=2)
        gl_E = ar(4 * 1024).rearrange("p (b w c) -> p b w c", b=2, w=2)
        gl_l = gl_E.rearrange("p b w c -> p (b w c)")[:, 0:2048]
        glrT = gl_v[0:RANK, 0, 0:2 * SEQ].rearrange("p (d t) -> p d t", d=2)
        glr_psum, glr_ready, ga_psum, ga_in, ga_act, ga_rows = (sem(s) for s in ("glr_psum", "glr_ready", "ga_psum", "ga_in",
                                                                                 "ga_act", "ga_rows"))
        gq_ready, gk_ready, gv_ready, gr_ready = (sem(s) for s in ("gq_ready", "gk_ready", "gv_ready", "gr_ready"))
        diag_psum, diag_ready, e_arg, e_exp, kd_ready, qd_ready = (sem(s) for s in ("diag_psum", "diag_ready", "e_arg", "e_exp",
                                                                                    "kd_ready", "qd_ready"))
        lv_psum, lv_done, go_psum = sem("lv_psum"), sem("lv_done"), sem("go_psum")
        b_in = sem("b_in")

        gla_mix = Mixer(gla_u[0:4] + gla_u[12:16], 2, chunk0["gla"])

        def gla_tensor(pe, gen):
            wait_xT(pe, gen)
            for d in range(2):
                for kk in range(KD):
                    last = nc.tensor.matmul(ps[7][0:RANK, d * SEQ:(d + 1) * SEQ],
                                            glr_w[:, kk * 32 + d * RANK:kk * 32 + (d + 1) * RANK], xT3[:, kk, :],
                                            start=(kk == 0), stop=(kk == KD - 1))
            last.then_inc(glr_psum, 1)
            for c in range(4):
                gla_mix.feature_chunk(pe, c, c // 2, None if c else ("x", gen))
            pe.wait_ge(glr_ready, 1)
            for d in range(2):
                for h in range(4):
                    last = nc.tensor.matmul(ps[4 + d * 2 + h // 2][:, (h % 2) * SEQ:(h % 2 + 1) * SEQ],
                                            gk_w[0:RANK, d * QK + h * DK:d * QK + (h + 1) * DK], glrT[:, d, :],
                                            start=True, stop=True)
            last.then_inc(ga_psum, 1)
            for c in range(4, 8):
                gla_mix.feature_chunk(pe, c, c // 2)
            pe.wait_ge(gq_ready, 2)
            pe.wait_ge(gk_ready, 2)
            for i in range(NT):
                for h in range(4):
                    c = slice(h * SEQ + i * P, h * SEQ + (i + 1) * P)
                    last = nc.tensor.matmul(ps[i][:, h * P:(h + 1) * P], gl_k[:, c], gl_q[:, c], start=True, stop=True)
            last.then_inc(diag_psum, 1)
            pe.wait_ge(ga_in, 8)

            def level(n):
                pe.wait_ge(kd_ready, n + 1)
                pe.wait_ge(qd_ready, n + 1)
                if n == 0:
                    pe.wait_ge(diag_ready, 2)
                else:
                    pe.wait_ge(lv_done, 2 * n)
                for i in range(NT):
                    ti = 1 - i if LEVELS[n] == P else i
                    for h in range(4):
                        last = nc.tensor.matmul(ps[i][:, h * P:(h + 1) * P],
                                                gl_E[:, n % 2, 0, h * SEQ + i * P:h * SEQ + (i + 1) * P],
                                                gl_E[:, n % 2, 1, h * SEQ + ti * P:h * SEQ + (ti + 1) * P],
                                                start=True, stop=True)
                last.then_inc(lv_psum, 1)

            for n in range(len(LEVELS)):
                m, i = n // 2, n % 2
                if m == 3:
                    pe.wait_ge(gv_ready, i + 1)
                token_major(pe, gla_u[4 + 2 * m:6 + 2 * m], i, 2 + n % 6)
                level(n)
            pe.wait_ge(lv_done, 2 * len(LEVELS))
            pe.wait_ge(gv_ready, 4)
            pe.wait_ge(gr_ready, 4)
            for i in range(NT):
                for h in range(4):
                    for s in range(NT):
                        last = nc.tensor.matmul(ps[4 + 2 * i + h // 2][:, (h % 2) * DV:(h % 2 + 1) * DV],
                                                gl_A[:, s, h, i * P:(i + 1) * P], gl_v[:, s, h * DV:(h + 1) * DV],
                                                start=(s == 0), stop=(s == NT - 1))
                last.then_inc(go_psum, 1)
            transpose_z(pe, 1)
            for u in range(2):
                gla_mix.token_block(pe, 2 + u, (4 + 2 * u, 5 + 2 * u), None if u else ("z", 1))

        def go_bank(i, h):
            return ps[4 + 2 * i + h // 2][:, (h % 2) * DV:(h % 2 + 1) * DV]

        def gla_scalar(act):
            hi = gla_mix.hi
            hi(act, 0, 1)
            act.wait_ge(glr_psum, 1)
            nc.scalar.activation(glrT.rearrange("p d t -> p (d t)"), ps[7][0:RANK, :], ACT.Copy).then_inc(glr_ready, 1)
            hi(act, 2, 3)
            for b in range(2):
                hi(act, 4 + b)
                act.wait_ge(chunk_done, gla_mix.done(2 * b + 1))
                nc.scalar.activation(gl_q[:, b * HALF:(b + 1) * HALF], ps[b][:, :], ACT.Copy,
                                     scale=DK ** -0.5).then_inc(gq_ready, 1)
            hi(act, 6, 7)
            act.wait_ge(ga_rows, 1)
            nc.scalar.activation(gl_l, gl_l, ACT.Exp).then_inc(ga_act, 1)
            act.wait_ge(ga_act, 1)
            nc.scalar.activation(gl_l, gl_l, ACT.Ln, bias=ones[:, 0:1]).then_inc(ga_act, 1)
            for b in range(2):
                act.wait_ge(chunk_done, gla_mix.done(2 * b + 5))
                nc.scalar.activation(gl_k[:, b * HALF:(b + 1) * HALF], ps[2 + b][:, :], ACT.Copy).then_inc(gk_ready, 1)
            for n in range(len(LEVELS)):
                for w in range(2):
                    act.wait_ge(e_arg, 2 * n + w + 1)
                    nc.scalar.activation(gl_E[:, n % 2, w, :], gl_E[:, n % 2, w, :], ACT.Exp,
                                         scale=1.0 / TAU).then_inc(e_exp, 1)
                if n % 2:
                    m = n // 2
                    act.wait_ge(unit_done, gla_u[5 + 2 * m].done_at())
                    for i in range(NT):
                        src = ps[2 + 2 * m % 6 + i][:, :]
                        if m < 2:
                            nc.scalar.activation(gl_v[:, i, m * HALF:(m + 1) * HALF], src, ACT.Copy).then_inc(gv_ready, 1)
                        else:
                            nc.scalar.activation(gl_r[:, i, (m - 2) * HALF:(m - 1) * HALF], src, ACT.Silu).then_inc(gr_ready, 1)
            hi(act, 8, 9)
            act.wait_ge(x_ready, NT * 2)
            head_std(act, 1, 0)
            for h in range(HEADS):
                head_scale(act, 1, h)
            head_std(act, 1, 1)
            zT_scalar(act, 1, gl_zT, lambda k: mix_cols[:, 8 + k:9 + k])
            hi(act, *range(10, 16))

        def gla_vector(dve, link):
            lo = gla_mix.lo
            lo(dve, *range(4))
            dve.wait_ge(ga_psum, 1)
            for d in range(2):
                lo(dve, 4 + d)
                for h in range(4):
                    nc.vector.tensor_scalar(gl_z[:, d * 1024 + h * SEQ:d * 1024 + (h + 1) * SEQ],
                                            ps[4 + d * 2 + h // 2][:, (h % 2) * SEQ:(h % 2 + 1) * SEQ],
                                            mix_cols[:, 25 + d * 4 + h:26 + d * 4 + h], None, ALU.add).then_inc(ga_in, 1)
            dve.wait_ge(ga_in, 8)
            nc.vector.scalar_tensor_tensor(gl_l, gl_z, -1.0, gl_z, ALU.mult, ALU.min).then_inc(ga_rows, 1)
            lo(dve, 6, 7)
            dve.wait_ge(ga_act, 2)
            link(nc.vector.scalar_tensor_tensor(gl_z, gl_z, 0.0, gl_l, ALU.min, ALU.subtract))
            dve.wait_ge(x_ready, NT * 2)
            for d in range(2):
                for h in range(4):
                    c = slice(h * SEQ, (h + 1) * SEQ)
                    src, dst = gl_z[:, d * 1024:(d + 1) * 1024][:, c], gl_B[:, d, c]
                    if d:
                        src, dst = src[:, ::-1], dst[:, ::-1]
                    ins = nc.vector.tensor_tensor_scan(dst, ones[:, :], src, 0.0, ALU.mult, ALU.add)
            link(ins)

            def args(n):
                l = LEVELS[n]
                if n >= 2:
                    dve.wait_ge(lv_psum, n - 1)
                f, b = (gl_B[:, d, :].rearrange("p (j c) -> p j c", c=2 * l) for d in range(2))
                ek, eq = (gl_E[:, n % 2, w, :].rearrange("p (j c) -> p j c", c=2 * l) for w in range(2))
                ev, od = slice(0, l), slice(l, 2 * l)
                nb = 1024 // (2 * l)
                rf, rb = f[:, :, l - 1:l].broadcast_to([P, nb, l]), b[:, :, l:l + 1].broadcast_to([P, nb, l])
                nc.vector.tensor_tensor(ek[:, :, ev], rf, f[:, :, ev], ALU.subtract)
                nc.vector.tensor_tensor(ek[:, :, od], rb, b[:, :, od], ALU.subtract).then_inc(e_arg, 1)
                nc.vector.tensor_tensor(eq[:, :, od], f[:, :, od], rf, ALU.subtract)
                nc.vector.tensor_tensor(eq[:, :, ev], b[:, :, ev], rb, ALU.subtract).then_inc(e_arg, 1)

            def q_side(n):
                dve.wait_ge(e_exp, 2 * n + 2)
                dve.wait_ge(gq_ready, 2)
                nc.vector.tensor_tensor(gl_E[:, n % 2, 1, :], gl_E[:, n % 2, 1, :], gl_q, ALU.mult).then_inc(qd_ready, 1)

            def merge(n):
                dve.wait_ge(lv_psum, n + 1)
                l = LEVELS[n]
                if n:
                    dve.wait_ge(lv_done, 2 * n)
                for i in range(NT):
                    prod = ps[i][:, :].rearrange("p (h t) -> p h t", h=4)
                    if l < P:
                        m = lvl_mask[:, n * P:(n + 1) * P][:, None, :].broadcast_to([P, 4, P])
                        ins = nc.vector.copy_predicated(gl_A[:, i, :, i * P:(i + 1) * P], m, prod)
                    else:
                        ins = nc.vector.tensor_copy(gl_A[:, i, :, (1 - i) * P:(2 - i) * P], prod)
                    ins.then_inc(lv_done, 1)

            args(0)
            dve.wait_ge(diag_psum, 1)
            for i in range(NT):
                nc.vector.tensor_scalar(gl_A[:, i, :, i * P:(i + 1) * P], ps[i][:, :].rearrange("p (h t) -> p h t", h=4),
                                        2.0, None, ALU.mult).then_inc(diag_ready, 1)
            q_side(0)
            args(1)
            dve.wait_ge(diag_ready, 2)
            for n in range(len(LEVELS)):
                if n + 1 < len(LEVELS):
                    q_side(n + 1)
                merge(n)
                if n + 2 < len(LEVELS):
                    args(n + 2)
            lo(dve, 8, 9)
            dve.wait_ge(gr_ready, 4)
            for i in range(NT):
                dve.wait_ge(go_psum, i + 1)
                for h in range(HEADS):
                    ins = nc.vector.bn_stats(stats[:, i * 24 + h * 6:i * 24 + h * 6 + 6], go_bank(i, h))
                link(ins)
                head_stats(i)
                dve.wait_ge(hstat_ready, NT + i + 1)
                for h in range(HEADS):
                    head_center(i, h, go_bank(i, h), gl_r)
                head_rstd(dve, 1, i)
            head_scale_vector(dve, 1)
            zT_vector(dve, 1, gl_zT)
            lo(dve, *range(10, 16))
            residual(dve, [(chunk_done, gla_mix.done(c)) for c in (11, 15)], link, 2)

        def gla_gpsimd(pool):
            pool.wait_ge(gk_ready, 2)
            for n in range(len(LEVELS)):
                pool.wait_ge(e_exp, 2 * n + 1)
                nc.gpsimd.tensor_tensor(gl_E[:, n % 2, 0, :], gl_E[:, n % 2, 0, :], gl_k, ALU.mult).then_inc(kd_ready, 1)

        def gla_sync(sp):
            mixer_sync(sp, gla_u, a["gla_w_in"][0], a["gla_w_out"][0], 2)

        ar = Arena()
        band = ar(NT * 4 * SEQ).rearrange("p (s g t) -> p s g t", s=NT, g=4)
        dT = ar(KD * SEQ).rearrange("p (k t) -> p k t", k=KD)
        scale_bc = ar(D)
        band_in, scale_in, scale_ready, d_psum, d_act, d_vec = (sem(s) for s in ("band_in", "scale_in", "scale_ready",
                                                                                 "d_psum", "d_act", "d_vec"))

        def pool_tensor(pe, gen):
            pe.wait_ge(band_in, 16)
            pe.wait_ge(x_ready, NT * gen)
            for k in range(KD):
                for s in range(NT):
                    last = nc.tensor.matmul(ps[k // 2][:, (k % 2) * SEQ:(k % 2 + 1) * SEQ], x3[:, s, k * P:(k + 1) * P],
                                            band[:, s, k // 2, :], start=(s == 0), stop=(s == NT - 1))
                if k % 2:
                    last.then_inc(d_psum, 1)
            pe.wait_ge(d_act, 2)
            pe.wait_ge(d_vec, 2)
            u = pool_u
            pe.wait_ge(slot_landed[u.slot], u.landed)
            w = ring[:, u.slot * SLOT:(u.slot + 1) * SLOT].rearrange("p (g k n) -> p g k n", g=4, k=2)
            for i in range(NT):
                for g in range(4):
                    for k in range(2):
                        last = nc.tensor.matmul(ps[4 + 2 * (g // 2) + i][:, (g % 2) * 256:(g % 2 + 1) * 256],
                                                dT[:, 2 * g + k, i * P:(i + 1) * P], w[:, g, k, :],
                                                start=(k == 0), stop=(k == 1))
            last.then_inc(unit_done, 1)

        def pool_scalar(act):
            for k in (0, 4):
                act.wait_ge(d_psum, k // 2 + 1)
                nc.scalar.activation(dT[:, k:k + 2, :], ps[k // 2][:, :].rearrange("p (k t) -> p k t", k=2),
                                     ACT.Copy).then_inc(d_act, 1)

        def pool_vector(dve, link):
            for k in (2, 6):
                dve.wait_ge(d_psum, k // 2 + 1)
                nc.vector.tensor_copy(dT[:, k:k + 2, :],
                                      ps[k // 2][:, :].rearrange("p (k t) -> p k t", k=2)).then_inc(d_vec, 1)
            dve.wait_ge(unit_done, pool_u.done_at())
            dve.wait_ge(scale_ready, 1)
            dve.wait_ge(x_ready, NT * 4)
            for i in range(NT):
                for u in range(2):
                    c = slice(u * HALF, (u + 1) * HALF)
                    ins = nc.vector.tensor_tensor(y3[:, i, c], ps[4 + 2 * u + i][:, :], scale_bc[:, c], ALU.mult)
                link(ins)
                ins = nc.vector.scalar_tensor_tensor(y3[:, i, :], x3[:, i, :], ALPHA, y3[:, i, :], ALU.mult, ALU.add)
                link(ins)

        def pool_gpsimd(pool, link, gen):
            pool.wait_ge(y_added, 32)
            pool.dma_start(band.rearrange("p s g t -> p (s g t)"), a["band"]).then_inc(band_in, 16)
            pool.dma_start(scale_bc[0:1, :], a["pool_scale_2"]).then_inc(scale_in, 16)
            skew = rel_dram[:, P - 1:P - 1 + P * (3 * P - 1)].rearrange("h (q c) -> q h c", c=3 * P - 1)
            pool.wait_ge(rel_out, 16)
            pool.dma_start(at_bias[:, :, P:3 * P], skew[:, :, 0:2 * P]).then_inc(rel_in, 16)
            pool.dma_start(at_bias[:, :, 0:P], skew[:, :, P:2 * P]).then_inc(rel_in, 16)
            pool.wait_ge(scale_in, 16)
            nc.gpsimd.partition_broadcast(scale_bc, scale_bc[0:1, :], channels=P).then_inc(scale_ready, 1)

        def pool_sync(sp):
            u = pool_u
            wait_free(sp, u)
            sp.dma_start(ring[:, u.slot * SLOT:(u.slot + 1) * SLOT].rearrange("p (g k n) -> p g k n", g=4, k=2),
                         a["pool_w_2"][0].rearrange("g (k p) n -> p g k n", p=P)).then_inc(slot_landed[u.slot], 16)

        ar = Arena()
        ar(3 * NT * D + A_HEADS * 3 * P)
        f_silu = ar(4 * SEQ).rearrange("p (b t) -> p b t", b=4)
        fsilu_ready, fprod_ready, fhi_ready, fh_ready = (sem(s) for s in ("fsilu_ready", "fprod_ready", "fhi_ready",
                                                                          "fh_ready"))

        def gate_up_chunk(us, f, n):
            return slot(us[n], KD)[:, :, f * P:(f + 1) * P]

        def down_chunk(u, f):
            return slot(u, 2)[:, f:f + 1, :]

        def ffn_tensor(pe, m, gen):
            first, body, last_u = ffn_u[m]
            for b in range(4, 8):
                nc.tensor.matmul(ps[b][:, :], cst[32:64, C_EYE:C_EYE + P], cst[32:64, C_EYE:C_EYE + HALF],
                                 start=True, stop=False)

            def gate_up(s, at, first=False):
                for f in range(2):
                    for n in range(2):
                        buf = n
                        pe.wait_ge(split_ready, at + (2 * f + n + 1))
                        for k in range(KD):
                            if first and f == n == 0 and k % 2 == 0:
                                pe.wait_ge(xlo_ready, split_before("x", gen) + k // 2 + 1)
                            for p, (wp, xp) in enumerate(PARTS):
                                last = nc.tensor.matmul(ps[2 * s + f][:, n * SEQ:(n + 1) * SEQ],
                                                        w_parts[wp][:, buf, k * P:(k + 1) * P],
                                                        (xT_hi3, xT_lo3)[xp][:, k, :],
                                                        start=(k == 0 and p == 0), stop=(k == KD - 1 and p == 2))
                                if f == 1 and k == 0 and p == 0:
                                    last.then_inc(unit_done, 1)
                        last.then_inc(chunk_done, 1)

            def down(s, at, units, base, end=False):
                for f in range(2):
                    pe.wait_ge(split_ready, at + (f + 1))
                    pe.wait_ge(fh_ready, base + (f + 1))
                    for i in range(NT):
                        for c in range(2):
                            for p, (wp, hp) in enumerate(PARTS):
                                last = nc.tensor.matmul(ps[4 + 2 * c + i][:, :], h_parts[hp][:, 2 * s + f, i * P:(i + 1) * P],
                                                        w_parts[wp][:, f, c * HALF:(c + 1) * HALF],
                                                        start=False, stop=(end and f == 1 and p == 2))
                                if f == 1 and i == 0 and c == 0 and p == 0:
                                    last.then_inc(unit_done, units)
                    last.then_inc(chunk_done, 1)

            c0 = chunk0[f"ffn{m}"]
            gate_up(0, c0, first=True)
            with pe.Fori(0, 5) as g:
                for s in range(2):
                    at = g * 12 + (c0 + 4 + 6 * s)
                    gate_up(1 - s, at)
                    down(s, at + 4, 2, g * 4 + (m * NF + 2 * s))
            down(0, c0 + FFN_CHUNKS - 2, 1, m * NF + 20, end=True)

        def ffn_scalar(act, m):
            first, body, last_u = ffn_u[m]
            c0 = chunk0[f"ffn{m}"]

            def gate_up(us, g, at, first=False):
                for f in range(2):
                    for n in range(2):
                        split_hi(act, us[n], g, gate_up_chunk(us, f, n), n, at + (2 * f + n), first and f == 0)

            def silu(s, f, at):
                b = 2 * s + f
                act.wait_ge(chunk_done, at + (2 * f + 2))
                nc.scalar.activation(f_silu[:, b, :], ps[b][:, 0:SEQ], ACT.Silu).then_inc(fsilu_ready, 1)

            gate_up(first, 0, c0, c0 == 0)
            for f in range(2):
                silu(0, f, c0)
            with act.Fori(0, 5) as g:
                for s in range(2):
                    at = g * 12 + (c0 + 4 + 6 * s)
                    gate_up(body[3 * s:3 * s + 2], g, at)
                    silu(1 - s, 0, at)
                    for f in range(2):
                        split_hi(act, body[3 * s + 2], g, down_chunk(body[3 * s + 2], f), f, at + (4 + f))
                    silu(1 - s, 1, at)
            for f in range(2):
                split_hi(act, last_u, 0, down_chunk(last_u, f), f, c0 + FFN_CHUNKS - 2 + f)

        def ffn_vector(dve, link, m, gen):
            first, body, last_u = ffn_u[m]
            c0 = chunk0[f"ffn{m}"]

            def gate_up(us, at):
                for f in range(2):
                    for n in range(2):
                        split_lo(dve, gate_up_chunk(us, f, n), n, at + (2 * f + n))

            def hidden(s, f, blocks):
                b = 2 * s + f
                dve.wait_ge(fsilu_ready, blocks + 1)
                nc.vector.tensor_tensor(f_silu[:, b, :], f_silu[:, b, :], ps[b][:, SEQ:2 * SEQ], ALU.mult).then_inc(fprod_ready, 1)
                dve.wait_ge(fprod_ready, blocks + 1)
                nc.vector.tensor_copy(h_parts[0][:, b, :], f_silu[:, b, :]).then_inc(fhi_ready, 1)
                dve.wait_ge(fhi_ready, blocks + 1)
                nc.vector.tensor_tensor(h_parts[1][:, b, :], f_silu[:, b, :], h_parts[0][:, b, :].bitcast(F32),
                                        ALU.subtract).then_inc(fh_ready, 1)

            gate_up(first, c0)
            for f in range(2):
                hidden(0, f, m * NF + f)
            with dve.Fori(0, 5) as g:
                for s in range(2):
                    at, blocks = g * 12 + (c0 + 4 + 6 * s), g * 4 + (m * NF + 2 * s + 2)
                    gate_up(body[3 * s:3 * s + 2], at)
                    hidden(1 - s, 0, blocks)
                    for f in range(2):
                        split_lo(dve, down_chunk(body[3 * s + 2], f), f, at + (4 + f))
                    hidden(1 - s, 1, blocks + 1)
            for f in range(2):
                split_lo(dve, down_chunk(last_u, f), f, c0 + FFN_CHUNKS - 2 + f)
            done = chunk_done, c0 + FFN_CHUNKS
            residual(dve, (done, done), link, gen)

        def ffn_sync(sp, m):
            first, body, last_u = ffn_u[m]
            wg, wu = (a[n][m].rearrange("(k p) f -> p k f", p=P) for n in ("w_gate_2", "w_up_2"))
            wd = a["w_down_2"][m].rearrange("(f p) d -> p f d", p=P)

            def load(u, g, src):
                sp.wait_ge(unit_done, u.free_at(g))
                sp.dma_start(slot(u, src.shape[1]), src).then_inc(slot_landed[u.slot], 16)

            for u, w in zip(first, (wg, wu)):
                load(u, 0, w[:, :, 0:SEQ])
            with sp.Fori(0, 5) as g:
                for s in range(2):
                    for u, w in zip(body[3 * s:3 * s + 2], (wg, wu)):
                        load(u, g, w[:, :, bass.ds(g * 512 + (1 + s) * 256, 256)])
                    load(body[3 * s + 2], g, wd[:, bass.ds(g * 4 + 2 * s, 2), :])
            load(last_u, 0, wd[:, NF - 2:NF, :])

        ar = Arena()
        at_q = ar(A_HEADS * SEQ).rearrange("p (h t) -> p h t", h=A_HEADS)
        at_k = ar(A_HEADS * SEQ).rearrange("p (h t) -> p h t", h=A_HEADS)
        at_zT = at_q
        at_v = ar(NT * D).rearrange("p (i d) -> p i d", i=NT)
        at_bias = ar(A_HEADS * 3 * P).rearrange("p (h c) -> p h c", h=A_HEADS)
        ar(4 * SEQ)
        at_e = ar(2 * 2 * 384).rearrange("p (b c n) -> p b c n", b=2, c=2)
        at_a = ar(2 * 384).rearrange("p (b n) -> p b n", b=2)
        at_aT = ar(2 * 384).rearrange("p (b n) -> p b n", b=2)
        KEYS = (slice(0, P), slice(P, 3 * P))
        at_max = small[:, 64:72].rearrange("p (b c i) -> p b c i", b=2, c=2)
        at_sum = small[:, 72:80].rearrange("p (b c i) -> p b c i", b=2, c=2)
        at_rec = small[:, 80:88].rearrange("p (b c i) -> p b c i", b=2, c=2)
        at_ss = small[:, 96:112]
        o_std = small[:, 112:128]
        aq_ready, ak_ready, av_act, av_vec = (sem(s) for s in ("aq_ready", "ak_ready", "av_act", "av_vec"))
        as_psum, amax_ready, aexp_ready, arec_ready, alam_ready, aw_ready, aT_psum, aT_ready, ao_psum, ao_vec, ao_act = (
            sem(s) for s in ("as_psum", "amax_ready", "aexp_ready", "arec_ready", "alam_ready", "aw_ready", "aT_psum",
                             "aT_ready", "ao_psum", "ao_vec", "ao_act"))
        ostd_ready = sem("ostd_ready")

        att_mix = Mixer(att_u, 4, chunk0["att"])

        def att_tensor(pe, gen):
            for c in range(16):
                att_mix.feature_chunk(pe, c, c // 2, None if c else ("x", gen))

            def scores(h):
                if h >= 2:
                    pe.wait_ge(amax_ready, h - 1)
                for i in range(NT):
                    for c in range(2):
                        r = slice(HD * c, HD * (c + 1))
                        last = nc.tensor.matmul(ps[4 + 2 * (h % 2) + c][:, KEYS[i]], at_q[r, h, i * P:(i + 1) * P],
                                                at_k[r, h, 0:(i + 1) * P], start=True, stop=True)
                last.then_inc(as_psum, 1)

            def transpose_weights(h):
                pe.wait_ge(aw_ready, h + 1)
                for b in range(3):
                    last = nc.tensor.transpose(ps[h % 2][:, b * P:(b + 1) * P], at_a[:, h % 2, b * P:(b + 1) * P], ident)
                last.then_inc(aT_psum, 1)

            def values(h):
                pe.wait_ge(aT_ready, h + 1)
                if h >= 2:
                    pe.wait_ge(ao_vec, h - 1)
                for i, blocks in enumerate((((0, 0),), ((0, 1), (1, 2)))):
                    for n, (s, b) in enumerate(blocks):
                        last = nc.tensor.matmul(ps[2 + h % 2][:, i * P:(i + 1) * P], at_aT[:, h % 2, b * P:(b + 1) * P],
                                                at_v[:, s, h * V_DIM:(h + 1) * V_DIM], start=(n == 0),
                                                stop=(n == len(blocks) - 1))
                last.then_inc(ao_psum, 1)

            pe.wait_ge(aq_ready, 4)
            att_mix.token_block(pe, 4, (0, 1))
            pe.wait_ge(ak_ready, 4)
            scores(0)
            scores(1)
            att_mix.token_block(pe, 5, (2, 3))
            pe.wait_ge(av_act, 2)
            pe.wait_ge(av_vec, 2)
            for h in range(A_HEADS):
                if h + 2 < A_HEADS:
                    scores(h + 2)
                if h:
                    values(h - 1)
                transpose_weights(h)
            values(A_HEADS - 1)
            transpose_z(pe, 2)
            for u in range(2):
                att_mix.token_block(pe, 6 + u, (4 + 2 * u, 5 + 2 * u), None if u else ("z", 2))

        def att_scalar(act, gen):
            att_mix.hi(act, 0, 1)
            for b in range(4):
                att_mix.hi(act, 2 * b + 2, 2 * b + 3)
                act.wait_ge(chunk_done, att_mix.done(2 * b + 1))
                nc.scalar.activation(at_q[:, 2 * b:2 * b + 2, :],
                                     ps[b][:, :].rearrange("p (h t) -> p h t", h=2), ACT.Copy).then_inc(aq_ready, 1)
            att_mix.hi(act, *range(10, 22))

            def v_half(m):
                act.wait_ge(chunk_done, att_mix.done(19 + 4 * m))
                nc.scalar.activation(at_v[:, 0, m * HALF:(m + 1) * HALF], ps[2 * m][:, :], ACT.Copy).then_inc(av_act, 1)

            def squares(h):
                act.wait_ge(ao_vec, h + 1)
                if h:
                    act.wait_ge(ao_act, h)
                for i in range(NT):
                    ins = nc.scalar.activation(small_sq[:, i, 0:P], y3[:, i, h * V_DIM:(h + 1) * V_DIM], ACT.Square,
                                               accum_out=at_ss[:, i * 8 + h:i * 8 + h + 1])
                ins.then_inc(ao_act, 1)

            def exps(h):
                act.wait_ge(amax_ready, h + 1)
                b = h % 2
                for c in range(2):
                    for i in range(NT):
                        ins = nc.scalar.activation(at_e[:, b, c, KEYS[i]], at_e[:, b, c, KEYS[i]], ACT.Exp,
                                                   bias=at_max[:, b, c, i:i + 1], accum_out=at_sum[:, b, c, i:i + 1])
                ins.then_inc(aexp_ready, 1)

            v_half(0)
            att_mix.hi(act, 22)
            exps(0)
            att_mix.hi(act, 23)
            exps(1)
            v_half(1)
            att_mix.hi(act, 24, 25)
            for h in range(A_HEADS):
                act.wait_ge(aT_psum, h + 1)
                nc.scalar.activation(at_aT[:, h % 2, :], ps[h % 2][:, 0:384], ACT.Copy).then_inc(aT_ready, 1)
                if h + 2 < A_HEADS:
                    exps(h + 2)
                if h:
                    squares(h - 1)
            squares(A_HEADS - 1)
            act.wait_ge(ao_act, A_HEADS)
            nc.scalar.activation(o_std, at_ss, ACT.Sqrt, bias=eps, scale=1.0 / V_DIM).then_inc(ostd_ready, 1)
            zT_scalar(act, 2, at_zT, lambda k: sub_g)
            att_mix.hi(act, *range(26, 32))

        def att_vector(dve, link, gen):
            att_mix.lo(dve, *range(10))
            for b in range(4):
                att_mix.lo(dve, 2 * b + 10, 2 * b + 11)
                dve.wait_ge(chunk_done, att_mix.done(2 * b + 9))
                nc.vector.tensor_copy(at_k[:, 2 * b:2 * b + 2, :],
                                      ps[4 + b][:, :].rearrange("p (h t) -> p h t", h=2)).then_inc(ak_ready, 1)
            att_mix.lo(dve, *range(18, 22))
            dve.wait_ge(rel_in, 32)

            def v_half(m):
                dve.wait_ge(chunk_done, att_mix.done(19 + 4 * m))
                nc.vector.tensor_copy(at_v[:, 1, m * HALF:(m + 1) * HALF], ps[2 * m + 1][:, :]).then_inc(av_vec, 1)

            def logits(h):
                if h >= 2:
                    dve.wait_ge(aw_ready, h - 1)
                dve.wait_ge(as_psum, h + 1)
                b = h % 2
                for c in range(2):
                    ins = nc.vector.scalar_tensor_tensor(at_e[:, b, c, :], ps[4 + 2 * b + c][:, 0:384], HD ** -0.5,
                                                         at_bias[:, h, :], ALU.mult, ALU.add)
                link(ins)
                for i in range(NT):
                    ins = nc.vector.tensor_reduce(at_max[:, b, :, i], at_e[:, b, :, KEYS[i]], AX.X, ALU.max, negate=True)
                ins.then_inc(amax_ready, 1)

            def combine(h):
                dve.wait_ge(aexp_ready, h + 1)
                b = h % 2
                link(nc.vector.reciprocal(at_rec[:, b], at_sum[:, b]))
                link(nc.vector.tensor_scalar(at_rec[:, b, 1, :], at_rec[:, b, 1, :], neglam, None, ALU.mult))
                for i in range(NT):
                    ins = nc.vector.tensor_scalar(at_e[:, b, 1, KEYS[i]], at_e[:, b, 1, KEYS[i]], at_rec[:, b, 1, i:i + 1],
                                                  None, ALU.mult)
                link(ins)
                for i in range(NT):
                    ins = nc.vector.scalar_tensor_tensor(at_a[:, b, KEYS[i]], at_e[:, b, 0, KEYS[i]], at_rec[:, b, 0, i:i + 1],
                                                         at_e[:, b, 1, KEYS[i]], ALU.mult, ALU.add)
                ins.then_inc(aw_ready, 1)

            def outputs(h):
                dve.wait_ge(ao_psum, h + 1)
                nc.vector.tensor_copy(y3[:, :, h * V_DIM:(h + 1) * V_DIM],
                                      ps[2 + h % 2][:, 0:2 * P].rearrange("p (i d) -> p i d", i=NT)).then_inc(ao_vec, 1)

            dve.wait_ge(x_ready, NT * gen)
            v_half(0)
            logits(0)
            att_mix.lo(dve, 22)
            logits(1)
            att_mix.lo(dve, 23)
            combine(0)
            v_half(1)
            att_mix.lo(dve, 24, 25)
            for h in range(A_HEADS):
                if h:
                    combine(h)
                if h + 2 < A_HEADS:
                    logits(h + 2)
                if h:
                    outputs(h - 1)
            outputs(A_HEADS - 1)
            dve.wait_ge(ostd_ready, 1)
            link(nc.vector.reciprocal(o_std, o_std))
            dve.wait_ge(ao_vec, A_HEADS)
            for i in range(NT):
                v = y3[:, i, :].rearrange("p (h d) -> p h d", h=A_HEADS)
                nc.vector.tensor_tensor(v, v, o_std[:, 8 * i:8 * i + 8].unsqueeze(2).broadcast_to([P, A_HEADS, V_DIM]),
                                        ALU.mult).then_inc(z_ready, 1)
            zT_vector(dve, 2, at_zT)
            att_mix.lo(dve, *range(26, 32))
            residual(dve, [(chunk_done, att_mix.done(c)) for c in (27, 31)], link, gen)

        def att_sync(sp):
            mixer_sync(sp, att_u, a["w_qkv_2"][0], a["w_o_2"][0], 4)

        small_sq = f_silu

        MISC = 16 * 7
        PAR = 16 * 11
        n_w = 2 * QK + 2 * D

        def setup_sync(sp):
            sp.dma_start(ident, a["consts"][:, C_ID:C_ID + P]).then_inc(ident_in, 16)
            for i in range(NT):
                sp.dma_start(x3[:, i, :], a["x"][0, i * P:(i + 1) * P, :]).then_inc(x_in, 16)
            sp.dma_start(gate_w[:, :].rearrange("p (k n) -> p k n", k=KD),
                         a["mlstm_w_in"][0][:, n_w:n_w + 16].rearrange("(k p) n -> p k n", p=P)).then_inc(gate_in, 16)
            sp.dma_start(gate_b[0:4, :], a["mlstm_gate_b"].rearrange("o d t h -> h (o d t)"),
                         allow_slow_non_contiguous=True).then_inc(gate_in, 16)

        def setup_scalar(act):
            act.dma_start(cst[:, C_EYE:], a["consts"][:, C_EYE:]).then_inc(const_in, 16)

        def setup_gpsimd(pool):
            at = 0
            for name in ("ln_g", "ln_b"):
                pool.dma_start(ln_rows[at:at + 32, :], a[name].rearrange("l s (k c) -> (l s k) c", c=P)).then_inc(par_in, 16)
                at += 32
            for name in ("ln_mix_g_2", "ln_mix_b_2", "ln_ffn_g_2", "ln_ffn_b_2"):
                pool.dma_start(ln_rows[at:at + 16, :], a[name].rearrange("l (k c) -> (l k) c", c=P)).then_inc(par_in, 16)
                at += 16
            for n, name in enumerate(("mlstm_norm_g", "gla_norm_g", "pool_scale_2")):
                pool.dma_start(mix_rows[8 * n:8 * n + 8, :], a[name].rearrange("o (k c) -> (o k) c", c=P)).then_inc(par_in, 16)
            pool.dma_start(mix_rows[24:25, :], a["subln_g_2"]).then_inc(par_in, 16)
            pool.dma_start(mix_rows[25:33, :], a["gla_gate_b"].rearrange("o g (h c) -> (o g h) c", c=P)).then_inc(par_in, 16)
            pool.dma_start(rel_t[0:BUCKETS, :], a["rel_table_2"]).then_inc(misc_in, 16)
            pool.dma_start(lam_p[:, :], a["lam_p_2"].rearrange("o r c -> o (r c)").broadcast_to([P, 4 * HD])).then_inc(misc_in, 16)
            pool.dma_start(glr_w[:, :].rearrange("p (k n) -> p k n", k=KD),
                          a["gla_w_in"][0][:, n_w:n_w + 32].rearrange("(k p) n -> p k n", p=P)).then_inc(misc_in, 16)
            for l in range(2):
                pool.dma_start(rout_w[:, l * KD * NE:(l + 1) * KD * NE].rearrange("p (k n) -> p k n", k=KD),
                              a["moe_router"][l].rearrange("(k p) n -> p k n", p=P)).then_inc(misc_in, 16)
            for d in range(2):
                pool.dma_start(gk_w[0:RANK, d * QK:(d + 1) * QK], a["gla_gate_w"][0, d]).then_inc(misc_in, 16)

        def setup_vector(dve):
            nc.vector.memset(ones[:, :], 1.0)
            nc.vector.memset(rel_t[BUCKETS:BUCKETS + 1, :], MASKED).then_inc(const_ready, 1)
            dve.wait_ge(const_in, 16)
            for n in range(7):
                ins = nc.vector.tensor_scalar(lvl_mask[:, n * P:(n + 1) * P], cst[:, C_XOR:C_XOR + P], float(LEVELS[n]), None,
                                              ALU.is_ge)
            ins.then_inc(const_ready, 1)
            dve.wait_ge(const_ready, 2)

        block = ctx.enter_context(nc.Block())

        @block.sync
        def _(sp):
            setup_sync(sp)
            parts = [lambda: ml_sync(sp), lambda: moe_sync(sp, 0), lambda: gla_sync(sp), lambda: moe_sync(sp, 1),
                     lambda: pool_sync(sp), lambda: ffn_sync(sp, 0), lambda: att_sync(sp), lambda: ffn_sync(sp, 1)]
            for n in range(upto):
                parts[n]()
            sp.wait_ge(x_ready, NT * upto)
            sp.dma_start(out.rearrange("o (i p) d -> p (o i) d", p=P), x3).then_inc(x_out, 16)
            sp.wait_ge(x_out, 16)

        @block.tensor
        def _(pe):
            transpose_x(pe, 0)
            parts = [lambda: ml_tensor(pe), lambda: moe_tensor(pe, 0, 1), lambda: gla_tensor(pe, 2),
                     lambda: moe_tensor(pe, 1, 3), lambda: pool_tensor(pe, 4), lambda: ffn_tensor(pe, 0, 5),
                     lambda: att_tensor(pe, 6), lambda: ffn_tensor(pe, 1, 7)]
            for n in range(upto):
                parts[n]()
                if n + 1 < upto and T_INDEX[n + 1] is not None:
                    transpose_x(pe, n + 1)

        @block.scalar
        def _(act):
            setup_scalar(act)
            xT_scalar(act, 0)
            parts = [lambda: ml_scalar(act), lambda: moe_scalar(act, 0), lambda: gla_scalar(act),
                     lambda: moe_scalar(act, 1), lambda: pool_scalar(act), lambda: ffn_scalar(act, 0),
                     lambda: att_scalar(act, 6), lambda: ffn_scalar(act, 1)]
            for n in range(upto):
                parts[n]()
                ln_scalar(act, n)
                if n + 1 < upto and T_INDEX[n + 1] is not None:
                    xT_scalar(act, n + 1)

        @block.vector
        def _(dve):
            link = chain(dve, vec_chain)
            xT_vector(dve, 0)
            setup_vector(dve)
            parts = [lambda: ml_vector(dve, link), lambda: moe_vector(dve, link, 0), lambda: gla_vector(dve, link),
                     lambda: moe_vector(dve, link, 1), lambda: pool_vector(dve, link), lambda: ffn_vector(dve, link, 0, 5),
                     lambda: att_vector(dve, link, 6), lambda: ffn_vector(dve, link, 1, 7)]
            for n in range(upto):
                parts[n]()
                ln_vector(dve, link, n, ((0, 0), (1, 0)) if n in (0, 2, 6) else ())
                if n + 1 < upto and T_INDEX[n + 1] is not None:
                    xT_vector(dve, n + 1)

        @block.gpsimd
        def _(pool):
            link = chain(pool, pool_chain)
            setup_gpsimd(pool)
            parts = [lambda: ml_gpsimd(pool), lambda: moe_gpsimd(pool, 0, 1), lambda: gla_gpsimd(pool),
                     lambda: moe_gpsimd(pool, 1, 3), lambda: pool_gpsimd(pool, link, 4), None, None, None]
            for n in range(upto):
                if parts[n]:
                    parts[n]()
                ln_gpsimd(pool, link, n, *ln_dram_rows(n))


_INS = ["x", "mlstm_w_in", "mlstm_gate_b", "mlstm_norm_g", "mlstm_w_out", "gla_w_in", "gla_gate_w", "gla_gate_b",
        "gla_norm_g", "gla_w_out", "moe_router", "moe_w_gate", "moe_w_up", "moe_w_down", "ln_g", "ln_b", "pool_w_2",
        "pool_scale_2", "w_qkv_2", "w_o_2", "lam_p_2", "subln_g_2", "rel_table_2", "w_gate_2", "w_up_2", "w_down_2",
        "ln_mix_g_2", "ln_mix_b_2", "ln_ffn_g_2", "ln_ffn_b_2"]


def kernel(**inputs):
    import concourse.bacc as bacc
    from concourse.bass_utils import run_bass_kernel_spmd

    nc = bacc.Bacc("TRN2", target_bir_lowering=False, num_devices=1)
    arrays = {f"in_{n}": np.ascontiguousarray(inputs[n]) for n in _INS}
    arrays["in_consts"], arrays["in_band"] = shape_constants()
    aps = {n[3:]: nc.dram_tensor(n, v.shape, mybir.dt.from_np(v.dtype), kind="ExternalInput").ap()
           for n, v in arrays.items()}
    out = nc.dram_tensor("out_x", (1, SEQ, D), F32, kind="ExternalOutput").ap()
    program(nc, aps, out)
    r = run_bass_kernel_spmd(nc, [arrays], core_ids=[0])
    return r.results[0]["out_x"]
```

```python
import math
from contextlib import ExitStack

import numpy as np

import concourse.bass as bass
import concourse.mybir as mybir
from concourse.alu_op_type import AluOpType as ALU

ACT = mybir.ActivationFunctionType
AX = mybir.AxisListType
F32 = mybir.dt.float32
F32R = mybir.dt.float32r
U32 = mybir.dt.uint32
U8 = mybir.dt.uint8

P = 128
SEQ, D = 256, 1024
NT = SEQ // P
KD = D // P
DEPTH = 2
ALPHA = (2 * DEPTH) ** 0.25
EPS = 1e-5
HALF = 512

HEADS = 4
DK, DV = 128, 256
QK = HEADS * DK
RANK, TAU = 16, 16.0

NE, FF, CAP = 16, 1024, 32
GROUP = 4
NGROUP = NE // GROUP
SLOTS_E = GROUP * CAP

WINDOWS = (2, 4, 8, 16)
A_HEADS, HD = 8, 64
V_DIM = 2 * HD
BUCKETS, MAX_EXACT, MAX_DIST = 32, 16, 128
D_FF = 2816
NF = D_FF // P
LAMBDA_INIT = 0.8 - 0.6 * math.exp(-0.3)
MASKED = -1e30

RING = 8
MOE_RING = 16
SLOT = 2048
CHUNK = 1024
LEVELS = (1, 2, 4, 8, 16, 32, 64, 128)

C_ID, C_EYE, C_SEL, C_XOR, C_REL, C_TOK, C_EPS = 0, 128, 640, 1152, 1280, 1664, 1666
C_W = 1668


def shape_constants():
    c = np.zeros((P, C_W), np.float32)
    c[:, C_ID:C_ID + P] = np.eye(P)
    for e in range(NE):
        c[e, C_EYE + e * CAP:C_EYE + (e + 1) * CAP] = 1.0
    for h in range(HEADS):
        c[h, C_SEL + h * P:C_SEL + (h + 1) * P] = 1.0
    s = np.arange(P)
    c[:, C_XOR:C_XOR + P] = s[:, None] ^ s[None, :]
    for m in range(3 * P):
        rel = 255 - m
        if rel < 0:
            b = BUCKETS
        elif rel < MAX_EXACT:
            b = rel
        else:
            b = MAX_EXACT + int(math.log(rel / MAX_EXACT) / math.log(MAX_DIST / MAX_EXACT) * (BUCKETS - MAX_EXACT))
            b = min(b, BUCKETS - 1)
        c[b, C_REL + m] = 1.0
    for i in range(NT):
        c[:, C_TOK + i] = s + i * P
    c[:, C_EPS] = EPS
    band = np.zeros((SEQ, len(WINDOWS), SEQ), np.float32)
    for g, win in enumerate(WINDOWS):
        for t in range(SEQ):
            n = min(t + 1, win)
            band[t - n + 1:t + 1, g, t] = np.float32(1.0) / np.float32(n)
            band[t, g, t] -= 1.0
    band = band.reshape(NT, P, len(WINDOWS), SEQ).transpose(1, 0, 2, 3).reshape(P, -1)
    return c, np.ascontiguousarray(band)


class Unit:

    def __init__(self, n, slot, landed, lag, n_step=0, landed_step=0):
        self.n, self.slot, self.landed, self.lag = n, slot, landed, lag
        self.n_step, self.landed_step = n_step, landed_step

    def landed_at(self, i=0):
        return self.landed + i * self.landed_step if self.landed_step else self.landed

    def done_at(self, i=0):
        return i * self.n_step + self.n + 1 if self.n_step else self.n + 1

    def free_at(self, i=0):
        return i * self.n_step + self.n + 1 - self.lag if self.n_step else self.n + 1 - self.lag


class Stream:

    def __init__(self):
        self.n, self.landed = 0, [0] * MOE_RING
        self.last = [slot - RING for slot in range(MOE_RING)]

    def unit(self):
        s = min(range(RING), key=lambda slot: self.last[slot])
        self.landed[s] += 16
        u = Unit(self.n, s, self.landed[s], self.n - self.last[s])
        self.last[s] = self.n
        self.n += 1
        return u

    def units(self, count):
        return [self.unit() for _ in range(count)]

    def loop(self, count, used, ring=RING):
        assert len(used) % ring == 0
        self.n += ring - RING
        order = sorted(range(RING), key=lambda slot: self.last[slot]) + list(range(RING, ring))
        per, start, body = [0] * MOE_RING, list(self.landed), []
        for b, use in enumerate(used):
            s = order[b % ring]
            if b < ring and s < RING:
                assert self.last[s] <= self.n + b - ring
            if use:
                per[s] += 16
                body.append((self.n + b, s, start[s] + per[s]))
        self.n += count * len(used)
        self.landed = [a + count * p for a, p in zip(start, per)]
        for b in range(ring):
            self.last[order[b]] = self.n - ring + b
        return [Unit(n, s, at, ring, len(used), per[s]) for n, s, at in body]


def program(nc, a, out, upto=8):
    ctx = ExitStack()
    with ctx:
        def sb(name, cols, dt=F32):
            return ctx.enter_context(nc.sbuf_tensor(name, [P, cols], dt))

        def sem(name):
            return ctx.enter_context(nc.semaphore(name))

        ring = sb("ring", RING * SLOT)
        cst = sb("cst", C_W)
        lvl_mask = sb("lvl_mask", 7 * P, U8)
        ln_rows, ln_cols = sb("ln_rows", P), sb("ln_cols", P)
        mix_rows, mix_cols = sb("mix_rows", P), sb("mix_cols", 33)
        x_tok, xT, y, gb = sb("x_tok", NT * D), sb("xT", KD * SEQ), sb("y", NT * D), sb("gb", 2 * D)
        gate_w = sb("gate_w", KD * 16)
        glr_w = sb("glr_w", KD * 32)
        rout_w = sb("rout_w", 2 * KD * NE)
        gk_w = sb("gk_w", 2 * QK)
        gate_b = sb("gate_b", 4)
        lam_p = sb("lam_p", 4 * HD)
        rel_t = sb("rel_t", A_HEADS)
        ones = sb("ones", SEQ)
        with nc.sbuf_tensor("xT_hi", [P, KD * SEQ], F32R) as xT_hi, nc.sbuf_tensor("xT_lo", [P, KD * SEQ], F32R) as xT_lo, \
                nc.sbuf_tensor("w_hi", [P, 2 * CHUNK], F32R) as w_hi, nc.sbuf_tensor("w_lo", [P, 2 * CHUNK], F32R) as w_lo:
            pass
        moe_slots = sb("moe_slots", 4 * SLOT)
        h_hi, h_lo = sb("h_hi", 4 * SEQ, F32R), sb("h_lo", 4 * SEQ, F32R)
        stats = sb("stats", 64)
        mv = sb("mv", 16)
        std, rstd, nmr = sb("std", 8), sb("rstd", 8), sb("nmr", 8)
        small = sb("small", 128)
        arena_w = 13312
        arena = sb("arena", arena_w)

        class Arena:
            def __init__(self):
                self.at = 0

            def __call__(self, cols):
                self.at += cols
                assert self.at <= arena_w, self.at
                return arena[:, self.at - cols:self.at]

        ident = cst[:, C_ID:C_ID + P]
        eye16 = cst[0:NE, C_EYE:C_EYE + NE * CAP]
        eps = cst[:, C_EPS:C_EPS + 1]
        x3, y3 = (t[:, :].rearrange("p (i d) -> p i d", i=NT) for t in (x_tok, y))
        xT3, xT_hi3, xT_lo3 = (t[:, :].rearrange("p (k t) -> p k t", k=KD) for t in (xT, xT_hi, xT_lo))
        w_parts = [t[:, :].rearrange("p (b n) -> p b n", b=2) for t in (w_hi, w_lo)]
        h_parts = [t[:, :].rearrange("p (b t) -> p b t", b=4) for t in (h_hi, h_lo)]
        PARTS = ((0, 0), (0, 1), (1, 0))
        ps = [ctx.enter_context(nc.psum_tensor(f"bank{b}", [P, HALF], F32)) for b in range(8)]
        rel_dram = nc.dram_tensor("rel_scratch", (A_HEADS, P * 3 * P), F32, kind="Internal").ap()

        slots = [ring[:, n * SLOT:(n + 1) * SLOT] for n in range(RING)]
        slots += [arena[:, arena_w - (n + 1) * SLOT:arena_w - n * SLOT] for n in range(3)]
        slots += [moe_slots[:, n * SLOT:(n + 1) * SLOT] for n in range(4)] + [xT[:, :]]

        def slot(u, k):
            return slots[u.slot].rearrange("p (k n) -> p k n", k=k)

        st = Stream()
        MOE_UNITS = 48
        ml_u = st.units(16)
        moe_u = [None, None]
        moe_u[0] = st.loop(NGROUP, [1] * MOE_UNITS, MOE_RING)
        gla_u = st.units(16)
        moe_u[1] = st.loop(NGROUP, [1] * MOE_UNITS, MOE_RING)
        pool_u = st.unit()

        def ffn_units():
            return st.units(2), st.loop(5, [1, 1, 1, 0] * 2), st.unit()

        ffn_u = [ffn_units(), None]
        att_u = st.units(16)
        ffn_u[1] = ffn_units()

        slot_landed = [sem(f"slot{s}_landed") for s in range(MOE_RING)]
        unit_done = sem("unit_done")
        hi_ready, split_ready, chunk_done = sem("hi_ready"), sem("split_ready"), sem("chunk_done")
        xhi_vec, xlo_ready = sem("xhi_vec"), sem("xlo_ready")
        x_in, ident_in, const_in = [sem(f"x{i}_in") for i in range(NT)], sem("ident_in"), sem("const_in")
        gate_in, par_in, misc_in = sem("gate_in"), sem("par_in"), sem("misc_in")
        vec_chain, pool_chain = sem("vec_chain"), sem("pool_chain")
        const_ready = sem("const_ready")
        rel_out, rel_in = sem("rel_out"), sem("rel_in")
        var_ready, std_ready, rstd_ready = sem("var_ready"), sem("std_ready"), sem("rstd_ready")
        xhat_act, xhat_vec = sem("xhat_act"), sem("xhat_vec")
        xT_psum, xT_act, xT_vec = sem("xT_psum"), sem("xT_act"), sem("xT_vec")
        tile0_done = sem("tile0_done")
        rows_in, x_ready = sem("rows_in"), sem("x_ready")
        y_free = sem("y_free")
        x_out = sem("x_out")

        def chain(eng, s):
            count = [0]

            def link(ins):
                count[0] += 1
                ins.then_inc(s, 1)
                eng.wait_ge(s, count[0])
            return link

        RESIDUALS = (0, 2, 4, 5, 6, 7)

        def ln_vector(dve, link, n, half=None, tile1=None):
            def add(i, c):
                cc = slice(c * HALF, (c + 1) * HALF)
                return nc.vector.scalar_tensor_tensor(y3[:, i, cc], x3[:, i, cc], ALPHA, ps[4 + 2 * c + i][:, :],
                                                      ALU.mult, ALU.add)

            def statistics(i, c):
                return nc.vector.bn_stats(stats[:, i * 12 + c * 6:i * 12 + c * 6 + 6], y3[:, i, c * HALF:(c + 1) * HALF])

            def inverse_std(i):
                dve.wait_ge(std_ready, NT * n + i + 1)
                link(nc.vector.reciprocal(rstd[:, i:i + 1], std[:, i:i + 1]))
                nc.vector.scalar_tensor_tensor(nmr[:, i:i + 1], mv[:, 2 * i:2 * i + 1], -1.0, rstd[:, i:i + 1],
                                               ALU.mult, ALU.mult).then_inc(rstd_ready, 1)

            if n:
                dve.wait_ge(x_ready, NT * n)
            rest = (0, 1)
            if half:
                rest = (1,)
                dve.wait_ge(*half)
                for i in range(NT):
                    ins = add(i, 0)
                link(ins)
                for i in range(NT):
                    statistics(i, 0)
            for i in range(NT):
                if tile1:
                    if i == 0:
                        dve.wait_ge(tile0_done, RESIDUALS.index(n) + 1)
                    else:
                        dve.wait_ge(*tile1)
                    for c in rest:
                        ins = add(i, c)
                    link(ins)
                if i:
                    inverse_std(0)
                if tile1:
                    for c in rest:
                        ins = statistics(i, c)
                    link(ins)
                nc.vector.bn_aggr(mv[:, 2 * i:2 * i + 2], stats[:, i * 12:i * 12 + 12]).then_inc(var_ready, 1)
            inverse_std(1)
            dve.wait_ge(rstd_ready, NT * n + NT)
            nc.vector.tensor_scalar(y3[:, 1, :], y3[:, 1, :], rstd[:, 1:2], nmr[:, 1:2],
                                    ALU.mult, ALU.add).then_inc(xhat_vec, 1)

        def ln_scalar(act, n):
            for i in range(NT):
                act.wait_ge(var_ready, NT * n + i + 1)
                nc.scalar.activation(std[:, i:i + 1], mv[:, 2 * i + 1:2 * i + 2], ACT.Sqrt,
                                     bias=eps).then_inc(std_ready, 1)
                if i == 0:
                    act.wait_ge(rstd_ready, NT * n + 1)
                    nc.scalar.activation(y3[:, 0, :], y3[:, 0, :], ACT.Identity, bias=nmr[:, 0:1],
                                         scale=rstd[:, 0:1]).then_inc(xhat_act, 1)

        def ln_gpsimd(pool, link, n, g_row, b_row):
            if n:
                pool.wait_ge(x_ready, NT * n)
            pool.dma_start(gb[0:1, 0:D], g_row).then_inc(rows_in, 16)
            pool.dma_start(gb[0:1, D:2 * D], b_row).then_inc(rows_in, 16)
            pool.wait_ge(rows_in, 32 * (n + 1))
            link(nc.gpsimd.partition_broadcast(gb[:, :], gb[0:1, :], channels=P))
            for i in range(NT):
                pool.wait_ge((xhat_act, xhat_vec)[i], n + 1)
                nc.gpsimd.tensor_tensor(x3[:, i, :], y3[:, i, :], gb[:, 0:D], ALU.mult).then_inc(y_free, 1)
                pool.wait_ge(y_free, NT * n + i + 1)
                nc.gpsimd.tensor_tensor(x3[:, i, :], x3[:, i, :], gb[:, D:2 * D], ALU.add).then_inc(x_ready, 1)

        T_INDEX = (0, 1, 2, 3, None, 4, 5, 6)
        SPLIT = (0, 2, 5, 6, 7)

        def keep_clock(bank, count):
            for n in range(count):
                nc.tensor.matmul(ps[bank][:, 0:P], ident, ident, start=True, stop=True)

        def transpose_x(pe, gen):
            src = y3 if gen else x3
            if gen > 0 and gen in SPLIT:
                keep_clock(0, 12)
            if not gen:
                pe.wait_ge(ident_in, 16)
            for i in range(NT):
                if gen:
                    pe.wait_ge((xhat_act, xhat_vec)[i], gen)
                else:
                    pe.wait_ge(x_in[i], 16)
                for k in range(KD):
                    last = nc.tensor.transpose(ps[k // 2][:, (k % 2) * SEQ + i * P:(k % 2) * SEQ + (i + 1) * P],
                                               src[:, i, k * P:(k + 1) * P], ident)
                    if i and k % 2:
                        last.then_inc(xT_psum, 1)

        def xT_scalar(act, gen):
            for k in range(KD) if gen in SPLIT else (0, 1, 4, 5):
                act.wait_ge(xT_psum, KD // 2 * T_INDEX[gen] + k // 2 + 1)
                src = ps[k // 2][:, k % 2 * SEQ:(k % 2 + 1) * SEQ]
                if gen:
                    g, b = ln_col(gen - 1)
                    nc.scalar.activation(xT3[:, k, :], src, ACT.Identity, bias=ln_cols[:, b + k:b + k + 1],
                                         scale=ln_cols[:, g + k:g + k + 1]).then_inc(xT_act, 1)
                else:
                    nc.scalar.activation(xT3[:, k, :], src, ACT.Copy).then_inc(xT_act, 1)

        def xT_vector(dve, gen):
            if gen in SPLIT:
                split_T(dve, "x", gen, xT3, xT_act, xT_acts(gen) - KD)
                return
            for k in (2, 3, 6, 7):
                dve.wait_ge(xT_psum, KD // 2 * T_INDEX[gen] + k // 2 + 1)
                src = ps[k // 2][:, k % 2 * SEQ:(k % 2 + 1) * SEQ]
                if gen:
                    g, b = ln_col(gen - 1)
                    nc.vector.tensor_scalar(xT3[:, k, :], src, ln_cols[:, g + k:g + k + 1],
                                            ln_cols[:, b + k:b + k + 1], ALU.mult, ALU.add).then_inc(xT_vec, 1)
                else:
                    nc.vector.tensor_copy(xT3[:, k, :], src).then_inc(xT_vec, 1)

        SPLIT_ORDER = [("x", 0), ("z", 0), ("x", 2), ("z", 1), ("x", 5), ("x", 6), ("z", 2), ("x", 7)]

        def split_before(kind, n):
            return 4 * SPLIT_ORDER.index((kind, n))

        def split_T(dve, kind, m, src, ready, before):
            n = split_before(kind, m)
            for b in range(4):
                c = slice(2 * b, 2 * b + 2)
                dve.wait_ge(ready, before + 2 * b + 2)
                nc.vector.tensor_copy(xT_hi3[:, c, :], src[:, c, :]).then_inc(xhi_vec, 1)
                dve.wait_ge(xhi_vec, n + b + 1)
                nc.vector.tensor_tensor(xT_lo3[:, c, :], src[:, c, :], xT_hi3[:, c, :].bitcast(F32),
                                        ALU.subtract).then_inc(xlo_ready, 1)

        def xT_acts(gen):
            return sum((KD if g in SPLIT else KD // 2) for g in range(gen + 1) if T_INDEX[g] is not None)

        def xT_vecs(gen):
            return sum(0 if g in SPLIT else KD // 2 for g in range(gen + 1) if T_INDEX[g] is not None)

        def wait_xT(eng, gen):
            eng.wait_ge(xT_act, xT_acts(gen))
            eng.wait_ge(xT_vec, xT_vecs(gen))

        def ln_col(n):
            if n < 4:
                return 8 * n, 32 + 8 * n
            layer, ffn = (n - 4) // 2, (n - 4) % 2
            return (96 if ffn else 64) + 8 * layer, (112 if ffn else 80) + 8 * layer

        def ln_dram_rows(n):
            if n < 4:
                g, b = a["ln_g"][n // 2, n % 2], a["ln_b"][n // 2, n % 2]
            else:
                kind = "ffn" if n % 2 else "mix"
                g, b = a[f"ln_{kind}_g_2"][(n - 4) // 2], a[f"ln_{kind}_b_2"][(n - 4) // 2]
            return g.rearrange("(o d) -> o d", o=1), b.rearrange("(o d) -> o d", o=1)

        def token_major(pe, us, i, bank):
            for n, u in enumerate(us):
                pe.wait_ge(slot_landed[u.slot], u.landed)
                w = slot(u, KD // 2)
                for k in range(KD // 2):
                    kk = n * KD // 2 + k
                    last = nc.tensor.matmul(ps[bank][:, :], xT3[:, kk, i * P:(i + 1) * P], w[:, k, :],
                                            start=(kk == 0), stop=(kk == KD - 1))
            if i == NT - 1:
                last.then_inc(unit_done, 2)

        def mixer_sync(sp, us, w_in, w_out, n_feature):
            n = 0
            for src, blocks in ((w_in, 6), (w_out, 2)):
                src = src.rearrange("(k p) n -> p k n", p=P)
                for b in range(blocks):
                    for half in range(2):
                        u = us[n]
                        wait_free(sp, u)
                        if n < 2 * n_feature:
                            part = src[:, :, b * HALF + half * 256:b * HALF + (half + 1) * 256]
                        else:
                            part = src[:, half * KD // 2:(half + 1) * KD // 2, b * HALF:(b + 1) * HALF]
                        sp.dma_start(slot(u, part.shape[1]), part).then_inc(slot_landed[u.slot], 16)
                        n += 1

        def wait_free(sp, u):
            if u.free_at() > 0:
                sp.wait_ge(unit_done, u.free_at())

        z_ready = sem("z_ready")
        zT_psum, zT_act = sem("zT_psum"), sem("zT_act")

        def transpose_z(pe, m):
            pe.wait_ge(z_ready, NT * (m + 1))
            for k in range(KD):
                for i in range(NT):
                    last = nc.tensor.transpose(ps[k // 2][:, (k % 2) * SEQ + i * P:(k % 2) * SEQ + (i + 1) * P],
                                               y3[:, i, k * P:(k + 1) * P], ident)
                if k % 2:
                    last.then_inc(zT_psum, 1)

        def zT_scalar(act, m, zT, col):
            for k in range(KD):
                act.wait_ge(zT_psum, KD // 2 * m + k // 2 + 1)
                nc.scalar.activation(zT[:, k, :], ps[k // 2][:, k % 2 * SEQ:(k % 2 + 1) * SEQ], ACT.Copy,
                                     scale=col(k)).then_inc(zT_act, 1)

        def zT_vector(dve, m, zT):
            split_T(dve, "z", m, zT, zT_act, KD * m)

        MIX_CHUNKS, FFN_CHUNKS = 32, 3 * NF
        chunk0, chunks = {}, 0
        for name, count in (("ml", MIX_CHUNKS), ("gla", 16), ("ffn0", FFN_CHUNKS), ("att", MIX_CHUNKS),
                            ("ffn1", FFN_CHUNKS)):
            chunk0[name], chunks = chunks, chunks + count

        def split_hi(act, u, g, raw, buf, at, first=False):
            act.wait_ge(slot_landed[u.slot], u.landed_at(g))
            if not first:
                act.wait_ge(chunk_done, at - 1)
            dst = w_parts[0][:, buf, :].rearrange("p (k n) -> p k n", k=raw.shape[1])
            nc.scalar.activation(dst, raw, ACT.Copy).then_inc(hi_ready, 1)

        def split_lo(dve, raw, buf, at):
            dve.wait_ge(hi_ready, at + 1)
            hi, lo = (w[:, buf, :].rearrange("p (k n) -> p k n", k=raw.shape[1]) for w in w_parts)
            nc.vector.tensor_tensor(lo, raw, hi.bitcast(F32), ALU.subtract).then_inc(split_ready, 1)

        class Mixer:

            def __init__(self, units, n_feature, at, frees=0):
                self.units, self.n_feature, self.at, self.frees = units, n_feature, at, frees
                self.count = 2 * len(units)

            def raw(self, c):
                u = self.units[c // 2]
                if c // 4 < self.n_feature:
                    return slot(u, KD)[:, :, c % 2 * P:(c % 2 + 1) * P]
                return slot(u, KD // 2)[:, c % 2 * 2:c % 2 * 2 + 2, :]

            def done(self, c):
                return self.at + c + 1

            def hi(self, act, *chunks):
                for c in chunks:
                    split_hi(act, self.units[c // 2], 0, self.raw(c), c % 2, self.at + c, first=self.at + c < 2)

            def lo(self, dve, *chunks):
                for c in chunks:
                    split_lo(dve, self.raw(c), c % 2, self.at + c)

            def products(self, pe, c, todo, operand):
                pe.wait_ge(split_ready, self.at + c + 1)
                for n, (dst, cols, act_at, start, stop, weights_first) in enumerate(todo):
                    if operand and (start or act_at[1] % 2 == 0):
                        pe.wait_ge(xlo_ready, split_before(*operand) + act_at[1] // 2 + 1)
                    for p, (wp, xp) in enumerate(PARTS):
                        ops = [w_parts[wp][:, c % 2, cols], (xT_hi3, xT_lo3)[xp][act_at]]
                        last = nc.tensor.matmul(dst, *(ops if weights_first else ops[::-1]),
                                                start=(start and p == 0), stop=(stop and p == 2))
                        if c % 2 and n == 0 and p == 0:
                            last.then_inc(unit_done, 1 + (self.frees if c == self.count - 1 else 0))
                        if c == self.count - 1 and n == 1 and p == 2:
                            last.then_inc(tile0_done, 1)
                last.then_inc(chunk_done, 1)

            def feature_chunk(self, pe, c, bank, operand=None):
                self.products(pe, c, [(ps[bank][:, c % 2 * SEQ:(c % 2 + 1) * SEQ], slice(k * P, (k + 1) * P),
                                       (slice(None), k), k == 0, k == KD - 1, True) for k in range(KD)], operand)

            def token_chunk(self, pe, c, banks, operand=None):
                self.products(pe, c, [(ps[banks[i]][:, :], slice(k2 * HALF, (k2 + 1) * HALF),
                                       (slice(None), c % 4 * 2 + k2, slice(i * P, (i + 1) * P)),
                                       c % 4 * 2 + k2 == 0, c % 4 * 2 + k2 == KD - 1, False)
                                      for i in range(NT) for k2 in range(2)], operand)

            def token_block(self, pe, b, banks, operand=None):
                for c in range(4 * b, 4 * b + 4):
                    self.token_chunk(pe, c, banks, operand)

        hstat_ready, hstd_ready, hrstd_ready = (sem(s) for s in ("hstat_ready", "hstd_ready", "hrstd_ready"))

        ar = Arena()
        ml_qkT = ar(2 * 4 * SEQ)
        ml_q = ml_qkT[:, 0:1024].rearrange("p (h t) -> p h t", h=4)
        ml_k = ml_qkT[:, 1024:2048].rearrange("p (h t) -> p h t", h=4)
        ml_zT = ml_qkT.rearrange("p (k t) -> p k t", k=KD)
        ml_v = ar(NT * D).rearrange("p (i d) -> p i d", i=NT)
        ml_o = ar(NT * D).rearrange("p (i d) -> p i d", i=NT)
        ml_A = ar(4 * 2 * 384).rearrange("p (h d c) -> p h d c", h=4, d=2)
        row = lambda: ar(2 * SEQ)[0:HEADS, :].rearrange("p (d t) -> p d t", d=2)
        r_i, r_f, r_e, r_l, r_B = (row() for _ in range(5))
        r_a, r_M, r_nm = r_e, r_f, r_l
        ml_t = ar(4 * DV).rearrange("p (h c) -> p h c", h=4)
        a_col = small[:, 0:16].rearrange("p (i d h) -> p i d h", i=2, d=2)
        em_col = small[:, 16:32].rearrange("p (i d h) -> p i d h", i=2, d=2)
        den_c = small[:, 32:48].rearrange("p (i h d) -> p i h d", i=2, d=2)
        gates_psum, gates_in, gate_rows, cols_psum = sem("gates_psum"), sem("gates_in"), sem("gate_rows"), sem("cols_psum")
        cols_ready, em_ready = sem("cols_ready"), sem("em_ready")
        q_ready, k_ready, sc_psum, bc_psum = sem("q_ready"), sem("k_ready"), sem("sc_psum"), sem("bc_psum")
        arg_ready, w_exp, w_masked, w_ready = sem("arg_ready"), sem("w_exp"), sem("w_masked"), sem("w_ready")
        v_ready, o_ready = sem("v_ready"), sem("o_ready")
        den_psum, num_psum, den_ready, bpart_ready, h_done = (sem(s) for s in ("den_psum", "num_psum", "den_ready",
                                                                               "bpart_ready", "h_done"))
        gate_act = sem("gate_act")
        rel_row = y[0:A_HEADS, 0:3 * P]
        neglam, lam_e, sub_g = small[:, 54:55], small[:, 56:58], small[:, 58:59]
        lam_ready, lam_exp = sem("lam_ready"), sem("lam_exp")
        AV_BANK = {(i, h): (h if i == 0 else (5, 6, 7, 0)[h]) for i in range(NT) for h in range(4)}

        ml_mix = Mixer(ml_u, 2, chunk0["ml"], MOE_RING - RING - 1)

        def ml_tensor(pe):
            wait_xT(pe, 0)
            pe.wait_ge(gate_in, 32)
            for kk in range(KD):
                for t in range(2):
                    for d in range(2):
                        g = 2 * t + d
                        last = nc.tensor.matmul(ps[4][32 * g:32 * g + 4, 0:SEQ],
                                                gate_w[:, kk * 16 + d * 8 + t * 4:kk * 16 + d * 8 + t * 4 + 4],
                                                xT3[:, kk, :], start=(kk == 0), stop=(kk == KD - 1),
                                                tile_position=(0, 32 * g))
            last.then_inc(gates_psum, 1)
            for c in range(8):
                ml_mix.feature_chunk(pe, c, c // 2, None if c else ("x", 0))
            pe.wait_ge(gate_rows, 2)
            pe.wait_ge(q_ready, 2)
            for i in range(NT):
                for d in range(2):
                    for n, r in enumerate((r_a, r_nm)):
                        c = n * 16 + i * 8 + d * 4
                        nc.tensor.transpose(ps[1][:, c:c + 4], r[:, d, i * P:(i + 1) * P], ident[0:4, 0:4])
            pe.wait_ge(par_in, PAR)
            nc.tensor.transpose(ps[1][:, P:2 * P], ln_rows[:, :], ident)
            nc.tensor.transpose(ps[1][:, 2 * P:2 * P + 33], mix_rows[0:33, :], ident[0:33, 0:33])
            pe.wait_ge(misc_in, MISC)
            pe.wait_ge(const_ready, 2)
            nc.tensor.matmul(ps[0][0:A_HEADS, 0:3 * P], rel_t[0:BUCKETS + 1, :], cst[0:BUCKETS + 1, C_REL:C_REL + 3 * P],
                             start=True, stop=True).then_inc(cols_psum, 1)
            pe.wait_ge(k_ready, 2)
            pe.wait_ge(gates_in, 4)
            for h in range(4):
                for s in range(NT):
                    last = nc.tensor.matmul(ps[4 + h][:, s * SEQ:(s + 1) * SEQ], ml_k[:, h, s * P:(s + 1) * P],
                                            ml_q[:, h, :], start=True, stop=True)
                last.then_inc(sc_psum, 1)

            def broadcast(h):
                if h >= 2:
                    pe.wait_ge(arg_ready, h - 1)
                for d in range(2):
                    last = nc.tensor.matmul(ps[2 + h % 2][:, d * SEQ:(d + 1) * SEQ],
                                            cst[0:4, C_SEL + h * P:C_SEL + (h + 1) * P], r_M[:, d, :],
                                            start=True, stop=True)
                last.then_inc(bc_psum, 1)

            broadcast(0)
            broadcast(1)
            pe.wait_ge(cols_ready, 1)
            ml_mix.token_block(pe, 2, (0, 1))
            broadcast(2)
            broadcast(3)
            pe.wait_ge(v_ready, 2)
            ml_mix.token_block(pe, 3, (0, 1))
            pe.wait_ge(arg_ready, 4)
            ml_mix.token_block(pe, 4, (2, 3))
            pe.wait_ge(v_ready, 4)
            ml_mix.token_block(pe, 5, (0, 1))
            pe.wait_ge(w_ready, 4)
            blocks = {(0, 0): [(0, 0)], (0, 1): [(0, 128), (1, 256)], (1, 0): [(0, 0), (1, 128)], (1, 1): [(1, 256)]}
            for i in range(NT):
                for h in range(4):
                    for d in range(2):
                        todo = blocks[d, i]
                        for n, (s, c) in enumerate(todo):
                            last = nc.tensor.matmul(ps[4][:, i * 8 + h * 2 + d:i * 8 + h * 2 + d + 1],
                                                    ml_A[:, h, d, c:c + P], ones[:, 0:1],
                                                    start=(n == 0), stop=(n == len(todo) - 1))
            last.then_inc(den_psum, 1)
            pe.wait_ge(o_ready, 4)
            for i in range(NT):
                for h in range(4):
                    if i == 1 and h == 3:
                        pe.wait_ge(h_done, 1)
                    for d in range(2):
                        todo = blocks[d, i]
                        for n, (s, c) in enumerate(todo):
                            last = nc.tensor.matmul(ps[AV_BANK[i, h]][:, d * DV:(d + 1) * DV],
                                                    ml_A[:, h, d, c:c + P], ml_v[:, s, h * DV:(h + 1) * DV],
                                                    start=(n == 0), stop=(n == len(todo) - 1))
                    last.then_inc(num_psum, 1)
            transpose_z(pe, 0)
            for u in range(2):
                ml_mix.token_block(pe, 6 + u, (4 + 2 * u, 5 + 2 * u), None if u else ("z", 0))

        def ml_scalar(act):
            hi = ml_mix.hi
            hi(act, *range(4))
            act.wait_ge(gate_rows, 1)
            nc.scalar.activation(r_e, r_e, ACT.Exp).then_inc(gate_act, 1)
            act.wait_ge(gate_act, 1)
            nc.scalar.activation(r_l, r_e, ACT.Ln, bias=ones[0:4, 0:1]).then_inc(gate_act, 1)
            for b in range(2):
                hi(act, 2 * b + 4)
                act.wait_ge(chunk_done, ml_mix.done(2 * b + 1))
                nc.scalar.activation(ml_qkT[:, b * HALF:(b + 1) * HALF], ps[b][:, :], ACT.Copy,
                                     scale=DK ** -0.5).then_inc(q_ready, 1)
                hi(act, 2 * b + 5)
            for b in range(2):
                act.wait_ge(chunk_done, ml_mix.done(2 * b + 5))
                nc.scalar.activation(ml_qkT[:, 1024 + b * HALF:1024 + (b + 1) * HALF], ps[2 + b][:, :],
                                     ACT.Copy).then_inc(k_ready, 1)
            hi(act, 8, 9)
            act.wait_ge(cols_ready, 1)
            nc.scalar.activation(em_col, em_col, ACT.Exp).then_inc(em_ready, 1)
            act.dma_start(rel_dram.rearrange("h (p c) -> h p c", p=P),
                          rel_row[:, None, :].broadcast_to([A_HEADS, P, 3 * P])).then_inc(rel_out, 16)

            def weights(h):
                act.wait_ge(arg_ready, h + 1)
                nc.scalar.activation(ml_A[:, h], ml_A[:, h], ACT.Exp).then_inc(w_exp, 1)

            def values(u):
                act.wait_ge(chunk_done, ml_mix.done(11 + 4 * u))
                for i in range(NT):
                    nc.scalar.activation(ml_v[:, i, u * HALF:(u + 1) * HALF], ps[i][:, :],
                                         ACT.Copy).then_inc(v_ready, 1)

            weights(0)
            hi(act, 10)
            weights(1)
            hi(act, 11, 12, 13)
            values(0)
            weights(2)
            hi(act, 14, 15)
            weights(3)
            hi(act, 16, 17)
            values(1)
            hi(act, 18, 19)
            act.wait_ge(lam_ready, 1)
            nc.scalar.activation(lam_e, lam_e, ACT.Exp).then_inc(lam_exp, 1)
            for u in range(2):
                hi(act, *range(20 + 4 * u, 22 + 4 * u), *((22, 23) if u == 0 else ()))
                act.wait_ge(chunk_done, ml_mix.done(19 + 4 * u))
                for i in range(NT):
                    nc.scalar.activation(ml_o[:, i, u * HALF:(u + 1) * HALF], ps[(2 if u == 0 else 0) + i][:, :],
                                         ACT.Sigmoid).then_inc(o_ready, 1)
            act.wait_ge(den_ready, 1)

            def backward_part(i, h):
                act.wait_ge(num_psum, 4 * i + h + 1)
                if i == 1:
                    act.wait_ge(h_done, h + 1)
                nc.scalar.activation(ml_t[:, h, :], ps[AV_BANK[i, h]][:, DV:2 * DV], ACT.Copy,
                                     scale=den_c[:, i, h, 1:2]).then_inc(bpart_ready, 1)

            for h in range(HEADS):
                backward_part(0, h)
            head_std(act, 0, 0)
            for h in range(HEADS):
                backward_part(1, h)
            for h in range(HEADS):
                head_scale(act, 0, h)
            head_std(act, 0, 1)
            zT_scalar(act, 0, ml_zT, lambda k: mix_cols[:, k:k + 1])
            hi(act, *range(26, 32))

        def head_std(act, m, i):
            act.wait_ge(hstat_ready, NT * m + i + 1)
            nc.scalar.activation(std[:, 4 * i:4 * i + 4], mv[:, 8 * i:8 * i + 8].rearrange("p (h s) -> p h s", s=2)[:, :, 1],
                                 ACT.Sqrt, bias=eps).then_inc(hstd_ready, 1)

        def head_scale(act, m, h):
            act.wait_ge(hrstd_ready, NT * m + 1)
            ins = nc.scalar.activation(y3[:, 0, h * DV:(h + 1) * DV], y3[:, 0, h * DV:(h + 1) * DV], ACT.Copy,
                                       scale=rstd[:, h:h + 1])
            if h == HEADS - 1:
                ins.then_inc(z_ready, 1)

        def head_stats(i):
            for h in range(HEADS):
                ins = nc.vector.bn_aggr(mv[:, 8 * i + 2 * h:8 * i + 2 * h + 2], stats[:, i * 24 + h * 6:i * 24 + h * 6 + 6])
            ins.then_inc(hstat_ready, 1)

        def head_center(i, h, src, gate):
            return nc.vector.scalar_tensor_tensor(y3[:, i, h * DV:(h + 1) * DV], src, mv[:, 8 * i + 2 * h:8 * i + 2 * h + 1],
                                                  gate[:, i, h * DV:(h + 1) * DV], ALU.subtract, ALU.mult)

        def head_rstd(dve, m, i):
            dve.wait_ge(hstd_ready, NT * m + i + 1)
            nc.vector.reciprocal(rstd[:, 4 * i:4 * i + 4], std[:, 4 * i:4 * i + 4]).then_inc(hrstd_ready, 1)

        def head_scale_vector(dve, m):
            dve.wait_ge(hrstd_ready, NT * m + 2)
            for h in range(HEADS):
                ins = nc.vector.tensor_scalar(y3[:, 1, h * DV:(h + 1) * DV], y3[:, 1, h * DV:(h + 1) * DV],
                                              rstd[:, 4 + h:5 + h], None, ALU.mult)
            ins.then_inc(z_ready, 1)

        def ml_vector(dve, link):
            lo = ml_mix.lo
            lo(dve, 0, 1)
            dve.wait_ge(gates_psum, 1)
            dve.wait_ge(gate_in, 32)
            for t, r in enumerate((r_i, r_f)):
                for d in range(2):
                    g = 2 * t + d
                    ins = nc.vector.tensor_scalar(r[:, d, :], ps[4][32 * g:32 * g + 4, 0:SEQ],
                                                  gate_b[0:4, 2 * d + t:2 * d + t + 1], None, ALU.add)
                    ins.then_inc(gates_in, 1)
            dve.wait_ge(gates_in, 4)
            nc.vector.scalar_tensor_tensor(r_e, r_f, -1.0, r_f, ALU.mult, ALU.min).then_inc(gate_rows, 1)
            lo(dve, 2, 3)
            dve.wait_ge(gate_act, 2)
            link(nc.vector.scalar_tensor_tensor(r_l, r_f, 0.0, r_l, ALU.min, ALU.subtract))
            order = (slice(None), slice(None, None, -1))
            for d in range(2):
                ins = nc.vector.tensor_tensor_scan(r_B[:, d, order[d]], ones[0:4, :], r_l[:, d, order[d]], 0.0,
                                                   ALU.mult, ALU.add)
            link(ins)
            link(nc.vector.tensor_tensor(r_a, r_i, r_B, ALU.subtract))
            lo(dve, 4)
            for d in range(2):
                ins = nc.vector.tensor_tensor_scan(r_M[:, d, order[d]], ones[0:4, :], r_a[:, d, order[d]], 0.0,
                                                   ALU.mult, ALU.max)
            link(ins)
            link(nc.vector.scalar_tensor_tensor(r_nm, r_B, -1.0, r_M, ALU.mult, ALU.subtract))
            nc.vector.tensor_scalar(r_M, r_M, -1.0, None, ALU.mult).then_inc(gate_rows, 1)
            lo(dve, *range(5, 10))
            dve.wait_ge(cols_psum, 1)
            nc.vector.tensor_copy(small[:, 0:32], ps[1][:, 0:32])
            nc.vector.tensor_copy(ln_cols[:, :], ps[1][:, P:2 * P])
            nc.vector.tensor_copy(mix_cols[:, :], ps[1][:, 2 * P:2 * P + 33])
            nc.vector.tensor_copy(rel_row, ps[0][0:A_HEADS, 0:3 * P]).then_inc(cols_ready, 1)
            dve.wait_ge(cols_ready, 1)

            def args(h):
                dve.wait_ge(bc_psum, h + 1)
                for d, s, t0, n, c in ((0, 0, 0, 256, 0), (0, 1, 128, 128, 256), (1, 0, 0, 128, 0), (1, 1, 0, 256, 128)):
                    ins = nc.vector.tensor_scalar(ml_A[:, h, d, c:c + n], ps[2 + h % 2][:, d * SEQ + t0:d * SEQ + t0 + n],
                                                  a_col[:, s, d, h:h + 1], 0.0, ALU.add, ALU.min)
                ins.then_inc(arg_ready, 1)

            def apply(h):
                dve.wait_ge(w_masked, 2 * h + 2)
                dve.wait_ge(sc_psum, h + 1)
                for d, s, t0, n, c in ((0, 0, 0, 256, 0), (0, 1, 128, 128, 256), (1, 0, 0, 128, 0), (1, 1, 0, 256, 128)):
                    ins = nc.vector.tensor_tensor(ml_A[:, h, d, c:c + n], ml_A[:, h, d, c:c + n],
                                                  ps[4 + h][:, s * SEQ + t0:s * SEQ + t0 + n], ALU.mult)
                ins.then_inc(w_ready, 1)

            args(0)
            args(1)
            lo(dve, *range(10, 14))
            args(2)
            apply(0)
            args(3)
            lo(dve, 14, 15)
            apply(1)
            lo(dve, 16, 17)
            apply(2)
            apply(3)
            nc.vector.tensor_scalar(sub_g, mix_cols[:, 24:25], 1.0 - LAMBDA_INIT, None, ALU.mult)
            dve.wait_ge(misc_in, MISC)
            lp = lam_p[:, :].rearrange("p (n a c) -> p n a c", n=2, a=2)
            link(nc.vector.tensor_tensor(lp[:, :, 0, :], lp[:, :, 0, :], lp[:, :, 1, :], ALU.mult))
            nc.vector.tensor_reduce(lam_e, lp[:, :, 0, :], AX.X, ALU.add).then_inc(lam_ready, 1)
            lo(dve, 18, 19)
            dve.wait_ge(lam_exp, 1)
            link(nc.vector.tensor_tensor(neglam, lam_e[:, 1:2], lam_e[:, 0:1], ALU.subtract))
            link(nc.vector.tensor_scalar(neglam, neglam, -LAMBDA_INIT, None, ALU.add))
            lo(dve, *range(20, 26))
            dve.wait_ge(den_psum, 1)
            dve.wait_ge(em_ready, 1)
            den_v = small[:, 32:48]
            link(nc.vector.tensor_copy(den_v, ps[4][:, 0:16]))
            link(nc.vector.scalar_tensor_tensor(den_v, den_v, -1.0, den_v, ALU.mult, ALU.max))
            for i in range(NT):
                ins = nc.vector.tensor_tensor(den_c[:, i], den_c[:, i], em_col[:, i].rearrange("p d h -> p h d"), ALU.max)
            link(ins)
            nc.vector.reciprocal(den_v, den_v).then_inc(den_ready, 1)
            dve.wait_ge(den_ready, 1)
            dve.wait_ge(rel_out, 16)
            dve.wait_ge(o_ready, 4)

            def head(i, h):
                dve.wait_ge(bpart_ready, 4 * i + h + 1)
                nc.vector.scalar_tensor_tensor(y3[:, i, h * DV:(h + 1) * DV], ps[AV_BANK[i, h]][:, 0:DV],
                                               den_c[:, i, h, 0:1], ml_t[:, h, :], ALU.mult, ALU.add).then_inc(h_done, 1)
                dve.wait_ge(h_done, 4 * i + h + 1)
                return nc.vector.bn_stats(stats[:, i * 24 + h * 6:i * 24 + h * 6 + 6], y3[:, i, h * DV:(h + 1) * DV])

            center = lambda i, h: head_center(i, h, y3[:, i, h * DV:(h + 1) * DV], ml_o)
            for h in range(HEADS):
                ins = head(0, h)
            link(ins)
            head_stats(0)
            dve.wait_ge(hstat_ready, 1)
            for h in range(HEADS):
                ins = head(1, h)
                if h < 2:
                    center(0, 2 * h)
                    ins = center(0, 2 * h + 1)
                if h == 1:
                    head_rstd(dve, 0, 0)
            link(ins)
            head_stats(1)
            dve.wait_ge(hstat_ready, 2)
            for h in range(HEADS):
                center(1, h)
            head_rstd(dve, 0, 1)
            head_scale_vector(dve, 0)
            zT_vector(dve, 0, ml_zT)
            lo(dve, *range(26, 32))

        def ml_gpsimd(pool):
            for h in range(4):
                pool.wait_ge(w_exp, h + 1)
                for d in range(2):
                    v = ml_A[:, h, d].rearrange("p (b t) -> p b t", t=P)[:, 0:3:2, :]
                    sign = 1 if d == 0 else -1
                    nc.gpsimd.affine_select(out=v, in_=v, compare_op=ALU.is_ge, fill=0.0, base=0,
                                            pattern=[[0, 2], [sign, P]], channel_multiplier=-sign).then_inc(w_masked, 1)

        def ml_sync(sp):
            mixer_sync(sp, ml_u, a["mlstm_w_in"][0], a["mlstm_w_out"][0], 2)

        ar = Arena()
        xin = ar(KD * SLOTS_E).rearrange("p (k c) -> p k c", k=KD)
        silu = ar(2 * HALF).rearrange("p (b n) -> p b n", b=2)
        hmid = ar(2 * HALF).rearrange("p (b n) -> p b n", b=2)
        hT = ar(2 * HALF).rearrange("p (b c) -> p b c", b=2)
        e_out = ar(D)
        idx_bc, gate_bc = ar(NE * CAP), ar(NE * CAP)
        pick = ar(NT * SLOTS_E).rearrange("p (i c) -> p i c", i=NT)
        pick_g = ar(NT * SLOTS_E).rearrange("p (i c) -> p i c", i=NT)
        pick_gT = ar(NT * P)
        aff = ar(NT * NE).rearrange("p (i e) -> p i e", i=NT)
        assert ar.at <= arena_w - 3 * SLOT
        ar = Arena()
        ar(KD * SLOTS_E)
        affT = [ar(SEQ)[0:NE, :] for _ in range(2)]
        top_v, top_f = ar(CAP)[0:NE, :], ar(CAP)[0:NE, :]
        top_i = ar(CAP).bitcast(U32)[0:NE, :]
        bd_i, bd_hi, bd_lo = h_hi[0:NE, 0:HALF], h_hi[0:NE, HALF:2 * HALF], h_lo[0:NE, 0:HALF]
        ones_r, v_hi, v_lo = h_lo[0:NE, HALF:HALF + P], h_lo[0:NE, 640:640 + CAP], h_lo[0:NE, 672:672 + CAP]
        nmax, esum, ersum = small[:, 48:50], small[:, 50:52], small[:, 52:54]
        lg_psum, lmax_ready, lexp_ready, aff_ready, affT_psum = (sem(s) for s in ("lg_psum", "lmax_ready", "lexp_ready",
                                                                                  "aff_ready", "affT_psum"))
        bdg_ready, bdg_psum = sem("bdg_ready"), sem("bdg_psum")
        bd_ready, bdc_psum, idxbc_ready, gatebc_ready = (sem(s) for s in ("bd_ready", "bdc_psum", "idxbc_ready",
                                                                         "gatebc_ready"))
        y_stats = sem("y_stats")
        y_init, pick_ready, pickg_ready, gathered = (sem(s) for s in ("y_init", "pick_ready", "pickg_ready", "gathered"))
        xin_act, xin_vec, pickT_psum, pickT_ready = (sem(s) for s in ("xin_act", "xin_vec", "pickT_psum", "pickT_ready"))
        silu_ready, h_ready, hT_psum, hT_ready = (sem(s) for s in ("silu_ready", "h_ready", "hT_psum", "hT_ready"))
        eout_act, eout_vec, scattered, y_added = (sem(s) for s in ("eout_act", "eout_vec", "scattered", "y_added"))
        B_GU, B_HT, B_DN, B_GA, B_PT = (0, 1), 2, (3, 4), (5, 6), 7
        SC_BANK = ((5, 6), (3, 4))

        def moe_tensor(pe, m, gen):
            us = moe_u[m]
            pe.wait_ge(misc_in, MISC)
            for k in range(KD):
                done, before = ((xT_act, xT_acts(gen)), (xT_vec, xT_vecs(gen)))[k // 2 % 2]
                pe.wait_ge(done, before - KD // 2 + k // 4 * 2 + k % 2 + 1)
                for i in range(NT):
                    last = nc.tensor.matmul(ps[B_PT][:, i * NE:(i + 1) * NE], xT3[:, k, i * P:(i + 1) * P],
                                            rout_w[:, (m * KD + k) * NE:(m * KD + k + 1) * NE],
                                            start=(k == i == 0), stop=(k == KD - 1 and i == NT - 1))
            last.then_inc(lg_psum, 1)
            pe.wait_ge(aff_ready, m + 1)
            for i in range(NT):
                last = nc.tensor.transpose(ps[B_GU[0]][0:NE, i * P:(i + 1) * P], aff[:, i, :], ident)
                if i == 0:
                    last.then_inc(unit_done, 1)
            last.then_inc(affT_psum, 1)
            pe.wait_ge(bd_ready, m + 1)
            nc.tensor.matmul(ps[B_GA[0]][:, :], ones_r, bd_i, start=True, stop=True).then_inc(bdc_psum, 1)
            pe.wait_ge(bdg_ready, m + 1)
            nc.tensor.matmul(ps[B_GA[1]][:, :], ones_r, bd_hi, start=True, stop=False)
            nc.tensor.matmul(ps[B_GA[1]][:, :], ones_r, bd_lo, start=False, stop=True).then_inc(bdg_psum, 1)
            pe.wait_ge(x_ready, NT * gen)
            pe.wait_ge(idxbc_ready, m + 1)
            with pe.Fori(0, NGROUP) as g:
                pe.wait_ge(pick_ready, g + (m * NGROUP + 1))
                for k in range(KD):
                    if k == 4:
                        pe.wait_ge(gatebc_ready, m + 1)
                    for i in range(NT):
                        last = nc.tensor.matmul(ps[B_GA[k // 4]][:, (k % 4) * P:(k % 4 + 1) * P],
                                                x3[:, i, k * P:(k + 1) * P], pick[:, i, :],
                                                start=(i == 0), stop=(i == NT - 1))
                    if k % 4 == 3:
                        last.then_inc(gathered, 1)
                pe.wait_ge(pickg_ready, g + (m * NGROUP + 1))
                for i in range(NT):
                    last = nc.tensor.transpose(ps[B_PT][:, i * P:(i + 1) * P], pick_g[:, i, :], ident)
                last.then_inc(pickT_psum, 1)
                pe.wait_ge(xin_act, g + (m * NGROUP + 1))

                def gate_up(j):
                    for part in range(4):
                        if j == 0 and part == 2:
                            pe.wait_ge(xin_vec, g + (m * NGROUP + 1))
                        ug, uu = us[8 * j + 2 * part], us[8 * j + 2 * part + 1]
                        pe.wait_ge(slot_landed[ug.slot], ug.landed_at(g))
                        pe.wait_ge(slot_landed[uu.slot], uu.landed_at(g))
                        for k2 in range(2):
                            k = 2 * part + k2
                            for c in range(4):
                                w = slot((ug, uu)[c // 2], 2)[:, k2, (c % 2) * HALF:(c % 2 + 1) * HALF]
                                last = nc.tensor.matmul(ps[B_GU[j % 2]][32 * c:32 * c + 32, :],
                                                        xin[:, k, j * CAP:(j + 1) * CAP], w, start=(k == 0),
                                                        stop=(k == KD - 1), tile_position=(0, 32 * c))
                        last.then_inc(unit_done, 2)

                def transpose_h(pair):
                    if pair:
                        pe.wait_ge(hT_ready, g * 2 + (m * 8 + pair))
                    pe.wait_ge(h_ready, g * 4 + (m * 16 + 2 * pair + 2))
                    for c in range(4):
                        last = nc.tensor.transpose(ps[B_HT][:, c * P:(c + 1) * P], hmid[:, pair, c * P:(c + 1) * P], ident)
                    last.then_inc(hT_psum, 1)

                gate_up(0)
                gate_up(1)
                pe.wait_ge(h_ready, g * 4 + (m * 16 + 1))
                gate_up(2)
                transpose_h(0)
                gate_up(3)
                transpose_h(1)
                pe.wait_ge(hT_ready, g * 2 + (m * 8 + 2))
                for f in range(KD):
                    ud = us[32 + 2 * f:34 + 2 * f]
                    for u in ud:
                        pe.wait_ge(slot_landed[u.slot], u.landed_at(g))
                    half, fh = f // 4, f % 4
                    for c in range(2):
                        for j in range(GROUP):
                            at = fh * P + (j % 2) * 64 + half * 32
                            last = nc.tensor.matmul(ps[B_DN[c]][32 * j:32 * j + 32, :], hT[:, j // 2, at:at + CAP],
                                                    slot(ud[j // 2], 2)[:, j % 2, c * HALF:(c + 1) * HALF],
                                                    start=(f == 0), stop=(f == KD - 1), tile_position=(0, 32 * j))
                    last.then_inc(unit_done, 2)
                pe.wait_ge(pickT_ready, g + (m * NGROUP + 1))
                pe.wait_ge(eout_act, g + (m * NGROUP + 1))
                pe.wait_ge(eout_vec, g + (m * NGROUP + 1))
                for i in range(NT):
                    for c in range(2):
                        nc.tensor.matmul(ps[SC_BANK[i][c]][:, :], pick_gT[:, i * P:(i + 1) * P],
                                         e_out[:, c * HALF:(c + 1) * HALF], start=True, stop=True).then_inc(scattered, 1)
                pe.wait_ge(y_added, g * 4 + (m * 16 + 4))

        def moe_scalar(act, m):
            act.wait_ge(lmax_ready, m + 1)
            for i in range(NT):
                ins = nc.scalar.activation(aff[:, i, :], ps[B_PT][:, i * NE:(i + 1) * NE], ACT.Exp, bias=nmax[:, i:i + 1],
                                           accum_out=esum[:, i:i + 1])
            ins.then_inc(lexp_ready, 1)
            act.wait_ge(bdc_psum, m + 1)
            nc.scalar.activation(idx_bc, ps[B_GA[0]][:, :], ACT.Copy).then_inc(idxbc_ready, 1)
            act.wait_ge(bdg_psum, m + 1)
            nc.scalar.activation(gate_bc, ps[B_GA[1]][:, :], ACT.Copy).then_inc(gatebc_ready, 1)
            us = moe_u[m]
            with act.Fori(0, NGROUP) as g:
                act.wait_ge(gathered, g * 2 + (m * NGROUP * 2 + 1))
                nc.scalar.activation(xin[:, 0:4, :], ps[B_GA[0]][:, :].rearrange("p (k c) -> p k c", k=4),
                                     ACT.Copy).then_inc(xin_act, 1)
                act.wait_ge(pickT_psum, g + (m * NGROUP + 1))
                nc.scalar.activation(pick_gT, ps[B_PT][:, 0:SEQ], ACT.Copy).then_inc(pickT_ready, 1)
                for j in range(GROUP):
                    act.wait_ge(unit_done, us[8 * j + 7].done_at(g))
                    nc.scalar.activation(silu[64:128, j % 2, :], ps[B_GU[j % 2]][0:64, :], ACT.Silu).then_inc(silu_ready, 1)
                act.wait_ge(unit_done, us[MOE_UNITS - 1].done_at(g))
                nc.scalar.activation(e_out[:, 0:HALF], ps[B_DN[0]][:, :], ACT.Copy).then_inc(eout_act, 1)

        def moe_vector(dve, link, m):
            dve.wait_ge(lg_psum, m + 1)
            nc.vector.tensor_reduce(nmax, ps[B_PT][:, 0:NT * NE].rearrange("p (i e) -> p i e", i=NT), AX.X, ALU.max,
                                    negate=True).then_inc(lmax_ready, 1)
            dve.wait_ge(lexp_ready, m + 1)
            link(nc.vector.reciprocal(ersum, esum))
            for i in range(NT):
                ins = nc.vector.tensor_scalar(aff[:, i, :], aff[:, i, :], ersum[:, i:i + 1], None, ALU.mult)
            ins.then_inc(aff_ready, 1)
            dve.wait_ge(affT_psum, m + 1)
            link(nc.vector.tensor_copy(affT[0], ps[B_GU[0]][0:NE, 0:SEQ]))
            for r in range(CAP // 8):
                c, src, dst = slice(8 * r, 8 * r + 8), affT[r % 2], affT[1 - r % 2]
                link(nc.vector.max(top_v[:, c], src))
                ins = nc.vector.max_index(top_i[:, c], top_v[:, c], src)
                if r < CAP // 8 - 1:
                    ins = nc.vector.match_replace(dst, top_v[:, c], src, -1.0)
                link(ins)
            link(nc.vector.tensor_copy(top_f, top_i))
            eye3 = eye16.rearrange("p (e c) -> p e c", e=NE)

            def block_rows(dst, src):
                return nc.vector.tensor_tensor(dst.rearrange("p (e c) -> p e c", e=NE), eye3,
                                               src[:, None, :].broadcast_to([NE, NE, CAP]), ALU.mult)

            nc.vector.tensor_copy(ones_r, ones[0:NE, 0:P])
            block_rows(bd_i, top_f).then_inc(bd_ready, 1)
            link(nc.vector.tensor_copy(v_hi, top_v))
            link(nc.vector.tensor_tensor(v_lo, top_v, v_hi.bitcast(F32), ALU.subtract))
            block_rows(bd_hi, v_hi.bitcast(F32))
            block_rows(bd_lo, v_lo.bitcast(F32)).then_inc(bdg_ready, 1)
            dve.wait_ge(idxbc_ready, m + 1)
            dve.wait_ge(y_init, NT * (m + 1))
            us = moe_u[m]

            def hT_copy(g, j):
                if j % 2 == 0:
                    dve.wait_ge(hT_psum, g * 2 + (m * 8 + j // 2 + 1))
                    nc.vector.tensor_copy(hT[:, j // 2, :], ps[B_HT][:, :]).then_inc(hT_ready, 1)

            with dve.Fori(0, NGROUP) as g:
                cols = bass.ts(g, SLOTS_E)
                for i in range(NT):
                    ins = nc.vector.tensor_scalar(pick[:, i, :], idx_bc[:, cols], cst[:, C_TOK + i:C_TOK + i + 1], None,
                                                  ALU.is_equal)
                ins.then_inc(pick_ready, 1)
                dve.wait_ge(pick_ready, g + (m * NGROUP + 1))
                dve.wait_ge(gatebc_ready, m + 1)
                for i in range(NT):
                    ins = nc.vector.tensor_tensor(pick_g[:, i, :], pick[:, i, :], gate_bc[:, cols], ALU.mult)
                ins.then_inc(pickg_ready, 1)
                dve.wait_ge(gathered, g * 2 + (m * NGROUP * 2 + 2))
                nc.vector.tensor_copy(xin[:, 4:8, :], ps[B_GA[1]][:, :].rearrange("p (k c) -> p k c", k=4)).then_inc(xin_vec, 1)
                for j in range(GROUP):
                    dve.wait_ge(silu_ready, g * 4 + (m * 16 + j + 1))
                    nc.vector.tensor_tensor(hmid[64 * (j % 2):64 * (j % 2) + 64, j // 2, :], silu[64:128, j % 2, :],
                                            ps[B_GU[j % 2]][64:128, :], ALU.mult).then_inc(h_ready, 1)
                    if j >= 2:
                        hT_copy(g, j - 2)
                hT_copy(g, 2)
                dve.wait_ge(unit_done, us[MOE_UNITS - 1].done_at(g))
                nc.vector.tensor_copy(e_out[:, HALF:D], ps[B_DN[1]][:, :]).then_inc(eout_vec, 1)
                for i in range(NT):
                    for c in range(2):
                        dve.wait_ge(scattered, g * 4 + (m * 16 + 2 * i + c + 1))
                        cc = slice(c * HALF, (c + 1) * HALF)
                        nc.vector.tensor_tensor(y3[:, i, cc], y3[:, i, cc], ps[SC_BANK[i][c]][:, :],
                                                ALU.add).then_inc(y_added, 1)
                        dve.wait_ge(y_added, g * 4 + (m * 16 + 2 * i + c + 1))
                        nc.vector.bn_stats(stats[:, i * 12 + c * 6:i * 12 + c * 6 + 6], y3[:, i, cc]).then_inc(y_stats, 1)
                dve.wait_ge(y_stats, g * 4 + (m * 16 + 4))

        def moe_gpsimd(pool, m, gen):
            pool.wait_ge(x_ready, NT * gen)
            pool.wait_ge(xT_psum, KD // 2 * (T_INDEX[gen] + 1))
            for i in range(NT):
                nc.gpsimd.tensor_scalar(y3[:, i, :], x3[:, i, :], ALPHA, None, ALU.mult).then_inc(y_init, 1)

        def moe_sync(sp, m):
            us = moe_u[m]

            def wait_slot(u, g):
                sp.wait_ge(unit_done, u.free_at(g))
                if u.slot >= RING:
                    sp.wait_ge(chunk_done, chunk0[("ml", "gla")[m]] + (MIX_CHUNKS, 16)[m])

            with sp.Fori(0, NGROUP) as g:
                for j in range(GROUP):
                    for part in range(4):
                        for n, name in enumerate(("moe_w_gate", "moe_w_up")):
                            u = us[8 * j + 2 * part + n]
                            wait_slot(u, g)
                            src = a[name][m, g * GROUP + j].rearrange("(k p) f -> p k f", p=P)
                            sp.dma_start(slot(u, 2), src[:, 2 * part:2 * part + 2, :]).then_inc(slot_landed[u.slot], 16)
                for f in range(KD):
                    for pair in range(2):
                        u = us[32 + 2 * f + pair]
                        wait_slot(u, g)
                        src = a["moe_w_down"][m, bass.ds(g * GROUP + 2 * pair, 2), f * P:(f + 1) * P, :]
                        sp.dma_start(slot(u, 2), src.rearrange("e p d -> p e d")).then_inc(slot_landed[u.slot], 16)

        ar = Arena()
        gl_qkT = ar(2 * 4 * SEQ)
        gl_q, gl_k = gl_qkT[:, 0:1024], gl_qkT[:, 1024:2048]
        gl_zT = gl_qkT.rearrange("p (k t) -> p k t", k=KD)
        gl_v = ar(NT * D).rearrange("p (i d) -> p i d", i=NT)
        gl_r = ar(NT * D).rearrange("p (i d) -> p i d", i=NT)
        gl_z = ar(2 * 1024)
        gl_A = gl_z.rearrange("p (s h t) -> p s h t", s=NT, h=4)
        gl_B = y[:, :].rearrange("p (d c) -> p d c", d=2)
        gl_E = ar(4 * 1024).rearrange("p (b w c) -> p b w c", b=2, w=2)
        gl_l = gl_E.rearrange("p b w c -> p (b w c)")[:, 0:2048]
        glrT = gl_v[0:2 * RANK, 0, 0:SEQ]
        glr_psum, glr_ready, ga_psum, ga_in, ga_act, ga_rows = (sem(s) for s in ("glr_psum", "glr_ready", "ga_psum", "ga_in",
                                                                                 "ga_act", "ga_rows"))
        gq_ready, gk_ready, gv_ready, gr_ready = (sem(s) for s in ("gq_ready", "gk_ready", "gv_ready", "gr_ready"))
        diag_psum, diag_ready, e_arg, e_exp, kd_ready, qd_ready = (sem(s) for s in ("diag_psum", "diag_ready", "e_arg", "e_exp",
                                                                                    "kd_ready", "qd_ready"))
        lv_psum, lv_done, go_psum = sem("lv_psum"), sem("lv_done"), sem("go_psum")

        gla_mix = Mixer(gla_u[0:4] + gla_u[12:16], 2, chunk0["gla"], MOE_RING - RING - 1)

        def gla_tensor(pe, gen):
            wait_xT(pe, gen)
            for kk in range(KD):
                last = nc.tensor.matmul(ps[7][0:2 * RANK, 0:SEQ], glr_w[:, kk * 2 * RANK:(kk + 1) * 2 * RANK], xT3[:, kk, :],
                                        start=(kk == 0), stop=(kk == KD - 1))
            last.then_inc(glr_psum, 1)
            for c in range(4):
                gla_mix.feature_chunk(pe, c, c // 2, None if c else ("x", gen))
            pe.wait_ge(glr_ready, 1)
            for d in range(2):
                for h in range(4):
                    last = nc.tensor.matmul(ps[4 + d * 2 + h // 2][:, (h % 2) * SEQ:(h % 2 + 1) * SEQ],
                                            gk_w[0:2 * RANK, d * QK + h * DK:d * QK + (h + 1) * DK], glrT,
                                            start=True, stop=True)
            last.then_inc(ga_psum, 1)
            for c in range(4, 8):
                gla_mix.feature_chunk(pe, c, c // 2)
            pe.wait_ge(gq_ready, 2)
            pe.wait_ge(gk_ready, 2)
            for i in range(NT):
                for h in range(4):
                    c = slice(h * SEQ + i * P, h * SEQ + (i + 1) * P)
                    last = nc.tensor.matmul(ps[i][:, h * P:(h + 1) * P], gl_k[:, c], gl_q[:, c], start=True, stop=True)
            last.then_inc(diag_psum, 1)
            pe.wait_ge(ga_in, 8)

            def level(n):
                pe.wait_ge(kd_ready, n + 1)
                pe.wait_ge(qd_ready, n + 1)
                if n == 0:
                    pe.wait_ge(diag_ready, 2)
                else:
                    pe.wait_ge(lv_done, 2 * n)
                for i in range(NT):
                    ti = 1 - i if LEVELS[n] == P else i
                    for h in range(4):
                        last = nc.tensor.matmul(ps[i][:, h * P:(h + 1) * P],
                                                gl_E[:, n % 2, 0, h * SEQ + i * P:h * SEQ + (i + 1) * P],
                                                gl_E[:, n % 2, 1, h * SEQ + ti * P:h * SEQ + (ti + 1) * P],
                                                start=True, stop=True)
                last.then_inc(lv_psum, 1)

            for n in range(len(LEVELS)):
                m, i = n // 2, n % 2
                if m == 3:
                    pe.wait_ge(gv_ready, i + 1)
                token_major(pe, gla_u[4 + 2 * m:6 + 2 * m], i, 2 + n % 6)
                level(n)
            pe.wait_ge(lv_done, 2 * len(LEVELS))
            pe.wait_ge(gv_ready, 4)
            pe.wait_ge(gr_ready, 4)
            for i in range(NT):
                for h in range(4):
                    for s in range(NT):
                        last = nc.tensor.matmul(ps[4 + 2 * i + h // 2][:, (h % 2) * DV:(h % 2 + 1) * DV],
                                                gl_A[:, s, h, i * P:(i + 1) * P], gl_v[:, s, h * DV:(h + 1) * DV],
                                                start=(s == 0), stop=(s == NT - 1))
                last.then_inc(go_psum, 1)
            transpose_z(pe, 1)
            for u in range(2):
                gla_mix.token_block(pe, 2 + u, (4 + 2 * u, 5 + 2 * u), None if u else ("z", 1))

        def go_bank(i, h):
            return ps[4 + 2 * i + h // 2][:, (h % 2) * DV:(h % 2 + 1) * DV]

        def gla_scalar(act):
            hi = gla_mix.hi
            act.wait_ge(glr_psum, 1)
            nc.scalar.activation(glrT, ps[7][0:2 * RANK, 0:SEQ], ACT.Copy).then_inc(glr_ready, 1)
            hi(act, 2, 3)
            for b in range(2):
                hi(act, 4 + b)
                act.wait_ge(chunk_done, gla_mix.done(2 * b + 1))
                nc.scalar.activation(gl_q[:, b * HALF:(b + 1) * HALF], ps[b][:, :], ACT.Copy,
                                     scale=DK ** -0.5).then_inc(gq_ready, 1)
            hi(act, 6, 7)
            act.wait_ge(ga_rows, 1)
            nc.scalar.activation(gl_l, gl_l, ACT.Exp).then_inc(ga_act, 1)
            act.wait_ge(ga_act, 1)
            nc.scalar.activation(gl_l, gl_l, ACT.Ln, bias=ones[:, 0:1]).then_inc(ga_act, 1)
            for b in range(2):
                act.wait_ge(chunk_done, gla_mix.done(2 * b + 5))
                nc.scalar.activation(gl_k[:, b * HALF:(b + 1) * HALF], ps[2 + b][:, :], ACT.Copy).then_inc(gk_ready, 1)
            for n in range(len(LEVELS)):
                for w in range(2):
                    act.wait_ge(e_arg, 2 * n + w + 1)
                    nc.scalar.activation(gl_E[:, n % 2, w, :], gl_E[:, n % 2, w, :], ACT.Exp,
                                         scale=1.0 / TAU).then_inc(e_exp, 1)
                if n % 2:
                    m = n // 2
                    act.wait_ge(unit_done, gla_u[5 + 2 * m].done_at())
                    for i in range(NT):
                        src = ps[2 + 2 * m % 6 + i][:, :]
                        if m < 2:
                            nc.scalar.activation(gl_v[:, i, m * HALF:(m + 1) * HALF], src, ACT.Copy).then_inc(gv_ready, 1)
                        else:
                            nc.scalar.activation(gl_r[:, i, (m - 2) * HALF:(m - 1) * HALF], src, ACT.Silu).then_inc(gr_ready, 1)
            hi(act, 8, 9)
            act.wait_ge(x_ready, NT * 2)
            head_std(act, 1, 0)
            for h in range(HEADS):
                head_scale(act, 1, h)
            head_std(act, 1, 1)
            zT_scalar(act, 1, gl_zT, lambda k: mix_cols[:, 8 + k:9 + k])
            hi(act, *range(10, 16))

        def gla_vector(dve, link):
            lo = gla_mix.lo
            lo(dve, 2, 3)
            dve.wait_ge(ga_psum, 1)
            for d in range(2):
                lo(dve, 4 + d)
                for h in range(4):
                    nc.vector.tensor_scalar(gl_z[:, d * 1024 + h * SEQ:d * 1024 + (h + 1) * SEQ],
                                            ps[4 + d * 2 + h // 2][:, (h % 2) * SEQ:(h % 2 + 1) * SEQ],
                                            mix_cols[:, 25 + d * 4 + h:26 + d * 4 + h], None, ALU.add).then_inc(ga_in, 1)
            dve.wait_ge(ga_in, 8)
            nc.vector.scalar_tensor_tensor(gl_l, gl_z, -1.0, gl_z, ALU.mult, ALU.min).then_inc(ga_rows, 1)
            lo(dve, 6, 7)
            dve.wait_ge(ga_act, 2)
            link(nc.vector.scalar_tensor_tensor(gl_z, gl_z, 0.0, gl_l, ALU.min, ALU.subtract))
            dve.wait_ge(x_ready, NT * 2)
            for d in range(2):
                for h in range(4):
                    c = slice(h * SEQ, (h + 1) * SEQ)
                    src, dst = gl_z[:, d * 1024:(d + 1) * 1024][:, c], gl_B[:, d, c]
                    if d:
                        src, dst = src[:, ::-1], dst[:, ::-1]
                    ins = nc.vector.tensor_tensor_scan(dst, ones[:, :], src, 0.0, ALU.mult, ALU.add)
            link(ins)

            def args(n):
                l = LEVELS[n]
                if n >= 2:
                    dve.wait_ge(lv_psum, n - 1)
                f, b = (gl_B[:, d, :].rearrange("p (j c) -> p j c", c=2 * l) for d in range(2))
                ek, eq = (gl_E[:, n % 2, w, :].rearrange("p (j c) -> p j c", c=2 * l) for w in range(2))
                ev, od = slice(0, l), slice(l, 2 * l)
                nb = 1024 // (2 * l)
                rf, rb = f[:, :, l - 1:l].broadcast_to([P, nb, l]), b[:, :, l:l + 1].broadcast_to([P, nb, l])
                nc.vector.tensor_tensor(ek[:, :, ev], rf, f[:, :, ev], ALU.subtract)
                nc.vector.tensor_tensor(ek[:, :, od], rb, b[:, :, od], ALU.subtract).then_inc(e_arg, 1)
                nc.vector.tensor_tensor(eq[:, :, od], f[:, :, od], rf, ALU.subtract)
                nc.vector.tensor_tensor(eq[:, :, ev], b[:, :, ev], rb, ALU.subtract).then_inc(e_arg, 1)

            def q_side(n):
                dve.wait_ge(e_exp, 2 * n + 2)
                dve.wait_ge(gq_ready, 2)
                nc.vector.tensor_tensor(gl_E[:, n % 2, 1, :], gl_E[:, n % 2, 1, :], gl_q, ALU.mult).then_inc(qd_ready, 1)

            def merge(n):
                dve.wait_ge(lv_psum, n + 1)
                l = LEVELS[n]
                if n:
                    dve.wait_ge(lv_done, 2 * n)
                for i in range(NT):
                    prod = ps[i][:, :].rearrange("p (h t) -> p h t", h=4)
                    if l < P:
                        m = lvl_mask[:, n * P:(n + 1) * P][:, None, :].broadcast_to([P, 4, P])
                        ins = nc.vector.copy_predicated(gl_A[:, i, :, i * P:(i + 1) * P], m, prod)
                    else:
                        ins = nc.vector.tensor_copy(gl_A[:, i, :, (1 - i) * P:(2 - i) * P], prod)
                    ins.then_inc(lv_done, 1)

            args(0)
            dve.wait_ge(diag_psum, 1)
            for i in range(NT):
                nc.vector.tensor_scalar(gl_A[:, i, :, i * P:(i + 1) * P], ps[i][:, :].rearrange("p (h t) -> p h t", h=4),
                                        2.0, None, ALU.mult).then_inc(diag_ready, 1)
            q_side(0)
            args(1)
            dve.wait_ge(diag_ready, 2)
            for n in range(len(LEVELS)):
                if n + 1 < len(LEVELS):
                    q_side(n + 1)
                merge(n)
                if n + 2 < len(LEVELS):
                    args(n + 2)
            lo(dve, 8, 9)
            dve.wait_ge(gr_ready, 4)
            for i in range(NT):
                dve.wait_ge(go_psum, i + 1)
                for h in range(HEADS):
                    ins = nc.vector.bn_stats(stats[:, i * 24 + h * 6:i * 24 + h * 6 + 6], go_bank(i, h))
                link(ins)
                head_stats(i)
                dve.wait_ge(hstat_ready, NT + i + 1)
                for h in range(HEADS):
                    head_center(i, h, go_bank(i, h), gl_r)
                head_rstd(dve, 1, i)
            head_scale_vector(dve, 1)
            zT_vector(dve, 1, gl_zT)
            lo(dve, *range(10, 16))

        def gla_gpsimd(pool):
            pool.wait_ge(gk_ready, 2)
            for n in range(len(LEVELS)):
                pool.wait_ge(e_exp, 2 * n + 1)
                nc.gpsimd.tensor_tensor(gl_E[:, n % 2, 0, :], gl_E[:, n % 2, 0, :], gl_k, ALU.mult).then_inc(kd_ready, 1)

        def gla_sync(sp):
            mixer_sync(sp, gla_u, a["gla_w_in"][0], a["gla_w_out"][0], 2)

        ar = Arena()
        band = ar(NT * 4 * SEQ).rearrange("p (s g t) -> p s g t", s=NT, g=4)
        dT = ar(KD * SEQ).rearrange("p (k t) -> p k t", k=KD)
        scale_bc = ar(D)
        scaled_ready, mixed_psum = sem("scaled_ready"), sem("mixed_psum")
        band_in, scale_in, d_psum, d_act, d_vec = (sem(s) for s in ("band_in", "scale_in", "d_psum", "d_act", "d_vec"))

        def pool_tensor(pe, gen):
            pe.wait_ge(band_in, 16)
            for i in range(NT):
                pe.wait_ge((xhat_act, xhat_vec)[i], gen)
            for k in range(KD):
                for s in range(NT):
                    t = slice(s * P, SEQ)
                    last = nc.tensor.matmul(ps[k // 2][:, k % 2 * SEQ + s * P:(k % 2 + 1) * SEQ],
                                            y3[:, s, k * P:(k + 1) * P], band[:, s, k // 2, t],
                                            start=(s == 0), stop=(s == NT - 1))
                if k % 2:
                    last.then_inc(d_psum, 1)
            pe.wait_ge(d_act, 4)
            pe.wait_ge(d_vec, 4)
            pe.wait_ge(scaled_ready, 1)
            u = pool_u
            w = slots[u.slot].rearrange("p (g k n) -> p g k n", g=4, k=2)
            for g in range(4):
                for i in range(NT):
                    for k in range(2):
                        last = nc.tensor.matmul(ps[4 + 2 * (g // 2) + i][:, (g % 2) * 256:(g % 2 + 1) * 256],
                                                dT[:, 2 * g + k, i * P:(i + 1) * P], w[:, g, k, :],
                                                start=(k == 0), stop=(k == 1))
                    if g == 3 and i == 0:
                        last.then_inc(tile0_done, 1)
                if g == 1:
                    last.then_inc(mixed_psum, 1)
            last.then_inc(unit_done, 1)

        def pool_scalar(act):
            g, _ = ln_col(3)
            for k in (0, 1, 4, 5):
                act.wait_ge(d_psum, k // 2 + 1)
                nc.scalar.activation(dT[:, k, :], ps[k // 2][:, k % 2 * SEQ:(k % 2 + 1) * SEQ], ACT.Copy,
                                     scale=ln_cols[:, g + k:g + k + 1]).then_inc(d_act, 1)

        def pool_vector(dve, link):
            g, _ = ln_col(3)
            u = pool_u
            w = slots[u.slot].rearrange("p (g k n) -> p g k n", g=4, k=2)
            dve.wait_ge(slot_landed[u.slot], u.landed)
            dve.wait_ge(scale_in, 16)
            scale4 = scale_bc.rearrange("p (g n) -> p g n", g=4)[:, :, None, :].broadcast_to([P, 4, 2, 256])
            nc.vector.tensor_tensor(w, w, scale4, ALU.mult).then_inc(scaled_ready, 1)
            for k in (2, 3, 6, 7):
                dve.wait_ge(d_psum, k // 2 + 1)
                nc.vector.tensor_scalar(dT[:, k, :], ps[k // 2][:, k % 2 * SEQ:(k % 2 + 1) * SEQ],
                                        ln_cols[:, g + k:g + k + 1], None, ALU.mult).then_inc(d_vec, 1)

        def pool_gpsimd(pool, link, gen):
            pool.wait_ge(y_added, 32)
            skew = rel_dram[:, P - 1:P - 1 + P * (3 * P - 1)].rearrange("h (q c) -> q h c", c=3 * P - 1)
            pool.wait_ge(rel_out, 16)
            pool.dma_start(at_bias[:, :, P:3 * P], skew[:, :, 0:2 * P]).then_inc(rel_in, 16)
            pool.dma_start(at_bias[:, :, 0:P], skew[:, :, P:2 * P]).then_inc(rel_in, 16)

        def pool_sync(sp):
            u = pool_u
            wait_free(sp, u)
            sp.dma_start(slots[u.slot].rearrange("p (g k n) -> p g k n", g=4, k=2),
                         a["pool_w_2"][0].rearrange("g (k p) n -> p g k n", p=P)).then_inc(slot_landed[u.slot], 16)
            sp.wait_ge(y_added, 32)
            sp.dma_start(band.rearrange("p s g t -> p (s g t)"), a["band"]).then_inc(band_in, 16)
            sp.dma_start(scale_bc, a["pool_scale_2"].broadcast_to([P, D])).then_inc(scale_in, 16)

        ar = Arena()
        ar(3 * NT * D + A_HEADS * 3 * P)
        f_silu = ar(4 * SEQ).rearrange("p (b t) -> p b t", b=4)
        fsilu_ready, fprod_ready, fhi_ready, fh_ready = (sem(s) for s in ("fsilu_ready", "fprod_ready", "fhi_ready",
                                                                          "fh_ready"))

        def gate_up_chunk(us, f, n):
            return slot(us[n], KD)[:, :, f * P:(f + 1) * P]

        def down_chunk(u, f):
            return slot(u, 2)[:, f:f + 1, :]

        def ffn_tensor(pe, m, gen):
            first, body, last_u = ffn_u[m]
            for b in range(4, 8):
                nc.tensor.matmul(ps[b][:, :], cst[32:64, C_EYE:C_EYE + P], cst[32:64, C_EYE:C_EYE + HALF],
                                 start=True, stop=False)

            def gate_up(s, at, first=False):
                for f in range(2):
                    for n in range(2):
                        buf = n
                        pe.wait_ge(split_ready, at + (2 * f + n + 1))
                        for k in range(KD):
                            if first and f == n == 0 and k % 2 == 0:
                                pe.wait_ge(xlo_ready, split_before("x", gen) + k // 2 + 1)
                            for p, (wp, xp) in enumerate(PARTS):
                                last = nc.tensor.matmul(ps[2 * s + f][:, n * SEQ:(n + 1) * SEQ],
                                                        w_parts[wp][:, buf, k * P:(k + 1) * P],
                                                        (xT_hi3, xT_lo3)[xp][:, k, :],
                                                        start=(k == 0 and p == 0), stop=(k == KD - 1 and p == 2))
                                if f == 1 and k == 0 and p == 0:
                                    last.then_inc(unit_done, 1)
                        last.then_inc(chunk_done, 1)

            def down(s, at, units, base, end=False):
                for f in range(2):
                    pe.wait_ge(split_ready, at + (f + 1))
                    pe.wait_ge(fh_ready, base + (f + 1))
                    for i in range(NT):
                        for c in range(2):
                            for p, (wp, hp) in enumerate(PARTS):
                                last = nc.tensor.matmul(ps[4 + 2 * c + i][:, :], h_parts[hp][:, 2 * s + f, i * P:(i + 1) * P],
                                                        w_parts[wp][:, f, c * HALF:(c + 1) * HALF],
                                                        start=False, stop=(end and f == 1 and p == 2))
                                if f == 1 and i == 0 and c == 0 and p == 0:
                                    last.then_inc(unit_done, units)
                                if end and f == 1 and i == 0 and c == 1 and p == 2:
                                    last.then_inc(tile0_done, 1)
                    last.then_inc(chunk_done, 1)

            c0 = chunk0[f"ffn{m}"]
            gate_up(0, c0, first=True)
            with pe.Fori(0, 5) as g:
                for s in range(2):
                    at = g * 12 + (c0 + 4 + 6 * s)
                    gate_up(1 - s, at)
                    down(s, at + 4, 2, g * 4 + (m * NF + 2 * s))
            down(0, c0 + FFN_CHUNKS - 2, 1, m * NF + 20, end=True)

        def ffn_scalar(act, m):
            first, body, last_u = ffn_u[m]
            c0 = chunk0[f"ffn{m}"]

            def gate_up(us, g, at, blocks=(0, 1)):
                for f in blocks:
                    for n in range(2):
                        split_hi(act, us[n], g, gate_up_chunk(us, f, n), n, at + (2 * f + n))

            def silu(s, f, done):
                b = 2 * s + f
                act.wait_ge(chunk_done, done)
                nc.scalar.activation(f_silu[:, b, :], ps[b][:, 0:SEQ], ACT.Silu).then_inc(fsilu_ready, 1)

            gate_up(first, 0, c0, (1,))
            silu(0, 0, c0 + 2)
            with act.Fori(0, 5) as g:
                for s in range(2):
                    at = g * 12 + (c0 + 4 + 6 * s)
                    gate_up(body[3 * s:3 * s + 2], g, at, (0,))
                    silu(s, 1, at)
                    gate_up(body[3 * s:3 * s + 2], g, at, (1,))
                    silu(1 - s, 0, at + 2)
                    for f in range(2):
                        split_hi(act, body[3 * s + 2], g, down_chunk(body[3 * s + 2], f), f, at + (4 + f))
            for f in range(2):
                split_hi(act, last_u, 0, down_chunk(last_u, f), f, c0 + FFN_CHUNKS - 2 + f)
                if f == 0:
                    silu(0, 1, c0 + FFN_CHUNKS - 4)

        def ffn_vector(dve, link, m, gen):
            first, body, last_u = ffn_u[m]
            c0 = chunk0[f"ffn{m}"]

            def gate_up(us, at, blocks=(0, 1)):
                for f in blocks:
                    for n in range(2):
                        split_lo(dve, gate_up_chunk(us, f, n), n, at + (2 * f + n))

            def hidden(s, f, blocks):
                b = 2 * s + f
                dve.wait_ge(fsilu_ready, blocks + 1)
                nc.vector.tensor_tensor(f_silu[:, b, :], f_silu[:, b, :], ps[b][:, SEQ:2 * SEQ], ALU.mult).then_inc(fprod_ready, 1)
                dve.wait_ge(fprod_ready, blocks + 1)
                nc.vector.tensor_copy(h_parts[0][:, b, :], f_silu[:, b, :]).then_inc(fhi_ready, 1)
                dve.wait_ge(fhi_ready, blocks + 1)
                nc.vector.tensor_tensor(h_parts[1][:, b, :], f_silu[:, b, :], h_parts[0][:, b, :].bitcast(F32),
                                        ALU.subtract).then_inc(fh_ready, 1)

            gate_up(first, c0, (1,))
            hidden(0, 0, m * NF)
            with dve.Fori(0, 5) as g:
                for s in range(2):
                    at, blocks = g * 12 + (c0 + 4 + 6 * s), g * 4 + (m * NF + 2 * s + 1)
                    gate_up(body[3 * s:3 * s + 2], at, (0,))
                    hidden(s, 1, blocks)
                    gate_up(body[3 * s:3 * s + 2], at, (1,))
                    hidden(1 - s, 0, blocks + 1)
                    for f in range(2):
                        split_lo(dve, down_chunk(body[3 * s + 2], f), f, at + (4 + f))
            split_lo(dve, down_chunk(last_u, 0), 0, c0 + FFN_CHUNKS - 2)
            hidden(0, 1, m * NF + NF - 1)
            split_lo(dve, down_chunk(last_u, 1), 1, c0 + FFN_CHUNKS - 1)

        def ffn_first_hi(act, m):
            for n in range(2):
                split_hi(act, ffn_u[m][0][n], 0, gate_up_chunk(ffn_u[m][0], 0, n), n, chunk0[f"ffn{m}"] + n)

        def ffn_first_lo(dve, m):
            for n in range(2):
                split_lo(dve, gate_up_chunk(ffn_u[m][0], 0, n), n, chunk0[f"ffn{m}"] + n)

        def ffn_sync(sp, m):
            first, body, last_u = ffn_u[m]
            wg, wu = (a[n][m].rearrange("(k p) f -> p k f", p=P) for n in ("w_gate_2", "w_up_2"))
            wd = a["w_down_2"][m].rearrange("(f p) d -> p f d", p=P)

            def load(u, g, src):
                sp.wait_ge(unit_done, u.free_at(g))
                sp.dma_start(slot(u, src.shape[1]), src).then_inc(slot_landed[u.slot], 16)

            for u, w in zip(first, (wg, wu)):
                load(u, 0, w[:, :, 0:SEQ])
            with sp.Fori(0, 5) as g:
                for s in range(2):
                    for u, w in zip(body[3 * s:3 * s + 2], (wg, wu)):
                        load(u, g, w[:, :, bass.ds(g * 512 + (1 + s) * 256, 256)])
                    load(body[3 * s + 2], g, wd[:, bass.ds(g * 4 + 2 * s, 2), :])
            load(last_u, 0, wd[:, NF - 2:NF, :])

        ar = Arena()
        at_q = ar(A_HEADS * SEQ).rearrange("p (h t) -> p h t", h=A_HEADS)
        at_k = ar(A_HEADS * SEQ).rearrange("p (h t) -> p h t", h=A_HEADS)
        at_zT = at_q
        at_v = ar(NT * D).rearrange("p (i d) -> p i d", i=NT)
        at_bias = ar(A_HEADS * 3 * P).rearrange("p (h c) -> p h c", h=A_HEADS)
        ar(4 * SEQ)
        at_e = ar(2 * 2 * 384).rearrange("p (b c n) -> p b c n", b=2, c=2)
        at_a = ar(2 * 384).rearrange("p (b n) -> p b n", b=2)
        at_aT = ar(2 * 384).rearrange("p (b n) -> p b n", b=2)
        KEYS = (slice(0, P), slice(P, 3 * P))
        at_max = small[:, 64:72].rearrange("p (b c i) -> p b c i", b=2, c=2)
        at_sum = small[:, 72:80].rearrange("p (b c i) -> p b c i", b=2, c=2)
        at_rec = small[:, 80:88].rearrange("p (b c i) -> p b c i", b=2, c=2)
        at_ss = small[:, 96:112]
        o_std = small[:, 112:128]
        aq_ready, ak_ready, av_act, av_vec = (sem(s) for s in ("aq_ready", "ak_ready", "av_act", "av_vec"))
        as_psum, amax_ready, aexp_ready, aw_ready, aT_psum, aT_ready, ao_psum, ao_vec, ao_act = (
            sem(s) for s in ("as_psum", "amax_ready", "aexp_ready", "aw_ready", "aT_psum", "aT_ready", "ao_psum", "ao_vec",
                             "ao_act"))
        ostd_ready = sem("ostd_ready")
        LATE = (slice(0, A_HEADS - 1), slice(A_HEADS - 1, A_HEADS))

        att_mix = Mixer(att_u, 4, chunk0["att"])

        def att_tensor(pe, gen):
            for c in range(16):
                att_mix.feature_chunk(pe, c, c // 2, None if c else ("x", gen))

            def scores(h):
                if h >= 2:
                    pe.wait_ge(amax_ready, h - 1)
                for i in range(NT):
                    for c in range(2):
                        r = slice(HD * c, HD * (c + 1))
                        last = nc.tensor.matmul(ps[4 + 2 * (h % 2) + c][:, KEYS[i]], at_q[r, h, i * P:(i + 1) * P],
                                                at_k[r, h, 0:(i + 1) * P], start=True, stop=True)
                last.then_inc(as_psum, 1)

            def transpose_weights(h):
                pe.wait_ge(aw_ready, h + 1)
                for b in range(3):
                    last = nc.tensor.transpose(ps[h % 2][:, b * P:(b + 1) * P], at_a[:, h % 2, b * P:(b + 1) * P], ident)
                last.then_inc(aT_psum, 1)

            def values(h):
                pe.wait_ge(aT_ready, h + 1)
                if h >= 2:
                    pe.wait_ge(ao_vec, h - 1)
                for i, blocks in enumerate((((0, 0),), ((0, 1), (1, 2)))):
                    for n, (s, b) in enumerate(blocks):
                        last = nc.tensor.matmul(ps[2 + h % 2][:, i * P:(i + 1) * P], at_aT[:, h % 2, b * P:(b + 1) * P],
                                                at_v[:, s, h * V_DIM:(h + 1) * V_DIM], start=(n == 0),
                                                stop=(n == len(blocks) - 1))
                last.then_inc(ao_psum, 1)

            pe.wait_ge(aq_ready, 4)
            att_mix.token_block(pe, 4, (0, 1))
            pe.wait_ge(ak_ready, 4)
            scores(0)
            scores(1)
            att_mix.token_block(pe, 5, (2, 3))
            pe.wait_ge(av_act, 2)
            pe.wait_ge(av_vec, 2)
            for h in range(A_HEADS):
                if h + 2 < A_HEADS:
                    scores(h + 2)
                if h:
                    values(h - 1)
                transpose_weights(h)
            values(A_HEADS - 1)
            transpose_z(pe, 2)
            for u in range(2):
                att_mix.token_block(pe, 6 + u, (4 + 2 * u, 5 + 2 * u), None if u else ("z", 2))

        def att_scalar(act, gen):
            for b in range(4):
                att_mix.hi(act, 2 * b + 2, 2 * b + 3)
                act.wait_ge(chunk_done, att_mix.done(2 * b + 1))
                nc.scalar.activation(at_q[:, 2 * b:2 * b + 2, :],
                                     ps[b][:, :].rearrange("p (h t) -> p h t", h=2), ACT.Copy).then_inc(aq_ready, 1)
            att_mix.hi(act, *range(10, 22))

            def v_half(m):
                act.wait_ge(chunk_done, att_mix.done(19 + 4 * m))
                nc.scalar.activation(at_v[:, 0, m * HALF:(m + 1) * HALF], ps[2 * m][:, :], ACT.Copy).then_inc(av_act, 1)

            def squares(h):
                act.wait_ge(ao_vec, h + 1)
                if h:
                    act.wait_ge(ao_act, h)
                for i in range(NT):
                    ins = nc.scalar.activation(small_sq[:, i, 0:P], y3[:, i, h * V_DIM:(h + 1) * V_DIM], ACT.Square,
                                               accum_out=at_ss[:, i * 8 + h:i * 8 + h + 1])
                ins.then_inc(ao_act, 1)

            def exps(h):
                act.wait_ge(amax_ready, h + 1)
                b = h % 2
                for c in range(2):
                    for i in range(NT):
                        ins = nc.scalar.activation(at_e[:, b, c, KEYS[i]], at_e[:, b, c, KEYS[i]], ACT.Exp,
                                                   bias=at_max[:, b, c, i:i + 1], accum_out=at_sum[:, b, c, i:i + 1])
                ins.then_inc(aexp_ready, 1)

            v_half(0)
            att_mix.hi(act, 22)
            exps(0)
            att_mix.hi(act, 23)
            exps(1)
            v_half(1)
            att_mix.hi(act, 24, 25)
            for h in range(A_HEADS):
                act.wait_ge(aT_psum, h + 1)
                nc.scalar.activation(at_aT[:, h % 2, :], ps[h % 2][:, 0:384], ACT.Copy).then_inc(aT_ready, 1)
                if h + 2 < A_HEADS:
                    exps(h + 2)
                if h:
                    squares(h - 1)
            ss3, std3 = (t.rearrange("p (i h) -> p i h", i=NT) for t in (at_ss, o_std))
            for n, heads in enumerate(LATE):
                if n:
                    squares(A_HEADS - 1)
                act.wait_ge(ao_act, heads.stop)
                nc.scalar.activation(std3[:, :, heads], ss3[:, :, heads], ACT.Sqrt, bias=eps,
                                     scale=1.0 / V_DIM).then_inc(ostd_ready, 1)
            zT_scalar(act, 2, at_zT, lambda k: sub_g)
            att_mix.hi(act, *range(26, 32))

        def att_vector(dve, link, gen):
            att_mix.lo(dve, *range(2, 10))
            for b in range(4):
                att_mix.lo(dve, 2 * b + 10, 2 * b + 11)
                dve.wait_ge(chunk_done, att_mix.done(2 * b + 9))
                nc.vector.tensor_copy(at_k[:, 2 * b:2 * b + 2, :],
                                      ps[4 + b][:, :].rearrange("p (h t) -> p h t", h=2)).then_inc(ak_ready, 1)
            att_mix.lo(dve, *range(18, 22))
            dve.wait_ge(rel_in, 32)

            def v_half(m):
                dve.wait_ge(chunk_done, att_mix.done(19 + 4 * m))
                nc.vector.tensor_copy(at_v[:, 1, m * HALF:(m + 1) * HALF], ps[2 * m + 1][:, :]).then_inc(av_vec, 1)

            def logits(h):
                if h >= 2:
                    dve.wait_ge(aw_ready, h - 1)
                dve.wait_ge(as_psum, h + 1)
                b = h % 2
                for c in range(2):
                    ins = nc.vector.scalar_tensor_tensor(at_e[:, b, c, :], ps[4 + 2 * b + c][:, 0:384], HD ** -0.5,
                                                         at_bias[:, h, :], ALU.mult, ALU.add)
                link(ins)
                for i in range(NT):
                    ins = nc.vector.tensor_reduce(at_max[:, b, :, i], at_e[:, b, :, KEYS[i]], AX.X, ALU.max, negate=True)
                ins.then_inc(amax_ready, 1)

            def combine(h):
                dve.wait_ge(aexp_ready, h + 1)
                if h >= 2:
                    dve.wait_ge(ao_vec, h - 1)
                b = h % 2
                link(nc.vector.reciprocal(at_rec[:, b], at_sum[:, b]))
                link(nc.vector.scalar_tensor_tensor(at_rec[:, b, 1, :], at_rec[:, b, 1, :], neglam, at_sum[:, b, 0, :],
                                                    ALU.mult, ALU.mult))
                for i in range(NT):
                    ins = nc.vector.scalar_tensor_tensor(at_a[:, b, KEYS[i]], at_e[:, b, 1, KEYS[i]], at_rec[:, b, 1, i:i + 1],
                                                         at_e[:, b, 0, KEYS[i]], ALU.mult, ALU.add)
                ins.then_inc(aw_ready, 1)

            def outputs(h):
                dve.wait_ge(ao_psum, h + 1)
                for i in range(NT):
                    ins = nc.vector.tensor_scalar(y3[:, i, h * V_DIM:(h + 1) * V_DIM], ps[2 + h % 2][:, i * P:(i + 1) * P],
                                                  at_rec[:, h % 2, 0, i:i + 1], None, ALU.mult)
                ins.then_inc(ao_vec, 1)

            dve.wait_ge(x_ready, NT * gen)
            v_half(0)
            logits(0)
            att_mix.lo(dve, 22)
            logits(1)
            att_mix.lo(dve, 23)
            combine(0)
            v_half(1)
            att_mix.lo(dve, 24, 25)
            for h in range(A_HEADS):
                if h:
                    combine(h)
                if h + 2 < A_HEADS:
                    logits(h + 2)
                if h:
                    outputs(h - 1)
            outputs(A_HEADS - 1)
            dve.wait_ge(ao_vec, A_HEADS)
            std3 = o_std.rearrange("p (i h) -> p i h", i=NT)

            def scale(i, heads):
                v = y3[:, i, :].rearrange("p (h d) -> p h d", h=A_HEADS)[:, heads, :]
                inv = std3[:, i, heads].unsqueeze(2).broadcast_to([P, heads.stop - heads.start, V_DIM])
                return nc.vector.tensor_tensor(v, v, inv, ALU.mult)

            dve.wait_ge(ostd_ready, 1)
            link(nc.vector.reciprocal(std3[:, :, LATE[0]], std3[:, :, LATE[0]]))
            for i in range(NT):
                scale(i, LATE[0])
            dve.wait_ge(ostd_ready, 2)
            link(nc.vector.reciprocal(std3[:, :, LATE[1]], std3[:, :, LATE[1]]))
            for i in range(NT):
                scale(i, LATE[1]).then_inc(z_ready, 1)
            zT_vector(dve, 2, at_zT)
            att_mix.lo(dve, *range(26, 32))

        def att_sync(sp):
            mixer_sync(sp, att_u, a["w_qkv_2"][0], a["w_o_2"][0], 4)

        small_sq = f_silu

        MISC = 16 * 7
        PAR = 16 * 11
        n_w = 2 * QK + 2 * D

        def setup_sync(sp):
            sp.dma_start(ident, a["consts"][:, C_ID:C_ID + P]).then_inc(ident_in, 16)
            for i in range(NT):
                sp.dma_start(x3[:, i, :], a["x"][0, i * P:(i + 1) * P, :]).then_inc(x_in[i], 16)
            sp.dma_start(gate_w[:, :].rearrange("p (k n) -> p k n", k=KD),
                         a["mlstm_w_in"][0][:, n_w:n_w + 16].rearrange("(k p) n -> p k n", p=P)).then_inc(gate_in, 16)
            sp.dma_start(gate_b[0:4, :], a["mlstm_gate_b"].rearrange("o d t h -> h (o d t)"),
                         allow_slow_non_contiguous=True).then_inc(gate_in, 16)

        def setup_scalar(act):
            act.dma_start(cst[:, C_EYE:], a["consts"][:, C_EYE:]).then_inc(const_in, 16)

        def setup_gpsimd(pool, link):
            at = 0
            for name in ("ln_g", "ln_b"):
                pool.dma_start(ln_rows[at:at + 32, :], a[name].rearrange("l s (k c) -> (l s k) c", c=P)).then_inc(par_in, 16)
                at += 32
            for name in ("ln_mix_g_2", "ln_mix_b_2", "ln_ffn_g_2", "ln_ffn_b_2"):
                pool.dma_start(ln_rows[at:at + 16, :], a[name].rearrange("l (k c) -> (l k) c", c=P)).then_inc(par_in, 16)
                at += 16
            for n, name in enumerate(("mlstm_norm_g", "gla_norm_g", "pool_scale_2")):
                pool.dma_start(mix_rows[8 * n:8 * n + 8, :], a[name].rearrange("o (k c) -> (o k) c", c=P)).then_inc(par_in, 16)
            pool.dma_start(mix_rows[24:25, :], a["subln_g_2"]).then_inc(par_in, 16)
            pool.dma_start(mix_rows[25:33, :], a["gla_gate_b"].rearrange("o g (h c) -> (o g h) c", c=P)).then_inc(par_in, 16)
            pool.dma_start(rel_t[0:BUCKETS, :], a["rel_table_2"]).then_inc(misc_in, 16)
            pool.dma_start(lam_p[:, :], a["lam_p_2"].rearrange("o r c -> o (r c)").broadcast_to([P, 4 * HD])).then_inc(misc_in, 16)
            pool.dma_start(glr_w[:, :].rearrange("p (k n) -> p k n", k=KD),
                          a["gla_w_in"][0][:, n_w:n_w + 32].rearrange("(k p) n -> p k n", p=P)).then_inc(misc_in, 16)
            for l in range(2):
                pool.dma_start(rout_w[:, l * KD * NE:(l + 1) * KD * NE].rearrange("p (k n) -> p k n", k=KD),
                              a["moe_router"][l].rearrange("(k p) n -> p k n", p=P)).then_inc(misc_in, 16)
            link(nc.gpsimd.memset(gk_w[0:2 * RANK, :], 0.0))
            for d in range(2):
                pool.dma_start(gk_w[d * RANK:(d + 1) * RANK, d * QK:(d + 1) * QK], a["gla_gate_w"][0, d]).then_inc(misc_in, 16)

        def setup_vector(dve):
            nc.vector.memset(ones[:, :], 1.0)
            nc.vector.memset(rel_t[BUCKETS:BUCKETS + 1, :], MASKED).then_inc(const_ready, 1)
            dve.wait_ge(const_in, 16)
            for n in range(7):
                ins = nc.vector.tensor_scalar(lvl_mask[:, n * P:(n + 1) * P], cst[:, C_XOR:C_XOR + P], float(LEVELS[n]), None,
                                              ALU.is_ge)
            ins.then_inc(const_ready, 1)
            dve.wait_ge(const_ready, 2)

        block = ctx.enter_context(nc.Block())

        @block.sync
        def _(sp):
            setup_sync(sp)
            parts = [lambda: ml_sync(sp), lambda: moe_sync(sp, 0), lambda: gla_sync(sp), lambda: moe_sync(sp, 1),
                     lambda: pool_sync(sp), lambda: ffn_sync(sp, 0), lambda: att_sync(sp), lambda: ffn_sync(sp, 1)]
            for n in range(upto):
                parts[n]()
            sp.wait_ge(x_ready, NT * upto)
            sp.dma_start(out.rearrange("o (i p) d -> p (o i) d", p=P), x3).then_inc(x_out, 16)
            sp.wait_ge(x_out, 16)

        @block.tensor
        def _(pe):
            transpose_x(pe, 0)
            parts = [lambda: ml_tensor(pe), lambda: moe_tensor(pe, 0, 1), lambda: gla_tensor(pe, 2),
                     lambda: moe_tensor(pe, 1, 3), lambda: pool_tensor(pe, 4), lambda: ffn_tensor(pe, 0, 5),
                     lambda: att_tensor(pe, 6), lambda: ffn_tensor(pe, 1, 7)]
            for n in range(upto):
                parts[n]()
                if n + 1 < upto and T_INDEX[n + 1] is not None:
                    transpose_x(pe, n + 1)

        @block.scalar
        def _(act):
            setup_scalar(act)
            xT_scalar(act, 0)
            parts = [lambda: ml_scalar(act), lambda: moe_scalar(act, 0), lambda: gla_scalar(act),
                     lambda: moe_scalar(act, 1), lambda: pool_scalar(act), lambda: ffn_scalar(act, 0),
                     lambda: att_scalar(act, 6), lambda: ffn_scalar(act, 1)]
            first_hi = [None, None, lambda: gla_mix.hi(act, 0, 1), None, None, lambda: ffn_first_hi(act, 0),
                        lambda: att_mix.hi(act, 0, 1), lambda: ffn_first_hi(act, 1)]
            for n in range(upto):
                parts[n]()
                ln_scalar(act, n)
                if n + 1 < upto and T_INDEX[n + 1] is not None:
                    if first_hi[n + 1]:
                        first_hi[n + 1]()
                    xT_scalar(act, n + 1)

        @block.vector
        def _(dve):
            link = chain(dve, vec_chain)
            xT_vector(dve, 0)
            setup_vector(dve)
            parts = [lambda: ml_vector(dve, link), lambda: moe_vector(dve, link, 0), lambda: gla_vector(dve, link),
                     lambda: moe_vector(dve, link, 1), lambda: pool_vector(dve, link), lambda: ffn_vector(dve, link, 0, 5),
                     lambda: att_vector(dve, link, 6), lambda: ffn_vector(dve, link, 1, 7)]
            products_done = [
                [(chunk_done, ml_mix.done(27)), (chunk_done, ml_mix.done(31))], [],
                [(chunk_done, gla_mix.done(11)), (chunk_done, gla_mix.done(15))], [],
                [(mixed_psum, 1), (unit_done, pool_u.done_at())], [None, (chunk_done, chunk0["ffn0"] + FFN_CHUNKS)],
                [(chunk_done, att_mix.done(27)), (chunk_done, att_mix.done(31))],
                [None, (chunk_done, chunk0["ffn1"] + FFN_CHUNKS)]]
            first_lo = [None, None, lambda: gla_mix.lo(dve, 0, 1), None, None, lambda: ffn_first_lo(dve, 0),
                        lambda: att_mix.lo(dve, 0, 1), lambda: ffn_first_lo(dve, 1)]
            for n in range(upto):
                parts[n]()
                ln_vector(dve, link, n, *products_done[n])
                if n + 1 < upto and T_INDEX[n + 1] is not None:
                    if first_lo[n + 1]:
                        first_lo[n + 1]()
                    xT_vector(dve, n + 1)

        @block.gpsimd
        def _(pool):
            link = chain(pool, pool_chain)
            setup_gpsimd(pool, link)
            parts = [lambda: ml_gpsimd(pool), lambda: moe_gpsimd(pool, 0, 1), lambda: gla_gpsimd(pool),
                     lambda: moe_gpsimd(pool, 1, 3), lambda: pool_gpsimd(pool, link, 4), None, None, None]
            for n in range(upto):
                if parts[n]:
                    parts[n]()
                ln_gpsimd(pool, link, n, *ln_dram_rows(n))


_INS = ["x", "mlstm_w_in", "mlstm_gate_b", "mlstm_norm_g", "mlstm_w_out", "gla_w_in", "gla_gate_w", "gla_gate_b",
        "gla_norm_g", "gla_w_out", "moe_router", "moe_w_gate", "moe_w_up", "moe_w_down", "ln_g", "ln_b", "pool_w_2",
        "pool_scale_2", "w_qkv_2", "w_o_2", "lam_p_2", "subln_g_2", "rel_table_2", "w_gate_2", "w_up_2", "w_down_2",
        "ln_mix_g_2", "ln_mix_b_2", "ln_ffn_g_2", "ln_ffn_b_2"]


def kernel(**inputs):
    import concourse.bacc as bacc
    from concourse.bass_utils import run_bass_kernel_spmd

    nc = bacc.Bacc("TRN2", target_bir_lowering=False, num_devices=1)
    arrays = {f"in_{n}": np.ascontiguousarray(inputs[n]) for n in _INS}
    arrays["in_consts"], arrays["in_band"] = shape_constants()
    aps = {n[3:]: nc.dram_tensor(n, v.shape, mybir.dt.from_np(v.dtype), kind="ExternalInput").ap()
           for n, v in arrays.items()}
    out = nc.dram_tensor("out_x", (1, SEQ, D), F32, kind="ExternalOutput").ap()
    program(nc, aps, out)
    r = run_bass_kernel_spmd(nc, [arrays], core_ids=[0])
    return r.results[0]["out_x"]
```
